# Optimizing a Trainium2 kernel written in Bass

```python
import math
import jax
import jax.numpy as jnp
from jax import lax
import numpy as np

D_MODEL = 1024
BATCH = 1
SEQ = 4096
DEPTH = 1
DEC_BATCH = 8
DEC_SEQ = 8
PAST_LEN = 2048
PAGE_SIZE = 128

MIX_WIDTH = D_MODEL
BRANCH_WIDTH = MIX_WIDTH // 4
A_WIDTH = BRANCH_WIDTH
A_HEADS = 4
A_HEAD_DIM = A_WIDTH // A_HEADS
A_PATTERNS = ((128, 1), (512, 4), (2048, 16))
A_WINDOW_MAX = 2048
A_BLOCK = 128
B_WIDTH = BRANCH_WIDTH
B_HEADS = 4
B_DK = B_WIDTH // B_HEADS
B_DV = B_WIDTH // B_HEADS
CONV_W = 4
DELTA_CHUNK = 64
C_WIDTH = BRANCH_WIDTH
C_HEADS = 4
C_DK = C_WIDTH // C_HEADS
C_DV = C_WIDTH // C_HEADS
HGRN_CHUNK = 16
D_WIDTH = MIX_WIDTH - A_WIDTH - B_WIDTH - C_WIDTH
D_GROUPS = 4
D_GROUP_W = D_WIDTH // D_GROUPS
POOL_WINDOWS = (2, 4, 8, 16)
POOL_MAX = 16
NORM_EPS = 1e-6
NEG_MASK = -1e30
IN_SPLITS = (A_WIDTH, A_WIDTH, A_WIDTH, A_WIDTH,
             3 * B_WIDTH, B_WIDTH, B_HEADS, B_HEADS,
             C_WIDTH, C_WIDTH, C_WIDTH, C_WIDTH,
             D_WIDTH, D_WIDTH)
IN_WIDTH = sum(IN_SPLITS)
F32 = jnp.float32

kernel_name = 'hybrid_dilated_delta_hgrn2_pool_decode_step'

def _rms(x, w):
    xf = x.astype(F32)
    y = xf * lax.rsqrt(jnp.mean(xf * xf, axis=-1, keepdims=True) + NORM_EPS)
    return y * w.astype(F32)

def _l2norm(x):
    return x * lax.rsqrt(jnp.sum(x * x, axis=-1, keepdims=True) + 1e-6)

def _alibi_slopes():
    return 2.0 ** (-8.0 * (jnp.arange(A_HEADS, dtype=F32) + 1.0) / A_HEADS)

def _dilated_band(q, k, v, slopes, dil, steps):
    b, s, h, dh = q.shape
    n = s // dil

    def to_res(t):
        return t.reshape(b, n, dil, h, dh).transpose(0, 2, 1, 3, 4).reshape(b * dil, n, h, dh)

    qr, kr, vr = to_res(q), to_res(k), to_res(v)
    bq = math.gcd(n, A_BLOCK)
    nb = n // bq
    nk = bq + steps
    pad = ((0, 0), (steps, 0), (0, 0), (0, 0))
    idx = jnp.arange(nb)[:, None] * bq + jnp.arange(nk)[None, :]
    kb = jnp.pad(kr, pad)[:, idx]
    vb = jnp.pad(vr, pad)[:, idx]
    qb = qr.reshape(b * dil, nb, bq, h, dh)
    sc = jnp.einsum('znqhd,znkhd->znhqk', qb, kb)
    dist = (jnp.arange(bq)[:, None] + steps) - jnp.arange(nk)[None, :]
    valid = (dist >= 0) & (dist <= steps) & ((idx - steps)[:, None, :] >= 0)
    sc = sc - slopes[:, None, None] * (dist * dil).astype(F32)
    sc = jnp.where(valid[None, :, None], sc, NEG_MASK)
    m = sc.max(-1)
    p = jnp.exp(sc - m[..., None])
    den = p.sum(-1)
    num = jnp.einsum('znhqk,znkhd->znqhd', p, vb)

    def back(t):
        rest = t.shape[3:]
        t = t.reshape((b, dil, n) + rest)
        return jnp.swapaxes(t, 1, 2).reshape((b, s) + rest)

    return back(jnp.moveaxis(m, 2, 3)), back(jnp.moveaxis(den, 2, 3)), back(num)

def _dilated_gather(q, k_all, v_all, slopes, dil, steps, buf):
    t = q.shape[1]
    j = jnp.arange(steps + 1)
    c = buf + jnp.arange(t)[:, None] - j[None, :] * dil
    valid = c >= 0
    cc = jnp.maximum(c, 0)
    kg = k_all[:, cc]
    vg = v_all[:, cc]
    sc = jnp.einsum('bthd,btjhd->bthj', q, kg) - slopes[:, None] * (j * dil).astype(F32)[None, :]
    sc = jnp.where(valid[None, :, None, :], sc, NEG_MASK)
    m = sc.max(-1)
    p = jnp.exp(sc - m[..., None])
    den = p.sum(-1)
    num = jnp.einsum('bthj,btjhd->bthd', p, vg)
    return m, den, num

def _mixer_attn(q, k, v, gate, kv_cache):
    b, l, _ = q.shape

    def heads(t):
        return t.reshape(b, l, A_HEADS, A_HEAD_DIM)

    k_h, v_h = heads(k), heads(v)
    qf = heads(q).astype(F32) * (A_HEAD_DIM ** -0.5)
    kf, vf = k_h.astype(F32), v_h.astype(F32)
    slopes = _alibi_slopes()
    parts = []
    if kv_cache is None:
        for win, dil in A_PATTERNS:
            parts.append(_dilated_band(qf, kf, vf, slopes, dil, win // dil))
        keep = min(A_WINDOW_MAX, l)
        k_rows, v_rows = k_h[:, l - keep:], v_h[:, l - keep:]
    else:
        k_cache, v_cache = kv_cache
        buf = k_cache.shape[1]
        k_all = jnp.concatenate([k_cache.astype(F32), kf], axis=1)
        v_all = jnp.concatenate([v_cache.astype(F32), vf], axis=1)
        for win, dil in A_PATTERNS:
            parts.append(_dilated_gather(qf, k_all, v_all, slopes, dil, win // dil, buf))
        k_rows, v_rows = k_h, v_h
    m = jnp.stack([pt[0] for pt in parts])
    den = jnp.stack([pt[1] for pt in parts])
    num = jnp.stack([pt[2] for pt in parts])
    wgt = jnp.exp(m - m.max(0, keepdims=True))
    o = (wgt[..., None] * num).sum(0) / (wgt * den).sum(0)[..., None]
    y = o.reshape(b, l, A_WIDTH) * jax.nn.silu(gate.astype(F32))
    return y.astype(q.dtype), k_rows, v_rows

def _gated_delta_chunked(q, k, v, g, beta, s0):
    b, h, l, dk = q.shape
    dv = v.shape[-1]
    c = math.gcd(l, DELTA_CHUNK)
    n = l // c

    def rs(t):
        return t.reshape((b, h, n, c) + t.shape[3:])

    q, k, v, g, beta = rs(q), rs(k), rs(v), rs(g), rs(beta)
    gc = jnp.cumsum(g, axis=-1)
    tri = jnp.tril(jnp.ones((c, c), bool))
    decay = jnp.exp(jnp.where(tri, gc[..., :, None] - gc[..., None, :], NEG_MASK))
    kb = k * beta[..., None]
    vb = v * beta[..., None]
    a_mat = jnp.tril(jnp.einsum('bhnid,bhnjd->bhnij', kb, k) * decay, -1)
    t_mat = a_mat + jnp.eye(c, dtype=F32)
    u = lax.linalg.triangular_solve(t_mat, vb, left_side=True, lower=True, unit_diagonal=True)
    w = lax.linalg.triangular_solve(t_mat, kb * jnp.exp(gc)[..., None], left_side=True, lower=True,
                                    unit_diagonal=True)
    qk = jnp.einsum('bhnid,bhnjd->bhnij', q, k) * decay

    def step(s, xs):
        q_n, k_n, u_n, w_n, gc_n, qk_n = xs
        v_new = u_n - jnp.einsum('bhcd,bhde->bhce', w_n, s)
        o = (jnp.einsum('bhcd,bhde->bhce', q_n * jnp.exp(gc_n)[..., None], s)
             + jnp.einsum('bhij,bhje->bhie', qk_n, v_new))
        g_last = gc_n[..., -1]
        s = (s * jnp.exp(g_last)[..., None, None]
             + jnp.einsum('bhcd,bhce->bhde', k_n * jnp.exp(g_last[..., None] - gc_n)[..., None], v_new))
        return s, o

    xs = (q, k, u, w, gc, qk)
    xs = [jnp.moveaxis(t, 2, 0) for t in xs]
    s_fin, o = lax.scan(step, s0, xs)
    o = jnp.moveaxis(o, 0, 2).reshape(b, h, l, dv)
    return o, s_fin

def _mixer_delta(qkv, gate, beta_raw, a_raw, conv_prefix, s0, conv_w, a_log, dt_bias, norm_w):
    b, l, _ = qkv.shape
    xc = jnp.concatenate([conv_prefix.astype(qkv.dtype), qkv], axis=1)
    conv_new = xc[:, xc.shape[1] - (CONV_W - 1):]
    xcf = xc.astype(F32)
    cw = conv_w.astype(F32)
    conv = sum(xcf[:, tap:tap + l] * cw[tap] for tap in range(CONV_W))
    conv = jax.nn.silu(conv)
    q, k, v = jnp.split(conv, 3, axis=-1)

    def heads(t):
        return t.reshape(b, l, B_HEADS, -1).transpose(0, 2, 1, 3)

    q = _l2norm(heads(q)) * (B_DK ** -0.5)
    k = _l2norm(heads(k))
    v = heads(v)
    beta = jax.nn.sigmoid(beta_raw.astype(F32)).transpose(0, 2, 1)
    g = (-jnp.exp(a_log.astype(F32))
         * jax.nn.softplus(a_raw.astype(F32) + dt_bias.astype(F32))).transpose(0, 2, 1)
    o, s_new = _gated_delta_chunked(q, k, v, g, beta, s0.astype(F32))
    o = _rms(o.transpose(0, 2, 1, 3), norm_w).reshape(b, l, B_WIDTH)
    y = o * jax.nn.silu(gate.astype(F32))
    return y.astype(qkv.dtype), conv_new, s_new

def _hgrn_lower_bounds(raw):
    s = jax.nn.softmax(raw.astype(F32), axis=0)
    return jnp.cumsum(s, axis=0) - s[0:1]

def _gla_chunked(q, k, log_f, v, s0):
    b, h, l, dk = q.shape
    dv = v.shape[-1]
    c = math.gcd(l, HGRN_CHUNK)
    n = l // c

    def rs(t):
        return t.reshape((b, h, n, c) + t.shape[3:])

    q, k, log_f, v = rs(q), rs(k), rs(log_f), rs(v)
    gcum = jnp.cumsum(log_f, axis=3)
    tri = jnp.tril(jnp.ones((c, c), bool))
    diff = gcum[:, :, :, :, None, :] - gcum[:, :, :, None, :, :]
    decay = jnp.exp(jnp.where(tri[:, :, None], diff, NEG_MASK))
    a_mat = jnp.einsum('bhnic,bhnijc,bhnjc->bhnij', q, decay, k)
    intra = jnp.einsum('bhnij,bhnje->bhnie', a_mat, v)
    g_last = gcum[:, :, :, -1]
    qg = q * jnp.exp(gcum)
    kg = k * jnp.exp(g_last[:, :, :, None] - gcum)

    def step(s, xs):
        qg_n, kg_n, v_n, intra_n, gl_n = xs
        o = jnp.einsum('bhcd,bhde->bhce', qg_n, s) + intra_n
        s = s * jnp.exp(gl_n)[..., None] + jnp.einsum('bhcd,bhce->bhde', kg_n, v_n)
        return s, o

    xs = [jnp.moveaxis(t, 2, 0) for t in (qg, kg, v, intra, g_last)]
    s_fin, o = lax.scan(step, s0, xs)
    o = jnp.moveaxis(o, 0, 2).reshape(b, h, l, dv)
    return o, s_fin

def _mixer_hgrn(q, f_raw, i, gate, lb, s0, norm_w):
    b, l, _ = q.shape

    def heads(t):
        return t.astype(F32).reshape(b, l, C_HEADS, -1).transpose(0, 2, 1, 3)

    qh = jax.nn.silu(heads(q))
    fr = heads(f_raw)
    lbh = lb.reshape(C_HEADS, 1, C_DK)
    f = lbh + (1.0 - lbh) * jax.nn.sigmoid(fr)
    log_f = jnp.log(f)
    kh = (1.0 - lbh) * jax.nn.sigmoid(-fr)
    vh = heads(i)
    o, s_new = _gla_chunked(qh, kh, log_f, vh, s0.astype(F32))
    o = _rms(o.transpose(0, 2, 1, 3), norm_w).reshape(b, l, C_WIDTH)
    y = o * jax.nn.silu(gate.astype(F32))
    return y.astype(q.dtype), s_new

def _mixer_pool(xd, gate, prefix, start_pos, pool_w, pool_scale):
    b, l, _ = xd.shape
    p_len = POOL_MAX - 1
    xc = jnp.concatenate([prefix.astype(xd.dtype), xd], axis=1)
    pool_new = xc[:, xc.shape[1] - p_len:]
    xcf = xc.astype(F32)
    cs = jnp.concatenate([jnp.zeros((b, 1, D_WIDTH), F32), jnp.cumsum(xcf, axis=1)], axis=1)
    pos = start_pos + jnp.arange(l)
    means = []
    for gi, win in enumerate(POOL_WINDOWS):
        lo, hi = gi * D_GROUP_W, (gi + 1) * D_GROUP_W
        tot = cs[:, p_len + 1:p_len + 1 + l, lo:hi] - cs[:, p_len + 1 - win:p_len + 1 - win + l, lo:hi]
        cnt = jnp.minimum(pos + 1, win).astype(F32)
        means.append(tot / cnt[None, :, None])
    pooled = (jnp.concatenate(means, axis=-1) - xcf[:, p_len:]).reshape(b, l, D_GROUPS, D_GROUP_W)
    y = jnp.einsum('blgc,gcd->blgd', pooled, pool_w.astype(F32)).reshape(b, l, D_WIDTH)
    y = y * pool_scale.astype(F32) * jax.nn.silu(gate.astype(F32))
    return y.astype(xd.dtype), pool_new

def _trunk(x, start_pos, states, norm_w, w_in, w_out, delta_conv_w, delta_a_log, delta_dt_bias,
           delta_norm_w, hgrn_lb_raw, hgrn_norm_w, pool_w, pool_scale, final_norm_w):
    b = x.shape[0]
    dt = x.dtype
    split_pts = [int(s) for s in np.cumsum(IN_SPLITS)[:-1]]
    lower_bounds = _hgrn_lower_bounds(hgrn_lb_raw)
    ks, vs, ds, dcs, hs, ps = [], [], [], [], [], []
    for layer in range(DEPTH):
        if states is None:
            kv = None
            conv_prefix = jnp.zeros((b, CONV_W - 1, 3 * B_WIDTH), dt)
            s_delta = jnp.zeros((b, B_HEADS, B_DK, B_DV), F32)
            s_hgrn = jnp.zeros((b, C_HEADS, C_DK, C_DV), F32)
            pool_prefix = jnp.zeros((b, POOL_MAX - 1, D_WIDTH), dt)
        else:
            c_k, c_v, c_delta, c_conv, c_hgrn, c_pool = states
            kv = (c_k[layer], c_v[layer])
            conv_prefix = c_conv[layer]
            s_delta = c_delta[layer]
            s_hgrn = c_hgrn[layer]
            pool_prefix = c_pool[layer]
        h = _rms(x, norm_w[layer]).astype(dt)
        p = h @ w_in[layer]
        (a_q, a_k, a_v, a_g, b_qkv, b_g, b_beta, b_a,
         c_q, c_f, c_i, c_g, d_x, d_g) = jnp.split(p, split_pts, axis=-1)
        y_a, k_rows, v_rows = _mixer_attn(a_q, a_k, a_v, a_g, kv)
        y_b, conv_new, sd_new = _mixer_delta(b_qkv, b_g, b_beta, b_a, conv_prefix, s_delta,
                                             delta_conv_w[layer], delta_a_log[layer],
                                             delta_dt_bias[layer], delta_norm_w[layer])
        y_c, sh_new = _mixer_hgrn(c_q, c_f, c_i, c_g, lower_bounds[layer], s_hgrn, hgrn_norm_w[layer])
        y_d, pool_new = _mixer_pool(d_x, d_g, pool_prefix, start_pos, pool_w[layer], pool_scale[layer])
        y = jnp.concatenate([y_a, y_b, y_c, y_d], axis=-1) @ w_out[layer]
        x = x + y
        ks.append(k_rows)
        vs.append(v_rows)
        ds.append(sd_new)
        dcs.append(conv_new)
        hs.append(sh_new)
        ps.append(pool_new)
    out = _rms(x, final_norm_w).astype(dt)
    return out, (jnp.stack(ks), jnp.stack(vs), jnp.stack(ds), jnp.stack(dcs), jnp.stack(hs), jnp.stack(ps))

def setup_inputs(seed: int = 0) -> dict:
    key = jax.random.key(seed)
    ks = jax.random.split(key, 24)
    a_buf = min(A_WINDOW_MAX, PAST_LEN)

    def nrm(k, shape, scale):
        return scale * jax.random.normal(k, shape, F32)

    dt_init = jnp.exp(jax.random.uniform(ks[13], (DEPTH, B_HEADS), F32, math.log(1e-3), math.log(1e-1)))
    return {
        'x_prompt': nrm(ks[0], (BATCH, SEQ, D_MODEL), 1.0),
        'x_sample': nrm(ks[1], (DEC_BATCH, DEC_SEQ, D_MODEL), 1.0),
        'cache_attn_k': nrm(ks[2], (DEPTH, DEC_BATCH, a_buf, A_HEADS, A_HEAD_DIM), 1.0),
        'cache_attn_v': nrm(ks[3], (DEPTH, DEC_BATCH, a_buf, A_HEADS, A_HEAD_DIM), 1.0),
        'state_delta': nrm(ks[4], (DEPTH, DEC_BATCH, B_HEADS, B_DK, B_DV), 0.1),
        'state_delta_conv': nrm(ks[5], (DEPTH, DEC_BATCH, CONV_W - 1, 3 * B_WIDTH), 1.0),
        'state_hgrn': nrm(ks[6], (DEPTH, DEC_BATCH, C_HEADS, C_DK, C_DV), 0.3),
        'state_pool': nrm(ks[7], (DEPTH, DEC_BATCH, POOL_MAX - 1, D_WIDTH), 1.0),
        'norm_w': 1.0 + nrm(ks[8], (DEPTH, D_MODEL), 0.1),
        'w_in': nrm(ks[9], (DEPTH, D_MODEL, IN_WIDTH), D_MODEL ** -0.5),
        'w_out': nrm(ks[10], (DEPTH, MIX_WIDTH, D_MODEL), MIX_WIDTH ** -0.5),
        'delta_conv_w': nrm(ks[11], (DEPTH, CONV_W, 3 * B_WIDTH), CONV_W ** -0.5),
        'delta_a_log': jnp.log(jax.random.uniform(ks[12], (DEPTH, B_HEADS), F32, 1.0, 16.0)),
        'delta_dt_bias': dt_init + jnp.log(-jnp.expm1(-dt_init)),
        'delta_norm_w': 1.0 + nrm(ks[14], (DEPTH, B_DV), 0.1),
        'hgrn_lb_raw': 1.0 + nrm(ks[15], (DEPTH, C_WIDTH), 0.1),
        'hgrn_norm_w': 1.0 + nrm(ks[16], (DEPTH, C_DV), 0.1),
        'pool_w': nrm(ks[17], (DEPTH, D_GROUPS, D_GROUP_W, D_GROUP_W), D_GROUP_W ** -0.5),
        'pool_scale': 1.0 + nrm(ks[18], (DEPTH, D_WIDTH), 0.1),
        'final_norm_w': 1.0 + nrm(ks[19], (D_MODEL,), 0.1),
    }

def reference(x_prompt, x_sample, cache_attn_k, cache_attn_v, state_delta, state_delta_conv, state_hgrn,
              state_pool, norm_w, w_in, w_out, delta_conv_w, delta_a_log, delta_dt_bias, delta_norm_w,
              hgrn_lb_raw, hgrn_norm_w, pool_w, pool_scale, final_norm_w):
    y_prompt, st_p = _trunk(x_prompt, 0, None, norm_w, w_in, w_out, delta_conv_w, delta_a_log,
                            delta_dt_bias, delta_norm_w, hgrn_lb_raw, hgrn_norm_w, pool_w, pool_scale,
                            final_norm_w)
    y_sample, st_s = _trunk(x_sample, PAST_LEN,
                            (cache_attn_k, cache_attn_v, state_delta, state_delta_conv, state_hgrn, state_pool),
                            norm_w, w_in, w_out, delta_conv_w, delta_a_log, delta_dt_bias, delta_norm_w,
                            hgrn_lb_raw, hgrn_norm_w, pool_w, pool_scale, final_norm_w)
    k_p, v_p, d_p, dc_p, h_p, pl_p = st_p
    k_s, v_s, d_s, dc_s, h_s, pl_s = st_s
    return (y_prompt, y_sample, k_p, k_s, v_p, v_s, d_p, d_s, dc_p, dc_s, h_p, h_s, pl_p, pl_s)


_drawn_inputs = setup_inputs


def setup_inputs(seed=0):
    import zlib

    import numpy as np

    out = dict(_drawn_inputs(seed))
    spreads = {}
    factors = {'state_hgrn': 3.45}
    for name, (base, spread) in spreads.items():
        noise = np.random.default_rng([zlib.crc32(name.encode()), seed]).standard_normal(out[name].shape)
        drawn = base * np.exp(spread * noise) if base else spread * noise
        out[name] = jnp.asarray(drawn.astype(out[name].dtype))
    for name, factor in factors.items():
        out[name] = (out[name] * factor).astype(out[name].dtype)
    return out
```

```python
from contextlib import ExitStack

import numpy as np

import concourse.bass as bass
from concourse import mybir

F32 = mybir.dt.float32
ALU = mybir.AluOpType
ACT = mybir.ActivationFunctionType
AX_X = mybir.AxisListType.X

P = 128
DM = 1024
KD = DM // P
SEQ = 4096
NT = SEQ // P
DB, DS = 8, 8
TS = DB * DS
H, D = 4, 64
BW = H * D
AW = 4 * BW
CONV = 4
PMAX = 16
POOL_WINDOWS = (2, 4, 8, 16)
EPS = 1e-6
NEG = -1e30
MW = 3 * BW + BW + 2 * H + 4 * BW + 2 * BW
GROUPS = ((0, 512), (512, 512), (1032, 512), (1544, 512), (2056, 512), (1024, 8))
Q_QKV, Q_GB, Q_CQ, Q_CF, Q_CI, Q_CG, Q_DX, Q_DG, Q_BETA, Q_A = (
    0, 768, 1024, 1280, 1536, 1792, 2048, 2304, 2560, 2564)
LEVELS = {P: 7, TS: 3}


def _segments(rows):
    seg = rows if rows == P else DS
    return np.arange(rows), seg


def tile_constants(rows):
    n, seg = _segments(rows)
    j, i = n[:, None], n[None, :]
    same = (j // seg) == (i // seg)
    tri = (same & (j <= i)).astype(np.float32)
    neg = np.where(tri > 0, 0.0, NEG).astype(np.float32)
    parts = [tri, same.astype(np.float32), neg]
    s = 1
    while s < seg:
        parts.append((((j // s) % 2 == 0) & ((i // s) % 2 == 1)
                      & (j // (2 * s) == i // (2 * s)) & same).astype(np.float32))
        s *= 2
    parts.append((np.arange(rows // seg)[None, :] == (n // seg)[:, None]).astype(np.float32))
    return np.concatenate(parts, axis=1)


def pool_constants(rows, first):
    n, seg = _segments(rows)
    own, before = [], []
    for win in POOL_WINDOWS:
        j, i = n[:, None], n[None, :]
        cnt = np.minimum(i + 1, win) if first else np.full_like(i, win)
        near = (i - j >= 0) & (i - j < win) & ((j // seg) == (i // seg))
        own.append(near / cnt - (i == j))
        m = np.zeros((P, rows))
        if rows == P:
            dist = i - (n[:, None] - P)
            if not first:
                m = (dist < win) / cnt
        else:
            r = np.arange(DB * (PMAX - 1))[:, None]
            dist = (i % seg) - (r % (PMAX - 1) - (PMAX - 1))
            m[:r.size] = ((dist < win) & (r // (PMAX - 1) == i // seg)) / cnt
        before.append(m)
    own = [np.concatenate([o, np.zeros((P - rows, rows))]) for o in own]
    return np.concatenate(own + before, axis=1).astype(np.float32)


def host_constants():
    cols, parts, at = {}, [], 0
    for name, a in (("ident", np.eye(P, dtype=np.float32)),
                    ("tile_p", tile_constants(P)), ("tile_s", tile_constants(TS)),
                    ("pool_s", pool_constants(TS, False)), ("pool_0", pool_constants(P, True)),
                    ("pool_p", pool_constants(P, False)), ("cache", cache_constants()),
                    *((f"alibi_{d}_{f}", alibi_constants(d, f)) for d in DILATIONS for f in (0, 1))):
        full = np.zeros((P, a.shape[1]), np.float32)
        full[:a.shape[0]] = a
        cols[name] = at
        at += a.shape[1]
        parts.append(full)
    return np.concatenate(parts, axis=1), cols


class Tile:

    def __init__(self, rows, t, row=0, first=False, last=False):
        self.rows, self.t, self.row, self.first, self.last = rows, t, row, first, last
        self.sample = rows == TS
        self.segs = DB if self.sample else 1
        self.seg = rows // self.segs
        self.levels = LEVELS[rows]


class Count:

    def __init__(self, sem, per=1, first=0):
        self.sem, self.per, self.first = sem, per, first

    def wait(self, eng, tile, k=None):
        k = self.per if k is None else k
        if isinstance(tile.t, int) and tile.t <= self.first and k == 0:
            return
        eng.wait_ge(self.sem, tile.t * self.per + (k - self.first * self.per))


class Steps:

    def __init__(self, count, eng):
        self.count, self.eng, self.k = count, eng, 0

    def begin(self, tile):
        self.tile, self.k = tile, 0

    def do(self, ins):
        ins.then_inc(self.count.sem, 1)
        self.k += 1

    def sync(self):
        self.count.wait(self.eng, self.tile, self.k)

    def end(self):
        assert self.k == self.count.per, (self.count.sem, self.k, self.count.per)


def rows_of(tile, dram):
    if isinstance(tile.row, int):
        return dram[tile.row:tile.row + tile.rows, :]
    return dram[bass.ds(tile.row, tile.rows), :]


MIX_STEPS = {"prompt": (42, 19, 10), "sample": (61, 22, 6)}


ACT_FILLS = (0, 2, 4)


def mixers(nc, io, consts, ccols, kind):
    prompt = kind == "prompt"
    R = P if prompt else TS
    SEGS = 1 if prompt else DB
    SEG = R // SEGS
    NL = LEVELS[R]
    FIRST = 1 if prompt else 0
    NB = P if prompt else DB * (PMAX - 1)
    with ExitStack() as ctx:
        sems = []

        def sb(name, shape):
            return ctx.enter_context(nc.sbuf_tensor(f"{kind}_{name}", shape, F32))

        def semaphore(name):
            sems.append(ctx.enter_context(nc.semaphore(f"{kind}_{name}")))
            return sems[-1]

        ident = sb("ident", [P, P])
        mask = sb("mask", [R, 3 * R + NL * R + SEGS])
        pool_step = sb("pool_step", [P, 8 * R])
        pool_first = sb("pool_first", [P, 4 * R]) if prompt else pool_step
        convw = sb("convw", [P, 6, CONV])
        gatew = sb("gatew", [P, 2 * BW])
        pscale = sb("pscale", [P, BW])
        poolw = sb("poolw", [D, 4, D])
        ealog = sb("ealog", [P, H])
        dtb = sb("dtb", [P, H])
        one = sb("one", [P, 1])
        eps = sb("eps", [P, 1])
        pt = sb("pt", [P, MW])
        if prompt:
            w = sb("w", [P, KD, MW])
            normw = sb("normw", [P, KD])
            xin = sb("xin", [P, DM])
            xn = sb("xn", [P, DM])
            rstd = sb("rstd", [P, 2])
            hT = sb("hT", [P, KD, P])
        else:
            before = sb("before", [P, 3 * BW])

        xc = sb("xc", [P, 6, SEGS, SEG + CONV - 1])
        levels_a = sb("levels_a", [P, 2, H * P])
        cvs = levels_a[:, :, :].rearrange("p a n -> p (a n)")[:, 0:6 * R].rearrange("p (k t) -> p k t", k=6)
        X, Y = (levels_a[0:R, n, 0:H * R].rearrange("p (h t) -> p h t", h=H) for n in range(2))
        levels_b = sb("levels_b", [P, 2, H * P])
        sig_c = levels_b[:, :, :].rearrange("p a n -> p (a n)")[:, 0:6 * R].rearrange("p (k t) -> p k t", k=6)
        Am = [levels_b[0:R, n, 0:H * R].rearrange("p (h t) -> p h t", h=H) for n in range(2)]
        Z = sb("Z", [R, H, R])
        sq = sb("sq", [R, 8, D])
        qk = sb("qk", [R, 8, D])
        vB = sb("vB", [R, H, D])
        ss8 = sb("ss8", [R, 8])
        kb = sb("kb", [R, H, D])
        qg = sb("qg", [R, H, D])
        kbg = sb("kbg", [R, H, D])
        kend = sb("kend", [R, H, D])
        vb = sb("vb", [R, H, D])
        knT, kbT, qnT = (sb(n, [D, H, R]) for n in ("knT", "kbT", "qnT"))
        gcol = sb("gcol", [R, 2, H])
        gb = sb("gb", [R, H, R])
        dec = sb("dec", [R, H, R])
        At = sb("At", [R, H, R])
        QKt = sb("QKt", [R, H, R])
        vn = sb("vn", [R, H, D])
        WIDE = H * R if prompt else H * DB * (TS + DS)
        wTx = sb("wTx", [D, WIDE])
        qgx = sb("qgx", [D, WIDE])
        qcgx = wTx
        SB = sb("SB", [D, H, SEGS, D])
        eglB = sb("eglB", [D, H, SEGS])
        sig = sb("sig", [R, 4, BW])
        bet = sb("bet", [R, H])
        zf = sb("zf", [R, BW + H])
        lab = sb("lab", [R, BW + H])
        ls = sb("ls", [R, BW + H])
        vC = sb("vC", [R, H, D])
        G = sb("G", [D, H, R])
        kgT = sb("kgT", [D, H, R])
        EG = sb("EG", [D, H, R])
        qcT, kcT = sb("qcT", [D, H, R]), sb("kcT", [D, H, R])
        kg = sb("kg", [R, H, D])
        Ml = [sb(f"Ml{n}", [D, H, R]) for n in range(2)]
        acc = sb("acc", [R, H, R])
        tmp = sb("tmp", [R, H, R])
        eglC = sb("eglC", [D, H, SEGS])
        SC = sb("SC", [D, H, SEGS, D])
        xd = sb("xd", [P, BW])
        xdp = sb("xdp", [P, BW])
        pT = sb("pT", [D, 4, R])
        oBC = sb("oBC", [R, 8, D])
        y = sb("y", [R, 3 * BW])
        if not prompt:
            vBx, vCx = sb("vBx", [R, H, DB, D]), sb("vCx", [R, H, DB, D])
        else:
            vBx, vCx = vn, vC

        def bank(name):
            return ctx.enter_context(nc.psum_tensor(f"{kind}_{name}", [P, 512], F32))

        pj = [bank("pj0"), bank("pj1")]
        c = [bank(f"c{n}") for n in range(6)]

        tri, same, neg = (mask[:, n * R:(n + 1) * R] for n in range(3))
        level = [mask[:, (3 + n) * R:(4 + n) * R] for n in range(NL)]
        segm = mask[:, (3 + NL) * R:(3 + NL) * R + SEGS]

        def pool_matrix(tile, g):
            own = pool_first if tile.first else pool_step
            return own[0:R, g * R:(g + 1) * R], pool_step[0:NB, (4 + g) * R:(5 + g) * R]

        def hv(b, rows=R, width=R):
            return b[0:rows, 0:H * width].rearrange("p (h n) -> p h n", h=H)

        def window(buf, h, b):
            per = WIDE // H
            return buf[:, h * per + b * R:h * per + (b + 1) * R]

        def own_columns(buf):
            v = buf[:, :].rearrange("d (h t) -> d h t", h=H)
            if prompt:
                return v
            return buf[:, :].rearrange("d (h b t) -> d h b t", h=H, b=SEGS)[:, :, :, 0:SEG]

        def fm(ap):
            return ap if prompt else ap.rearrange("d h (b t) -> d h b t", b=SEGS)

        def halves(t, k):
            return t[:, :, :].rearrange("d h (n a s) -> d (h n) a s", a=2, s=2 ** k)

        S = {}
        mixed = """fwd_ps xc_ready halo_ready cv_ready sigc_ready cvs_ready back_ps qkv_tm ss_ready rn_ready
            qk_normed th_ready sg_ready zf_ready lab_ready ls_ready g_ready gb_ready lk_ready kC_ready
            vC_ready xd_ready xdp_ready pool_ps pT_ready poolw_ps yD_ready G_ps G_ready gcol_ps gcol_tm
            gcol_ready R_ps R_read dec_in dec_ready kb_ready qg_ready scaled_ready knT_ps
            kbT_ps qnT_ps qgT_ps qcT_ps kcT_ps knT_ready kbT_ready qnT_ready qgx_ready qcT_ready kcT_ready
            kk_ps kq_ps At_ready QKt_ready EL_in EL_ready kgT_ready wT_ps wT_ready vn_ps vn_ready
            vBx_ready vCx_ready oB_ps dSB_ps SB_ready kg_ps kg_ready qcg_ready oC_ps dSC_ps SC_ready
            oB_tm oC_tm ss2_ready rn2_ready gates_ready y_ready ecol_ready pscaled_ready""".split()
        for n in mixed:
            S[n] = Count(semaphore(n), 1, FIRST)
        for n, per in (("am_ready", NL), ("z_ps", NL), ("z_ready", NL - 1), ("xz_ps", NL - 2),
                       ("zy_ps", NL - 1), ("X_ready", NL - 1), ("Y_ready", NL), ("tmp_ready", NL), ("cd_ready", NL), ("ce_ready", NL), ("cl_ready", NL),
                       ("cprod_ps", NL + 1), ("cacc_ready", NL + 1), ("y_out", 16)):
            S[n] = Count(semaphore(n), per, FIRST)
        if prompt:
            for n, per in (("x_in", 16), ("sq_ready", 1), ("lnx_ready", 1), ("rstd_ready", 1), ("xn_ready", 1), ("ht_ps", 2), ("hT_ready", 2),
                           ("pj_ps", 6), ("pt_ready", 6)):
                S[n] = Count(semaphore(n), per)
            spill = semaphore("spill")
        loads, setup, state_out = semaphore("loads"), semaphore("setup"), semaphore("state_out")
        halved = semaphore("halved")
        steps_of = dict(zip(("dve", "act", "pool"), MIX_STEPS[kind]))
        own_steps = {e: Count(semaphore(f"{e}_steps"), n, FIRST) for e, n in steps_of.items()}
        n_loads, n_setup = (16 if prompt else 21), 10

        def need(eng, name, tile, k=None):
            S[name].wait(eng, tile, k)

        def free(eng, name, tile):
            S[name].wait(eng, tile, 0)

        def done(ins, name):
            ins.then_inc(S[name].sem, 1)

        def run(eng, iteration):
            if not prompt:
                iteration(None, Tile(TS, 0, SEQ), None)
                return
            own = Tile(TS, 0, 0)
            tile = lambda n, **k: Tile(P, n + 1, n * P, **k)
            iteration(None, None, own)
            iteration(own, None, tile(0))
            iteration(tile(0), None, tile(1))
            iteration(tile(1), tile(0, first=True), tile(2))
            with eng.Fori(2, NT - 1) as i:
                iteration(tile(i), tile(i - 1), tile(i + 1))
            iteration(tile(NT - 1), tile(NT - 2), None)
            iteration(None, tile(NT - 1, last=True), None)

        program = ExitStack()
        block = program.enter_context(nc.Block())

        @block.sync
        def _(sp):
            sent = [0]

            def load(dst, src):
                sp.dma_start(dst, src).then_inc(loads, 16)
                sent[0] += 1

            cx = ccols["tile_p" if prompt else "tile_s"]
            cp = ccols["pool_p" if prompt else "pool_s"]
            if prompt:
                win = io["w_in"][0].rearrange("(k p) n -> p k n", p=P)
                for k in range(4):
                    load(w[:, 2 * k:2 * k + 2, :], win[:, 2 * k:2 * k + 2, AW:AW + MW])
                load(normw[:, :], io["norm_w_fm"])
                load(pool_first[:, :], consts[:, ccols["pool_0"]:ccols["pool_0"] + 4 * R])
            else:
                load(pt[0:R, :], io["sample_rows"])
                load(before[0:DB * 3, :], io["state_delta_conv"][0].rearrange("b r n -> (b r) n"))
                load(xdp[0:NB, :], io["state_pool"][0].rearrange("b r n -> (b r) n"))
                for h in range(H):
                    load(SB[:, h, :, :], io["state_delta"][0][:, h].rearrange("b k v -> k b v"))
                    load(SC[:, h, :, :], io["state_hgrn"][0][:, h].rearrange("b k v -> k b v"))
            load(ident[:, :], consts[:, ccols["ident"]:ccols["ident"] + P])
            load(mask[:, :], consts[0:R, cx:cx + 3 * R + NL * R + SEGS])
            load(pool_step[:, :], consts[:, cp:cp + 8 * R])
            load(convw[:, :, :], io["conv_w_fm"])
            for n, name in enumerate(("delta_norm_w", "hgrn_norm_w")):
                load(gatew[:, n * BW:n * BW + D], io[name].broadcast_to([P, D]))
            load(pscale[:, :], io["pool_scale"].broadcast_to([P, BW]))
            load(poolw[:, :, :], io["pool_w"][0].rearrange("g c d -> c g d"))
            load(ealog[:, :], io["delta_a_log"].broadcast_to([P, H]))
            load(dtb[:, :], io["delta_dt_bias"].broadcast_to([P, H]))
            assert sent[0] == n_loads, sent[0]

            def iteration(pr, ch, nm):
                if nm:
                    free(sp, "xn_ready", nm)
                    sp.dma_start(xin[0:nm.rows, :], rows_of(nm, io["x_s" if nm.sample else "x_p"]))\
                        .then_inc(S["x_in"].sem, 16)
                if pr and pr.sample:
                    need(sp, "pt_ready", pr)
                    sp.dma_start(io["sample_rows"], pt[0:TS, :]).then_inc(spill, 16)

            run(sp, iteration)
            n_out = 0
            if prompt:
                sp.wait_ge(spill, 16)
                need(sp, "pt_ready", Tile(P, NT))
                sp.dma_start(io["conv_p"], pt[P - 3:P, 0:3 * BW]).then_inc(state_out, 16)
                sp.dma_start(io["pool_p"], pt[P - 15:P, Q_DX:Q_DX + BW]).then_inc(state_out, 16)
                last = Tile(P, NT)
            else:
                rows = io["sample_rows"].rearrange("(b s) n -> b s n", s=DS)
                sp.dma_start(io["conv_s"], rows[:, DS - 3:DS, 0:3 * BW]).then_inc(state_out, 16)
                sp.dma_start(io["pool_s"][:, 7:15, :], rows[:, :, Q_DX:Q_DX + BW]).then_inc(state_out, 16)
                sp.dma_start(io["pool_s"][:, 0:7, :], io["state_pool"][0][:, 8:15, :])\
                    .then_inc(state_out, 16)
                n_out = 1
                last = Tile(TS, 0)
            need(sp, "SB_ready", last)
            need(sp, "SC_ready", last)
            for h in range(H):
                for name, state in (("delta", SB), ("hgrn", SC)):
                    out = io[f"{name}_{kind}"][:, h].rearrange("b k v -> k b v")
                    sp.dma_start(out, state[:, h, :, :]).then_inc(state_out, 16)
            sp.wait_ge(state_out, 16 * (2 + n_out + 2 * H))
            need(sp, "y_out", last)

        @block.tensor
        def _(pe):
            mm = nc.tensor.matmul

            def transpose(out, in_):
                k = in_.shape[0]
                return nc.tensor.transpose(out, in_, ident[0:k, 0:k])

            pe.wait_ge(loads, n_loads * 16)
            if not prompt:
                for n in range(6):
                    last = transpose(c[5][:, 24 * n:24 * n + 24], before[0:24, P * n:P * n + P])
                last.then_inc(setup, 1)
            pe.wait_ge(setup, n_setup)

            def norm_transposes(tile):
                r = tile.rows
                need(pe, "xn_ready", tile)
                for half in range(2):
                    for k in range(4):
                        kk = 4 * half + k
                        last = transpose(pj[half][:, k * r:(k + 1) * r], xn[0:r, kk * P:(kk + 1) * P])
                    done(last, "ht_ps")

            def project(tile, g, k):
                at, n = GROUPS[g]
                if k == 0 and g < 2:
                    need(pe, "hT_ready", tile)
                if k == 0 and g >= 2:
                    need(pe, "pt_ready", tile, g - 1)
                last = mm(pj[g % 2][0:tile.rows, 0:n], hT[:, k, 0:tile.rows], w[:, k, at:at + n],
                          start=(k == 0), stop=(k == KD - 1))
                if k == KD - 1:
                    done(last, "pj_ps")

            def each_head(bank, width, lhs, rhs, name, rows=R):
                for h in range(H):
                    last = mm(bank[0:rows, h * width:(h + 1) * width], lhs(h), rhs(h),
                              start=True, stop=True)
                if name:
                    done(last, name)

            def settled():
                pe.wait_ge(setup, n_setup)

            def heads_to_fm(bank, src, name):
                for h in range(H):
                    last = transpose(bank[0:D, h * R:(h + 1) * R], src(h))
                done(last, name)

            def iteration(pr, ch, nm):
                part = [0]

                def fill(n):
                    for _ in range(n):
                        if pr and part[0] < 6 * KD:
                            project(pr, part[0] // KD, part[0] % KD)
                            part[0] += 1

                if ch:
                    mix(ch, fill)
                fill(6 * KD)
                if nm:
                    if pr:
                        need(pe, "pt_ready", pr)
                    norm_transposes(nm)

            def mix(ch, fill):
                if prompt:
                    need(pe, "pt_ready", ch)
                free(pe, "SC_ready", ch)
                free(pe, "vn_ready", ch)
                for n in range(6):
                    b, k = (c[0], n) if n < 4 else (c[1], n - 4)
                    last = transpose(b[:, k * R:(k + 1) * R], pt[0:R, n * P:(n + 1) * P])
                done(last, "fwd_ps")
                need(pe, "xd_ready", ch)
                free(pe, "xdp_ready", ch)
                free(pe, "oB_tm", ch)
                for g in range(4):
                    own, prev = pool_matrix(ch, g)
                    out = c[2][0:D, g * R:(g + 1) * R]
                    mm(out, xd[0:R, g * D:(g + 1) * D], own, start=True, stop=False)
                    last = mm(out, xdp[0:NB, g * D:(g + 1) * D], prev, start=False, stop=True)
                done(last, "pool_ps")
                fill(4)
                need(pe, "ls_ready", ch)
                free(pe, "oC_tm", ch)
                each_head(c[5], R, lambda h: ls[:, h * D:(h + 1) * D], lambda h: tri, "G_ps", D)
                need(pe, "gb_ready", ch)
                free(pe, "kg_ready", ch)
                mm(c[4][0:R, 0:H], tri, gb[:, :, 0], start=True, stop=True)
                last = mm(c[4][0:R, H:2 * H], same, gb[:, :, 0], start=True, stop=True)
                done(last, "gcol_ps")
                free(pe, "SB_ready", ch)
                each_head(c[3], R, lambda h: gb[:, h, :], lambda h: tri, "R_ps")
                fill(1)
                need(pe, "pT_ready", ch)
                each_head(c[2], D, lambda g: pT[:, g, :], lambda g: poolw[:, g, :], "poolw_ps")
                fill(6)
                settled()
                need(pe, "sg_ready", ch)
                need(pe, "R_read", ch)
                heads_to_fm(c[3], lambda h: sig[:, 1, h * D:(h + 1) * D], "qcT_ps")
                need(pe, "cvs_ready", ch)
                for n in range(6):
                    b, k = (c[0], n) if n < 4 else (c[1], n - 4)
                    last = transpose(b[0:R, k * P:(k + 1) * P], cvs[:, n, :])
                done(last, "back_ps")
                fill(2)
                settled()
                need(pe, "kC_ready", ch)
                need(pe, "gcol_tm", ch)
                heads_to_fm(c[4], lambda h: zf[:, h * D:(h + 1) * D], "kcT_ps")
                need(pe, "qcT_ready", ch)
                need(pe, "kcT_ready", ch)
                each_head(c[4], R, lambda h: kcT[:, h, :], lambda h: qcT[:, h, :], "cprod_ps")
                fill(3)
                settled()
                need(pe, "qk_normed", ch)
                heads_to_fm(c[0], lambda h: qk[:, 4 + h, :], "knT_ps")
                settled()
                need(pe, "kb_ready", ch)
                heads_to_fm(c[1], lambda h: kb[:, h, :], "kbT_ps")
                settled()
                need(pe, "yD_ready", ch)
                heads_to_fm(c[2], lambda h: qk[:, h, :], "qnT_ps")
                settled()
                need(pe, "G_ready", ch)
                need(pe, "qg_ready", ch)
                heads_to_fm(c[5], lambda h: qg[:, h, :], "qgT_ps")
                c_level(ch, 0)
                need(pe, "knT_ready", ch)
                need(pe, "kbT_ready", ch)
                each_head(c[0], R, lambda h: knT[:, h, :], lambda h: kbT[:, h, :], "kk_ps")
                need(pe, "qnT_ready", ch)
                each_head(c[1], R, lambda h: knT[:, h, :], lambda h: qnT[:, h, :], "kq_ps")
                fill(2)
                for k in range(NL):
                    need(pe, "am_ready", ch, k + 1)
                    if k:
                        need(pe, "X_ready", ch, k)
                    else:
                        need(pe, "At_ready", ch)
                    each_head(c[0], R, lambda h: Am[k % 2][:, h, :],
                              lambda h: X[:, h, :] if k else ident[0:R, 0:R], "z_ps")
                    if k + 1 < NL:
                        c_level(ch, k + 1)
                    if k:
                        need(pe, "z_ready", ch, k)
                        need(pe, "Y_ready", ch, k)
                        if k < NL - 1:
                            if k == 1:
                                need(pe, "QKt_ready", ch)
                            each_head(c[1], R, lambda h: Y[:, h, :], lambda h: Z[:, h, :], "xz_ps")
                        if k == 1:
                            need(pe, "qnT_ready", ch)
                        each_head(c[2], R, lambda h: Z[:, h, :], lambda h: Y[:, h, :], "zy_ps")
                    fill(3 if k < NL - 1 else 2)
                need(pe, "Y_ready", ch, NL)
                need(pe, "scaled_ready", ch)
                each_head(c[0], R, lambda h: kbg[:, h, :], lambda h: Y[:, h, :], "wT_ps", D)
                settled()
                need(pe, "kgT_ready", ch)
                need(pe, "tmp_ready", ch, NL)
                for h in range(H):
                    last = transpose(c[4][0:R, h * D:(h + 1) * D], kgT[:, h, :])
                done(last, "kg_ps")
                fill(1)
                need(pe, "wT_ready", ch)
                free(pe, "SB_ready", ch)
                for h in range(H):
                    out = c[1][0:R, h * D:(h + 1) * D]
                    mm(out, Y[:, h, :], vb[:, h, :], start=True, stop=False)
                    for b in range(SEGS):
                        last = mm(out, window(wTx, h, b), SB[:, h, b, :], start=False,
                                  stop=(b == SEGS - 1))
                done(last, "vn_ps")
                fill(2)
                need(pe, "vn_ready", ch)
                need(pe, "qgx_ready", ch)
                for h in range(H):
                    out = c[2][0:R, h * D:(h + 1) * D]
                    for b in range(SEGS):
                        mm(out, window(qgx, h, b), SB[:, h, b, :], start=(b == 0), stop=False)
                    last = mm(out, QKt[:, h, :], vn[:, h, :], start=False, stop=True)
                done(last, "oB_ps")
                need(pe, "qcT_ready", ch)
                need(pe, "kg_ready", ch)
                if not prompt:
                    need(pe, "vBx_ready", ch)
                for h in range(H):
                    out = c[3][0:D, h * D:(h + 1) * D] if prompt else (c[3], c[4], c[0], c[1])[h][0:D, :]
                    v = vBx[:, h, :] if prompt else vBx[:, h, :, :]
                    last = mm(out, kend[:, h, :], v, start=True, stop=True)
                done(last, "dSB_ps")
                fill(1)
                need(pe, "qcg_ready", ch)
                need(pe, "cacc_ready", ch)
                free(pe, "SC_ready", ch)
                for h in range(H):
                    out = c[5][0:R, h * D:(h + 1) * D]
                    for b in range(SEGS):
                        mm(out, window(qcgx, h, b), SC[:, h, b, :], start=(b == 0), stop=False)
                    last = mm(out, acc[:, h, :], vC[:, h, :], start=False, stop=True)
                done(last, "oC_ps")
                need(pe, "SB_ready", ch)
                if not prompt:
                    need(pe, "vCx_ready", ch)
                for h in range(H):
                    out = c[0][0:D, h * D:(h + 1) * D] if prompt else (c[0], c[1], c[3], c[4])[h][0:D, :]
                    v = vCx[:, h, :] if prompt else vCx[:, h, :, :]
                    last = mm(out, kg[:, h, :], v, start=True, stop=True)
                done(last, "dSC_ps")

            def c_level(ch, k):
                need(pe, "cl_ready", ch, k + 1)
                if k:
                    need(pe, "tmp_ready", ch, k)
                else:
                    need(pe, "cacc_ready", ch, 1)
                each_head(c[4], R, lambda h: Ml[k % 2][:, h, :], lambda h: Ml[k % 2][:, h, :], "cprod_ps")

            run(pe, iteration)

        @block.scalar
        def _(act):
            do_act = nc.scalar.activation
            st = Steps(own_steps["act"], act)
            act.wait_ge(loads, n_loads * 16)
            act.wait_ge(setup, n_setup - 1)
            do_act(ealog[:, :], ealog[:, :], ACT.Exp).then_inc(setup, 1)
            def copy_group(tile, g):
                at = 512 * g
                n = GROUPS[g][1]
                need(act, "pj_ps", tile, g + 1)
                done(do_act(pt[0:tile.rows, at:at + n], pj[g % 2][0:tile.rows, 0:n], ACT.Copy), "pt_ready")

            def normalise(tile):
                r = tile.rows
                need(act, "x_in", tile)
                free(act, "ht_ps", tile)
                done(do_act(xn[0:r, :], xin[0:r, :], ACT.Square, accum_out=rstd[0:r, 0:1]), "sq_ready")
                need(act, "sq_ready", tile)
                done(do_act(rstd[0:r, 1:2], rstd[0:r, 0:1], ACT.Ln, scale=1.0 / DM, bias=eps[0:r, :]),
                     "lnx_ready")
                need(act, "lnx_ready", tile)
                done(do_act(rstd[0:r, 0:1], rstd[0:r, 1:2], ACT.Exp, scale=-0.5), "rstd_ready")

            def iteration(pr, ch, nm):
                part = [0]

                def fill():
                    if pr and part[0] < 6:
                        if part[0] == 0:
                            if ch:
                                need(act, "fwd_ps", ch)
                                need(act, "sg_ready", ch)
                                need(act, "zf_ready", ch)
                            elif pr.t == 1:
                                act.wait_ge(spill, 16)
                        copy_group(pr, part[0])
                        part[0] += 1

                if ch:
                    st.begin(ch)
                    mix(ch, fill, nm)
                    st.end()
                elif nm and not pr:
                    normalise(nm)
                while pr and part[0] < 6:
                    fill()
                if pr and nm and not ch:
                    normalise(nm)

            def mix(ch, fill, nm):
                if prompt:
                    need(act, "pt_ready", ch)
                free(act, "xdp_ready", ch)
                done(do_act(xd[0:R, :], pt[0:R, Q_DX:Q_DX + BW], ACT.Copy), "xd_ready")
                free(act, "dSC_ps", ch)
                done(do_act(vC[:, :, :], pt[0:R, Q_CI:Q_CI + BW].rearrange("p (h d) -> p h d", h=H),
                            ACT.Copy), "vC_ready")
                need(act, "fwd_ps", ch)
                free(act, "halo_ready", ch)
                for b, k0, nk in ((c[0], 0, 4), (c[1], 4, 2)):
                    for k in range(nk):
                        ins = do_act(xc[:, k0 + k, :, CONV - 1:],
                                     b[:, k * R:(k + 1) * R].rearrange("p (b t) -> p b t", b=SEGS), ACT.Copy)
                        if k0 + k < 5:
                            st.do(ins)
                        else:
                            done(ins, "xc_ready")
                need(act, "zf_ready", ch)
                st.do(do_act(lab[:, :], zf[:, :], ACT.Abs))
                st.sync()
                st.do(do_act(lab[:, :], lab[:, :], ACT.Exp, scale=-1.0))
                st.sync()
                done(do_act(lab[:, :], lab[:, :], ACT.Ln, bias=one[0:R, :]), "lab_ready")
                free(act, "y_ready", ch)
                st.do(do_act(sig[:, 0:2, :], pt[0:R, Q_GB:Q_GB + 2 * BW]
                             .rearrange("p (a n) -> p a n", a=2), ACT.Tanh, scale=0.5))
                st.do(do_act(sig[:, 2, :], pt[0:R, Q_CG:Q_CG + BW], ACT.Tanh, scale=0.5))
                st.do(do_act(sig[:, 3, :], pt[0:R, Q_DG:Q_DG + BW], ACT.Tanh, scale=0.5))
                done(do_act(bet[:, :], pt[0:R, Q_BETA:Q_BETA + H], ACT.Tanh, scale=0.5), "th_ready")
                need(act, "pool_ps", ch)
                done(do_act(pT[:, :, :], hv(c[2], D), ACT.Copy), "pT_ready")
                need(act, "G_ps", ch)
                done(do_act(G[:, :, :], hv(c[5], D), ACT.Copy), "G_ready")
                need(act, "gcol_ps", ch)
                done(do_act(gcol[:, :, :], c[4][0:R, 0:2 * H].rearrange("p (a h) -> p a h", a=2), ACT.Copy),
                     "gcol_tm")
                need(act, "cv_ready", ch)
                done(do_act(sig_c, cvs, ACT.Tanh, scale=0.5), "sigc_ready")
                nc.scalar.preload_act_table_set("natural_log_exp_and_others")
                need(act, "lk_ready", ch)
                done(do_act(zf[:, 0:BW], zf[:, 0:BW], ACT.Exp), "kC_ready")
                need(act, "EL_in", ch)
                st.do(do_act(eglC[:, :, :], fm(G[:, :, :])[:, :, :, SEG - 1] if not prompt
                             else G[:, :, SEG - 1:SEG], ACT.Exp))
                need(act, "back_ps", ch)
                st.do(do_act(qk[:, :, :], c[0][0:R, :].rearrange("p (h d) -> p h d", h=8), ACT.Copy,
                             scale=0.5))
                free(act, "scaled_ready", ch)
                st.sync()
                done(do_act(vB[:, :, :], c[1][0:R, 0:BW].rearrange("p (h d) -> p h d", h=H), ACT.Copy,
                            scale=0.5), "qkv_tm")
                need(act, "gcol_ready", ch)
                need(act, "R_read", ch)
                done(do_act(gcol[:, :, :], gcol[:, :, :], ACT.Exp), "ecol_ready")
                need(act, "cd_ready", ch, 1)
                done(do_act(Ml[0][:, :, :], Ml[0][:, :, :], ACT.Exp), "ce_ready")
                need(act, "cd_ready", ch, 2)
                done(do_act(Ml[1][:, :, :], Ml[1][:, :, :], ACT.Exp), "ce_ready")
                need(act, "ss_ready", ch)
                st.do(do_act(ss8[:, :], ss8[:, :], ACT.Ln, bias=eps[0:R, :]))
                st.sync()
                done(do_act(ss8[:, :], ss8[:, :], ACT.Exp, scale=-0.5), "rn_ready")
                need(act, "dec_in", ch)
                st.do(do_act(eglB[:, :, :], eglB[:, :, :], ACT.Exp))
                done(do_act(dec[:, :, :], dec[:, :, :], ACT.Exp), "dec_ready")
                fill()
                need(act, "knT_ps", ch)
                done(do_act(knT[:, :, :], hv(c[0], D), ACT.Copy), "knT_ready")
                need(act, "kbT_ps", ch)
                done(do_act(kbT[:, :, :], hv(c[1], D), ACT.Copy), "kbT_ready")
                need(act, "qgT_ps", ch)
                if prompt:
                    done(do_act(own_columns(qgx), hv(c[5], D), ACT.Copy), "qgx_ready")
                else:
                    for h in range(H):
                        ins = do_act(own_columns(qgx)[:, h], c[5][0:D, h * R:(h + 1) * R]
                                     .rearrange("d (b t) -> d b t", b=SEGS), ACT.Copy)
                        if h < H - 1:
                            st.do(ins)
                        else:
                            done(ins, "qgx_ready")
                st.do(do_act(EG[:, :, :], G[:, :, :], ACT.Exp))
                done(do_act(kgT[:, :, :], kgT[:, :, :], ACT.Exp), "EL_ready")
                for k in range(NL):
                    if k:
                        need(act, "z_ps", ch, k + 1)
                        done(do_act(Z[:, :, :], hv(c[0]), ACT.Copy), "z_ready")
                    if k + 2 < NL:
                        need(act, "cd_ready", ch, k + 3)
                        m = Ml[k % 2]
                        done(do_act(m[:, :, :], m[:, :, :], ACT.Exp), "ce_ready")
                    if k in ACT_FILLS:
                        fill()
                    if k == 3 and nm:
                        normalise(nm)
                need(act, "wT_ps", ch)
                for h in range(H):
                    out = own_columns(wTx)[:, h]
                    src = c[0][0:D, h * R:(h + 1) * R]
                    ins = do_act(out, src if prompt else src.rearrange("d (b t) -> d b t", b=SEGS), ACT.Copy,
                                 scale=-1.0)
                    if h < H - 1:
                        st.do(ins)
                    else:
                        done(ins, "wT_ready")
                need(act, "kg_ps", ch)
                done(do_act(kg[:, :, :], hv(c[4], R, D), ACT.Copy), "kg_ready")
                need(act, "vn_ps", ch)
                done(do_act(vn[:, :, :], hv(c[1], R, D), ACT.Copy), "vn_ready")
                fill()
                need(act, "oB_ps", ch)
                done(do_act(oBC[:, 0:4, :], hv(c[2], R, D), ACT.Copy), "oB_tm")
                need(act, "oC_ps", ch)
                done(do_act(oBC[:, 4:8, :], hv(c[5], R, D), ACT.Copy), "oC_tm")
                need(act, "ss2_ready", ch)
                st.do(do_act(ss8[:, :], ss8[:, :], ACT.Ln, scale=1.0 / D, bias=eps[0:R, :]))
                st.sync()
                done(do_act(ss8[:, :], ss8[:, :], ACT.Exp, scale=-0.5), "rn2_ready")

            run(act, iteration)

        @block.vector
        def _(dve):
            V = nc.vector
            tt, ts, stt = V.tensor_tensor, V.tensor_scalar, V.scalar_tensor_tensor
            M, A, SUB = ALU.mult, ALU.add, ALU.subtract
            st = Steps(own_steps["dve"], dve)
            V.memset(one[:, :], 1.0).then_inc(setup, 1)
            V.memset(eps[:, :], EPS).then_inc(setup, 1)
            if prompt:
                V.memset(SB[:, :, :, :], 0.0).then_inc(setup, 1)
                V.memset(SC[:, :, :, :], 0.0).then_inc(setup, 1)
                V.memset(xc[:, :, :, 0:CONV - 1], 0.0).then_inc(setup, 1)
                V.memset(xdp[:, :], 0.0).then_inc(setup, 1)
            else:
                V.memset(wTx[:, :], 0.0).then_inc(setup, 1)
                V.memset(qgx[:, :], 0.0).then_inc(setup, 1)
            dve.wait_ge(loads, n_loads * 16)
            V.tensor_scalar(pscale[:, :], pscale[:, :], 0.5, None, M).then_inc(setup, 1)
            halves_of = gatew[:, :].rearrange("p (n a d) -> p n a d", n=2, a=H)[:, :, 0, :]
            V.tensor_scalar(halves_of, halves_of, 0.5, None, M).then_inc(halved, 1)
            dve.wait_ge(halved, 1)
            for n in range(2):
                src = gatew[:, n * BW:n * BW + D].rearrange("p (a d) -> p a d", a=1)
                V.tensor_copy(gatew[:, n * BW + D:(n + 1) * BW].rearrange("p (a d) -> p a d", a=3),
                              src.broadcast_to([P, 3, D])).then_inc(setup, 1)
            if not prompt:
                dve.wait_ge(setup, 8)
                V.tensor_copy(xc[:, :, :, 0:CONV - 1], c[5][:, 0:144]
                              .rearrange("p (k b t) -> p k b t", k=6, b=SEGS)).then_inc(setup, 1)
            dve.wait_ge(setup, n_setup)

            def xn_rows(tile):
                r = tile.rows
                need(dve, "rstd_ready", tile)
                done(ts(xn[0:r, :], xin[0:r, :], rstd[0:r, 0:1], None, M), "xn_ready")

            def hT_rows(tile):
                r = tile.rows
                for half in range(2):
                    need(dve, "ht_ps", tile, half + 1)
                    ks = slice(4 * half, 4 * half + 4)
                    done(tt(hT[:, ks, 0:r], pj[half][:, 0:4 * r].rearrange("p (k t) -> p k t", k=4),
                            normw[:, ks].unsqueeze(2).broadcast_to([P, 4, r]), M), "hT_ready")

            def iteration(pr, ch, nm):
                if ch:
                    st.begin(ch)
                    mix(ch, nm)
                    st.end()
                elif nm:
                    xn_rows(nm)
                if nm:
                    hT_rows(nm)

            def over(ap, shape):
                return ap.unsqueeze(len(ap.shape)).broadcast_to(shape)

            def per_head(ap):
                return ap.unsqueeze(1).broadcast_to([R, H, R])

            def decay_rows(ch, k):
                need(dve, "ce_ready", ch, k + 1)
                need(dve, "kcT_ready", ch)
                need(dve, "qcT_ready", ch)
                m = halves(Ml[k % 2], k)
                st.do(tt(m[:, :, 0, :], m[:, :, 0, :], halves(kcT, k)[:, :, 0, :], M))
                done(tt(m[:, :, 1, :], m[:, :, 1, :], halves(qcT, k)[:, :, 1, :], M), "cl_ready")

            def mix(ch, nm):
                if prompt:
                    need(dve, "pt_ready", ch)
                free(dve, "kcT_ps", ch)
                free(dve, "lk_ready", ch)
                st.do(V.tensor_copy(zf[:, 0:BW], pt[0:R, Q_CF:Q_CF + BW]))
                done(stt(zf[:, BW:], pt[0:R, Q_A:Q_A + H], -1.0, dtb[0:R, :], M, SUB), "zf_ready")
                need(dve, "lab_ready", ch)
                done(stt(ls[:, :], zf[:, :], 0.0, lab[:, :], ALU.min, SUB), "ls_ready")
                need(dve, "ls_ready", ch)
                done(tt(ls[:, BW:], ls[:, BW:], ealog[0:R, :], M), "g_ready")
                done(tt(zf[:, 0:BW], ls[:, 0:BW], zf[:, 0:BW], SUB), "lk_ready")
                need(dve, "g_ready", ch)
                done(V.tensor_copy(gb[:, :, :], over(ls[:, BW:], [R, H, R])), "gb_ready")
                need(dve, "xc_ready", ch)
                free(dve, "vn_ps", ch)
                for tap in range(CONV):
                    for k in range(6):
                        src = xc[:, k, :, tap:tap + SEG]
                        out = cvs[:, k, :].rearrange("p (b t) -> p b t", b=SEGS)
                        if tap == 0:
                            ins = ts(out, src, convw[:, k, 0:1], None, M)
                        else:
                            ins = stt(out, src, convw[:, k, tap:tap + 1], out, M, A)
                        if tap < CONV - 1 or k < 5:
                            st.do(ins)
                        else:
                            done(ins, "cv_ready")
                    if tap < CONV - 1:
                        st.sync()
                if prompt:
                    done(V.tensor_copy(xc[:, :, 0, 0:CONV - 1], xc[:, :, 0, SEG:SEG + CONV - 1]), "halo_ready")
                need(dve, "th_ready", ch)
                st.do(stt(sig[:, 0:2, :], sig[:, 0:2, :], 1.0,
                          pt[0:R, Q_GB:Q_GB + 2 * BW].rearrange("p (a n) -> p a n", a=2), A, M))
                st.do(stt(sig[:, 2, :], sig[:, 2, :], 1.0, pt[0:R, Q_CG:Q_CG + BW], A, M))
                st.do(ts(bet[:, :], bet[:, :], 1.0, 0.5, A, M))
                done(stt(sig[:, 3, :], sig[:, 3, :], 1.0, pt[0:R, Q_DG:Q_DG + BW], A, M), "sg_ready")
                need(dve, "sigc_ready", ch)
                done(stt(cvs, sig_c, 1.0, cvs, A, M), "cvs_ready")
                need(dve, "gcol_tm", ch)
                done(tt(gcol[:, 1, :], gcol[:, 1, :], gcol[:, 0, :], SUB), "gcol_ready")
                need(dve, "R_ps", ch)
                st.do(V.tensor_copy(eglB[:, :, :], hv(c[3], D).rearrange("d h (b t) -> d h b t", b=SEGS)
                                    [:, :, :, SEG - 1]))
                done(tt(dec[:, :, :], hv(c[3]), over(gcol[:, 0, :], [R, H, R]), SUB), "R_read")
                need(dve, "R_read", ch)
                done(tt(dec[:, :, :], dec[:, :, :], per_head(neg), A), "dec_in")
                need(dve, "qkv_tm", ch)
                st.do(tt(sq[:, :, :], qk[:, :, :], qk[:, :, :], M))
                st.sync()
                done(V.tensor_reduce(ss8[:, :], sq[:, :, :], AX_X, A), "ss_ready")
                need(dve, "qcT_ps", ch)
                done(ts(qcT[:, :, :], hv(c[3], D), 0.5, None, M), "qcT_ready")
                need(dve, "kcT_ps", ch)
                done(V.tensor_copy(kcT[:, :, :], hv(c[4], D)), "kcT_ready")
                need(dve, "rn_ready", ch)
                st.do(ts(ss8[:, 0:4], ss8[:, 0:4], D ** -0.5, None, M))
                st.sync()
                done(tt(qk[:, :, :], qk[:, :, :], over(ss8[:, :], [R, 8, D]), M), "qk_normed")
                need(dve, "qk_normed", ch)
                done(tt(kb[:, :, :], qk[:, 4:8, :], over(bet[:, :], [R, H, D]), M), "kb_ready")
                need(dve, "ecol_ready", ch)
                done(tt(qg[:, :, :], qk[:, 0:4, :], over(gcol[:, 0, :], [R, H, D]), M), "qg_ready")
                need(dve, "poolw_ps", ch)
                free(dve, "y_out", ch)
                need(dve, "pscaled_ready", ch)
                done(tt(y[:, 2 * BW:], c[2][0:R, 0:BW], sig[:, 3, :], M), "yD_ready")
                need(dve, "cprod_ps", ch, 1)
                free(dve, "oC_ps", ch)
                done(tt(acc[:, :, :], hv(c[4]), per_head(ident[0:R, 0:R]), M), "cacc_ready")
                decay_rows(ch, 0)
                need(dve, "qnT_ps", ch)
                done(V.tensor_copy(qnT[:, :, :], hv(c[2], D)), "qnT_ready")
                need(dve, "kk_ps", ch)
                need(dve, "dec_ready", ch)
                done(tt(At[:, :, :], hv(c[0]), dec[:, :, :], M), "At_ready")
                need(dve, "kq_ps", ch)
                done(tt(QKt[:, :, :], hv(c[1]), dec[:, :, :], M), "QKt_ready")
                for k in range(NL):
                    need(dve, "cprod_ps", ch, k + 2)
                    if k:
                        need(dve, "cacc_ready", ch, k + 1)
                    done(tt(tmp[:, :, :], hv(c[4]), per_head(level[k]), M), "tmp_ready")
                    if k + 1 < NL:
                        decay_rows(ch, k + 1)
                    if k == 0:
                        need(dve, "am_ready", ch, 1)
                        done(tt(Y[:, :, :], per_head(ident[0:R, 0:R]), Am[0][:, :, :], SUB), "Y_ready")
                        need(dve, "z_ps", ch, 1)
                        done(tt(X[:, :, :], per_head(ident[0:R, 0:R]), hv(c[0]), SUB), "X_ready")
                    else:
                        if k < NL - 1:
                            need(dve, "xz_ps", ch, k)
                            need(dve, "X_ready", ch, k)
                            done(tt(X[:, :, :], X[:, :, :], hv(c[1]), SUB), "X_ready")
                        need(dve, "zy_ps", ch, k)
                        need(dve, "Y_ready", ch, k)
                        done(tt(Y[:, :, :], Y[:, :, :], hv(c[2]), SUB), "Y_ready")
                    if k == 3 and nm:
                        xn_rows(nm)
                need(dve, "EL_ready", ch)
                done(tt(kgT[:, :, :], kgT[:, :, :], kcT[:, :, :], M), "kgT_ready")
                if not prompt:
                    for b in range(SEGS):
                        ins = ts(vCx[:, :, b, :], vC[:, :, :], segm[:, b:b + 1], None, M)
                        if b < SEGS - 1:
                            st.do(ins)
                        else:
                            done(ins, "vCx_ready")
                need(dve, "vn_ps", ch)
                for h in range(H if not prompt else 1):
                    out, e, q = (own_columns(qcgx), EG, qcT) if prompt else \
                        (own_columns(qcgx)[:, h], fm(EG[:, :, :])[:, h], fm(qcT[:, :, :])[:, h])
                    ins = tt(out, e[:, :, :], q[:, :, :], M)
                    if prompt or h == H - 1:
                        done(ins, "qcg_ready")
                    else:
                        st.do(ins)
                if not prompt:
                    need(dve, "vn_ready", ch)
                    for b in range(SEGS):
                        ins = ts(vBx[:, :, b, :], vn[:, :, :], segm[:, b:b + 1], None, M)
                        if b < SEGS - 1:
                            st.do(ins)
                        else:
                            done(ins, "vBx_ready")
                for state, egl, read, inc, banks, name in (
                        (SB, eglB, "oB_ps", "dSB_ps", (3, 4, 0, 1), "SB_ready"),
                        (SC, eglC, "oC_ps", "dSC_ps", (0, 1, 3, 4), "SC_ready")):
                    need(dve, read, ch)
                    flat = state[:, :, :, :].rearrange("k h b v -> k (h b) v")
                    st.do(tt(flat, flat, over(egl[:, :, :].rearrange("k h b -> k (h b)"),
                                              [D, H * SEGS, D]), M))
                    st.sync()
                    need(dve, inc, ch)
                    if prompt:
                        done(tt(flat, flat, hv(c[banks[0]], D, D), A), name)
                    else:
                        for h in range(H):
                            ins = tt(state[:, h, :, :], state[:, h, :, :],
                                     c[banks[h]][0:D, :].rearrange("k (b v) -> k b v", b=SEGS), A)
                            if h < H - 1:
                                st.do(ins)
                            else:
                                done(ins, name)
                need(dve, "oB_tm", ch)
                need(dve, "oC_tm", ch)
                st.do(tt(sq[:, :, :], oBC[:, :, :], oBC[:, :, :], M))
                st.sync()
                done(V.tensor_reduce(ss8[:, :], sq[:, :, :], AX_X, A), "ss2_ready")
                need(dve, "rn2_ready", ch)
                st.do(tt(oBC[:, :, :], oBC[:, :, :], over(ss8[:, :], [R, 8, D]), M))
                st.sync()
                need(dve, "gates_ready", ch)
                st.do(tt(y[:, 0:BW], oBC[:, 0:4, :].rearrange("p h d -> p (h d)"), sig[:, 0, :], M))
                done(tt(y[:, BW:2 * BW], oBC[:, 4:8, :].rearrange("p h d -> p (h d)"), sig[:, 2, :], M),
                     "y_ready")

            run(dve, iteration)

        @block.gpsimd
        def _(pool):
            V = nc.gpsimd
            tt = V.tensor_tensor
            M, ADD, SUB = ALU.mult, ALU.add, ALU.subtract
            st = Steps(own_steps["pool"], pool)
            pool.wait_ge(setup, n_setup)

            def iteration(pr, ch, nm):
                if ch:
                    st.begin(ch)
                    mix(ch)
                    st.end()

            def over(ap, shape):
                return ap.unsqueeze(len(ap.shape)).broadcast_to(shape)

            def coupling(ch, k):
                if k >= 2:
                    need(pool, "z_ps", ch, k - 1)
                    need(pool, "Y_ready", ch, 1)
                done(tt(Am[k % 2][:, :, :], At[:, :, :],
                        level[k].unsqueeze(1).broadcast_to([R, H, R]), M), "am_ready")

            def mix(ch):
                need(pool, "sg_ready", ch)
                done(tt(sig[:, 3, :], sig[:, 3, :], pscale[0:R, :], M), "pscaled_ready")
                st.do(tt(sig[:, 0, :], sig[:, 0, :], gatew[0:R, 0:BW], M))
                done(tt(sig[:, 2, :], sig[:, 2, :], gatew[0:R, BW:], M), "gates_ready")
                if prompt:
                    pool.wait_ge(setup, n_setup)
                    need(pool, "pool_ps", ch)
                    done(V.tensor_copy(xdp[:, :], xd[:, :]), "xdp_ready")
                need(pool, "G_ready", ch)
                free(pool, "kg_ps", ch)
                g4 = G[:, :, :].rearrange("d h (b t) -> d (h b) t", b=SEGS)
                done(tt(kgT[:, :, :].rearrange("d h (b t) -> d (h b) t", b=SEGS),
                        g4[:, :, SEG - 1:SEG].broadcast_to([D, H * SEGS, SEG]), g4, SUB), "EL_in")

                def differences(k):
                    if k >= 2:
                        need(pool, "cprod_ps", ch, k)
                    g, m = halves(G, k), halves(Ml[k % 2], k)
                    n, s = H * R // 2 ** (k + 1), 2 ** k
                    edge = g[:, :, 0, s - 1:s].broadcast_to([D, n, s])
                    st.do(tt(m[:, :, 0, :], edge, g[:, :, 0, :], SUB))
                    done(tt(m[:, :, 1, :], g[:, :, 1, :], edge, SUB), "cd_ready")

                free(pool, "cprod_ps", ch)
                differences(0)
                differences(1)
                need(pool, "qkv_tm", ch)
                need(pool, "th_ready", ch)
                need(pool, "sg_ready", ch)
                free(pool, "dSB_ps", ch)
                st.do(tt(vb[:, :, :], vB[:, :, :], over(bet[:, :], [R, H, D]), M))
                need(pool, "ecol_ready", ch)
                need(pool, "kb_ready", ch)
                st.do(tt(kend[:, :, :], qk[:, 4:8, :], over(gcol[:, 1, :], [R, H, D]), M))
                done(tt(kbg[:, :, :], kb[:, :, :], over(gcol[:, 0, :], [R, H, D]), M), "scaled_ready")
                need(pool, "At_ready", ch)
                coupling(ch, 0)
                coupling(ch, 1)
                for k in range(NL):
                    if k + 2 < NL:
                        coupling(ch, k + 2)
                        differences(k + 2)
                    need(pool, "tmp_ready", ch, k + 1)
                    need(pool, "cacc_ready", ch, k + 1)
                    done(tt(acc[:, :, :], acc[:, :, :], tmp[:, :, :], ADD), "cacc_ready")
                need(pool, "y_ready", ch)
                pool.dma_start(rows_of(ch, io["y_rows"]), y[:, :]).then_inc(S["y_out"].sem, 16)

            run(pool, iteration)

        program.close()
        nc.clear_and_free_semaphores(sems)
        nc.all_engine_barrier()


def project_attention(nc, io):
    with ExitStack() as ctx:
        sems = []

        def sb(name, shape):
            return ctx.enter_context(nc.sbuf_tensor(f"a_{name}", shape, F32))

        def semaphore(name):
            sems.append(ctx.enter_context(nc.semaphore(f"a_{name}")))
            return sems[-1]

        w = sb("w", [P, KD, AW])
        ident, normw, eps = sb("ident", [P, P]), sb("normw", [P, KD]), sb("eps", [P, 1])
        xin, xn, hT = sb("xin", [P, DM]), sb("xn", [P, DM]), sb("hT", [P, KD, P])
        rstd = sb("rstd", [P, 2])
        rows = sb("rows", [P, AW])
        nt, pj = ([ctx.enter_context(nc.psum_tensor(f"a_{n}{k}", [P, 512], F32)) for k in range(2)]
                  for n in ("nt", "pj"))
        S = {n: Count(semaphore(n), per) for n, per in (
            ("x_in", 16), ("sq_ready", 1), ("ln_ready", 1), ("rstd_ready", 1), ("xn_ready", 1),
            ("ht_ps", 2), ("hT_ready", 2), ("pj_ps", 2), ("rows_ready", 2), ("rows_out0", 16),
            ("rows_out1", 16))}
        loads, setup = semaphore("loads"), semaphore("setup")

        def need(eng, name, tile, k=None):
            S[name].wait(eng, tile, k)

        def free(eng, name, tile):
            S[name].wait(eng, tile, 0)

        def done(ins, name):
            ins.then_inc(S[name].sem, 1)

        def run(eng, iteration):
            own, tile = Tile(TS, 0, 0), lambda n: Tile(P, n + 1, n * P)
            iteration(None, own)
            iteration(own, tile(0))
            with eng.Fori(0, NT - 1) as i:
                iteration(tile(i), tile(i + 1))
            iteration(tile(NT - 1), None)

        program = ExitStack()
        block = program.enter_context(nc.Block())

        @block.sync
        def _(sp):
            win = io["w_in"][0].rearrange("(k p) n -> p k n", p=P)
            sp.dma_start(w[:, :, :], win[:, :, 0:AW]).then_inc(loads, 16)
            sp.dma_start(ident[:, :], io["consts"][:, io["cols"]["ident"]:io["cols"]["ident"] + P])\
                .then_inc(loads, 16)
            sp.dma_start(normw[:, :], io["norm_w_fm"]).then_inc(loads, 16)

            def iteration(pr, nm):
                if nm:
                    free(sp, "xn_ready", nm)
                    sp.dma_start(xin[0:nm.rows, :], rows_of(nm, io["x_s" if nm.sample else "x_p"]))\
                        .then_inc(S["x_in"].sem, 16)
                if pr:
                    out = io["att_s"] if pr.sample else rows_of(pr, io["att_rows"])
                    for g in range(2):
                        need(sp, "rows_ready", pr, g + 1)
                        cols = slice(512 * g, 512 * g + 512)
                        sp.dma_start(out[:, cols], rows[0:pr.rows, cols])\
                            .then_inc(S[f"rows_out{g}"].sem, 16)

            run(sp, iteration)
            need(sp, "rows_out0", Tile(P, NT))
            need(sp, "rows_out1", Tile(P, NT))

        @block.tensor
        def _(pe):
            pe.wait_ge(loads, 48)

            def iteration(pr, nm):
                if pr:
                    need(pe, "hT_ready", pr)
                    for g in range(2):
                        free(pe, "rows_ready", pr)
                        for k in range(KD):
                            last = nc.tensor.matmul(pj[g][0:pr.rows, :], hT[:, k, 0:pr.rows],
                                                    w[:, k, 512 * g:512 * g + 512],
                                                    start=(k == 0), stop=(k == KD - 1))
                        done(last, "pj_ps")
                if nm:
                    need(pe, "xn_ready", nm)
                    free(pe, "hT_ready", nm)
                    for half in range(2):
                        for k in range(4):
                            last = nc.tensor.transpose(
                                nt[half][:, k * nm.rows:(k + 1) * nm.rows],
                                xn[0:nm.rows, (4 * half + k) * P:(4 * half + k + 1) * P],
                                ident[0:nm.rows, 0:nm.rows])
                        done(last, "ht_ps")

            run(pe, iteration)

        @block.scalar
        def _(act):
            act.wait_ge(setup, 1)

            def iteration(pr, nm):
                if nm:
                    r = nm.rows
                    need(act, "x_in", nm)
                    free(act, "ht_ps", nm)
                    done(nc.scalar.activation(xn[0:r, :], xin[0:r, :], ACT.Square,
                                              accum_out=rstd[0:r, 0:1]), "sq_ready")
                    nc.scalar.preload_act_table_set("natural_log_exp_and_others")
                    need(act, "sq_ready", nm)
                    done(nc.scalar.activation(rstd[0:r, 1:2], rstd[0:r, 0:1], ACT.Ln, scale=1.0 / DM,
                                              bias=eps[0:r, :]), "ln_ready")
                    need(act, "ln_ready", nm)
                    done(nc.scalar.activation(rstd[0:r, 0:1], rstd[0:r, 1:2], ACT.Exp, scale=-0.5),
                         "rstd_ready")
                if pr:
                    for g in range(2):
                        free(act, f"rows_out{g}", pr)
                        need(act, "pj_ps", pr, g + 1)
                        cols = slice(512 * g, 512 * g + 512)
                        done(nc.scalar.activation(rows[0:pr.rows, cols], pj[g][0:pr.rows, :], ACT.Copy),
                             "rows_ready")

            run(act, iteration)

        @block.vector
        def _(dve):
            nc.vector.memset(eps[:, :], EPS).then_inc(setup, 1)
            dve.wait_ge(loads, 48)

            def iteration(pr, nm):
                if nm:
                    r = nm.rows
                    need(dve, "rstd_ready", nm)
                    done(nc.vector.tensor_scalar(xn[0:r, :], xin[0:r, :], rstd[0:r, 0:1], None, ALU.mult),
                         "xn_ready")
                    for half in range(2):
                        need(dve, "ht_ps", nm, half + 1)
                        ks = slice(4 * half, 4 * half + 4)
                        done(nc.vector.tensor_tensor(
                            hT[:, ks, 0:r], nt[half][:, 0:4 * r].rearrange("p (k t) -> p k t", k=4),
                            normw[:, ks].unsqueeze(2).broadcast_to([P, 4, r]), ALU.mult), "hT_ready")

            run(dve, iteration)

        program.close()
        nc.clear_and_free_semaphores(sems)
        nc.all_engine_barrier()


PATTERNS = ((128, 1), (512, 4), (2048, 16))
DILATIONS = (16, 4, 1)
SLOPES = [2.0 ** (-8.0 * (h + 1) / H) for h in range(H)]
PART = BW + 2 * H
OCTET = 8


def alibi_constants(dil, first):
    q, k = np.arange(P)[:, None], np.arange(P)[None, :]
    out = []
    for slope in SLOPES:
        own = np.where(q >= k, -slope * dil * (q - k), NEG)
        prev = np.where((q <= k) & (not first), -slope * dil * (q + P - k), NEG)
        out.append(np.concatenate([prev, own, prev], axis=1))
    return np.concatenate(out, axis=1).astype(np.float32)


def attend_classes(nc, io):
    BLOCKS = SEQ // P
    with ExitStack() as ctx:
        sems = []

        def sb(name, shape):
            return ctx.enter_context(nc.sbuf_tensor(f"c_{name}", shape, F32))

        def semaphore(name):
            sems.append(ctx.enter_context(nc.semaphore(f"c_{name}")))
            return sems[-1]

        def bank(name):
            return ctx.enter_context(nc.psum_tensor(f"c_{name}", [P, 512], F32))

        ident = sb("ident", [P, P])
        bias = {(d, f): sb(f"bias{d}_{f}", [P, H, 3 * P]) for d in DILATIONS for f in (0, 1)}
        rows = sb("rows", [P, OCTET, 3 * BW])
        qT = sb("qT", [D, 2, H, P])
        kT = sb("kT", [D, H, 2, P])
        sc = sb("sc", [P, 4, H, 2 * P])
        mx = sb("mx", [P, 4, H])
        PT = sb("PT", [P, 2, H * 2, P])
        res = sb("res", [P, OCTET, PART])
        tq, tk, o_ps = bank("tq"), bank("tk"), bank("o")
        s_ps, pt_ps = [bank("s0"), bank("s1")], [bank("p0"), bank("p1")]

        S = {n: Count(semaphore(n), per) for n, per in (
            ("q_ps", 1), ("k_ps", 1), ("qT_ready", 1), ("kT_ready", 1), ("s_done", 1),
            ("biased", 2), ("max_ready", 1), ("neg_ready", 1), ("exp_ready", 4), ("p_ps", 2),
            ("PT_ready", 2), ("o_done", 1), ("res_ready", 1))}
        loads, kT_zero = semaphore("loads"), semaphore("kT_zero")
        passed = {nc.tensor: semaphore("pe_passed"), nc.sync: semaphore("sp_passed")}
        n_loads = 7
        rows_in = [semaphore(f"rows_in{n}") for n in range(OCTET)]
        res_out = [semaphore(f"res_out{n}") for n in range(OCTET)]

        class At:

            def __init__(self, o, n):
                self.t, self.octet, self.n = o * OCTET + n, o + n // OCTET, n % OCTET

        def need(eng, name, b, k=None):
            S[name].wait(eng, b, k)

        def ago(eng, name, b, blocks):
            per = S[name].per
            if isinstance(b.t, int) and b.t < blocks:
                return
            eng.wait_ge(S[name].sem, b.t * per + per * (1 - blocks))

        def stored(eng, b):
            if isinstance(b.t, int) and b.t < OCTET:
                return
            eng.wait_ge(res_out[b.n], b.octet * 16)

        def apart(eng):
            eng.sem_inc(passed[eng], 1)

        def done(ins, name):
            ins.then_inc(S[name].sem, 1)

        def run(eng, step, by_dilation=False, lag=0):

            def octet(o, d, peeled=None):
                for n in range(OCTET):
                    first = (n % 2 == 0) if d == 16 else (n == 0 if d == 4 else peeled == 8 and n == 0)
                    step(o, n, d, first)
            octet(0, 16, 0)
            if by_dilation:
                with eng.Fori(1, 4) as o:
                    octet(o, 16)
                with eng.Fori(4, 8) as o:
                    octet(o, 4)
                octet(8, 1, 8)
                with eng.Fori(9, 11) as o:
                    octet(o, 1)
                octet(11, 1, 11)
            else:
                with eng.Fori(1, 12) as o:
                    octet(o, None)
            for n in range(lag):
                step(NOCT, n, None, False)

        NOCT = 3 * BLOCKS // OCTET

        def live(o, n, k=0):
            return not isinstance(o, int) or 0 <= o * OCTET + n - k < 3 * BLOCKS

        def row(d, o, n):
            if d == 16:
                return o * 4 + (n // 2 + (n % 2) * P * 16)
            if d == 4:
                return (o - 4) + n * P * 4
            return (o - 8) * (OCTET * P) + n * P

        def dram_rows(dram, d, o, n):
            r = row(d, o, n)
            if isinstance(r, int):
                return dram[r:r + (P - 1) * d + 1:d, :]
            return dram[bass.ds(r, P, step=d), :]

        program = ExitStack()
        block = program.enter_context(nc.Block())

        @block.sync
        def _(sp):
            sp.dma_start(ident[:, :], io["consts"][:, io["cols"]["ident"]:io["cols"]["ident"] + P])\
                .then_inc(loads, 16)
            for (d, f), buf in sorted(bias.items()):
                at = io["cols"][f"alibi_{d}_{f}"]
                sp.dma_start(buf[:, :, :].rearrange("p h k -> p (h k)"),
                             io["consts"][:, at:at + H * 3 * P]).then_inc(loads, 16)

            sp.wait_ge(kT_zero, 2)

            def step(o, n, d, first):
                b = At(o, n)
                ago(sp, "o_done", b, OCTET - 1)
                apart(sp)
                sp.dma_start(rows[:, n, :], dram_rows(io["att_rows"][:, 0:3 * BW], d, o, n))\
                    .then_inc(rows_in[n], 16)

            run(sp, step, by_dilation=True)

        @block.tensor
        def _(pe):
            pe.wait_ge(loads, 16 * n_loads)

            def step(o, n, d, first):
                if live(o, n):
                    b = At(o, n)
                    pe.wait_ge(rows_in[b.n], b.octet * 16 + 16)
                    ago(pe, "qT_ready", b, 1)
                    apart(pe)
                    for h in range(H):
                        last = nc.tensor.transpose(tq[0:D, h * P:(h + 1) * P],
                                                   rows[:, b.n, h * D:(h + 1) * D], ident[:, :])
                    done(last, "q_ps")
                    ago(pe, "kT_ready", b, 1)
                    apart(pe)
                    for h in range(H):
                        last = nc.tensor.transpose(tk[0:D, h * P:(h + 1) * P],
                                                   rows[:, b.n, BW + h * D:BW + (h + 1) * D], ident[:, :])
                    done(last, "k_ps")
                if live(o, n, 3):
                    b = At(o, n - 3)
                    for half in range(2):
                        need(pe, "exp_ready", b)
                        ago(pe, "PT_ready", b, 1)
                        apart(pe)
                        for k in range(4):
                            h, s = 2 * half + k // 2, k % 2
                            last = nc.tensor.transpose(pt_ps[half][:, k * P:(k + 1) * P],
                                                       sc[:, b.n % 4, h, s * P:(s + 1) * P], ident[:, :])
                        done(last, "p_ps")
                if live(o, n, 1):
                    b = At(o, n - 1)
                    need(pe, "kT_ready", b)
                    need(pe, "qT_ready", b)
                    ago(pe, "biased", b, 1)
                    for h in range(H):
                        last = nc.tensor.matmul(s_ps[h // 2][:, (h % 2) * 2 * P:(h % 2 + 1) * 2 * P],
                                                qT[:, b.n % 2, h, :],
                                                kT[:, h, :, :].rearrange("d s k -> d (s k)"),
                                                start=True, stop=True)
                    done(last, "s_done")
                if live(o, n, 4):
                    b = At(o, n - 4)
                    need(pe, "PT_ready", b)
                    ago(pe, "res_ready", b, 1)
                    for h in range(H):
                        for s in range(2):
                            v = rows[:, b.n if s == b.n % 2 else (b.n - 1) % OCTET,
                                     2 * BW + h * D:2 * BW + (h + 1) * D]
                            last = nc.tensor.matmul(o_ps[:, h * D:(h + 1) * D], PT[:, b.n % 2, 2 * h + s, :],
                                                    v, start=(s == 0), stop=(s == 1))
                    done(last, "o_done")

            run(pe, step, lag=4)

        @block.scalar
        def _(act):
            act.wait_ge(loads, 16)

            def step(o, n, d, first):
                if live(o, n):
                    b = At(o, n)
                    need(act, "q_ps", b)
                    ago(act, "s_done", b, 2)
                    done(nc.scalar.activation(qT[:, b.n % 2, :, :],
                                              tq[0:D, :].rearrange("d (h t) -> d h t", h=H), ACT.Copy,
                                              scale=D ** -0.5), "qT_ready")
                if live(o, n, 3):
                    b = At(o, n - 3)
                    need(act, "p_ps", b, 1)
                    ago(act, "o_done", b, 2)
                    done(nc.scalar.activation(PT[:, b.n % 2, 0:4, :],
                                              pt_ps[0][:, :].rearrange("p (k t) -> p k t", k=4), ACT.Copy),
                         "PT_ready")
                if live(o, n, 5):
                    b = At(o, n - 5)
                    need(act, "o_done", b)
                    done(nc.scalar.activation(res[:, b.n, 0:BW], o_ps[:, 0:BW], ACT.Copy), "res_ready")
                if live(o, n, 2):
                    b = At(o, n - 2)
                    need(act, "neg_ready", b)
                    stored(act, b)
                    for h in range(H):
                        done(nc.scalar.activation(sc[:, b.n % 4, h, :], sc[:, b.n % 4, h, :], ACT.Exp,
                                                  bias=mx[:, b.n % 4, h:h + 1],
                                                  accum_out=res[:, b.n, BW + h:BW + h + 1]), "exp_ready")

            run(act, step, lag=5)

        @block.vector
        def _(dve):
            nc.vector.memset(kT[:, :, :, :], 0.0).then_inc(kT_zero, 1)
            nc.vector.memset(rows[:, OCTET - 1, 2 * BW:], 0.0).then_inc(kT_zero, 1)
            dve.wait_ge(kT_zero, 2)
            dve.wait_ge(loads, 16 * n_loads)

            def biased(o, n, d, first):
                b = At(o, n)
                need(dve, "s_done", b)
                ago(dve, "p_ps", b, 4)
                stored(dve, b)
                cols = slice(P, 3 * P) if b.n % 2 == 0 else slice(0, 2 * P)
                table = bias[d, int(first)]
                for half in range(2):
                    hs = slice(2 * half, 2 * half + 2)
                    done(nc.vector.tensor_tensor(
                        sc[:, b.n % 4, hs, :], s_ps[half][:, :].rearrange("p (h k) -> p h k", h=2),
                        table[:, hs, cols], ALU.add), "biased")
                need(dve, "biased", b)
                done(nc.vector.tensor_reduce(res[:, b.n, BW + H:], sc[:, b.n % 4, :, :], AX_X, ALU.max),
                     "max_ready")
                need(dve, "max_ready", b)
                ago(dve, "exp_ready", b, 4)
                done(nc.vector.tensor_scalar(mx[:, b.n % 4, :], res[:, b.n, BW + H:], -1.0, None,
                                             ALU.mult), "neg_ready")

            def keys(o, n):
                b = At(o, n)
                need(dve, "k_ps", b)
                ago(dve, "s_done", b, 1)
                done(nc.vector.tensor_copy(kT[:, :, b.n % 2, :],
                                           tk[0:D, :].rearrange("d (h t) -> d h t", h=H)), "kT_ready")

            def probabilities(o, n):
                b = At(o, n)
                need(dve, "p_ps", b)
                ago(dve, "o_done", b, 2)
                done(nc.vector.tensor_copy(PT[:, b.n % 2, 4:8, :],
                                           pt_ps[1][:, :].rearrange("p (k t) -> p k t", k=4)), "PT_ready")

            def step(o, n, d, first):
                if live(o, n, 2):
                    probabilities(o, n - 2)
                if live(o, n + 1):
                    keys(o, n + 1)
                if live(o, n):
                    biased(o, n, d, first)

            keys(0, 0)
            run(dve, step, by_dilation=True, lag=2)

        @block.gpsimd
        def _(pool):
            def step(o, n, d, first):
                b = At(o, n)
                need(pool, "res_ready", b)
                part = DILATIONS.index(d)
                pool.dma_start(dram_rows(io["parts"][part], d, o, n), res[:, b.n, :])\
                    .then_inc(res_out[n], 16)

            run(pool, step, by_dilation=True)
            for sem in res_out:
                pool.wait_ge(sem, 16 * NOCT)

        program.close()
        nc.clear_and_free_semaphores(sems)
        nc.all_engine_barrier()


BUF = 2048
NEAR = 512
STEP, USED = 16, DS
FAR_TILES = (BUF - NEAR) // STEP * USED // P
CACHE_TILES = FAR_TILES + NEAR // P
KEYS = CACHE_TILES * P + DS
GROUP = 4


def cache_constants():
    pos = []
    for f in range(FAR_TILES):
        p = np.arange(P)
        pos.append((f * (P // USED) + p // USED) * STEP + p % USED)
    pos.append(np.arange(BUF - NEAR, BUF + DS))
    pos = np.concatenate(pos)
    rows = np.arange(P)
    head, new = (rows // DS) % H, rows % DS
    dist = BUF + new[:, None] - pos[None, :]
    times = sum(((dist >= 0) & (dist <= win) & (dist % dil == 0)).astype(np.float64)
                for win, dil in PATTERNS)
    slope = np.array(SLOPES)[head][:, None]
    bias = np.where(times > 0, -slope * dist + np.log(np.maximum(times, 1.0)), NEG)
    of_head = head[:, None] == np.arange(H)[None, :]
    return np.concatenate([bias, of_head], axis=1).astype(np.float32)


def attend_cache(nc, io):
    SPANS = ((0, 512), (512, 512), (1024, KEYS - 1024))
    NT_ALL = CACHE_TILES + 1
    with ExitStack() as ctx:
        sems = []

        def sb(name, shape):
            return ctx.enter_context(nc.sbuf_tensor(f"s_{name}", shape, F32))

        def semaphore(name):
            sems.append(ctx.enter_context(nc.semaphore(f"s_{name}")))
            return sems[-1]

        def bank(name):
            return ctx.enter_context(nc.psum_tensor(f"s_ps_{name}", [P, 512], F32))

        ident = sb("ident", [P, P])
        table = sb("table", [P, KEYS + H])
        new = sb("new", [DS, 2, DB, BW])
        q = sb("q", [TS, BW])
        k_buf = sb("k", [P, 3, CACHE_TILES, BW])
        v_buf = sb("v", [P, 5, CACHE_TILES, BW])
        qbd = sb("qbd", [P, 2, DB, H, DS])
        kT = sb("kT", [P, 2, KEYS])
        sc = sb("sc", [P, KEYS])
        mx = sb("mx", [P, 2])
        den = sb("den", [P, 2])
        PT = sb("PT", [P, NT_ALL, P])
        o = sb("o", [P, D])
        tr = [bank(f"t{n}") for n in range(4)]
        s_ps = [bank(f"s{n}") for n in range(3)]
        o_ps = bank("o")

        loads, zero = semaphore("loads"), semaphore("zero")
        k_in = [semaphore(f"k_in{n}") for n in range(3)]
        v_in = [semaphore(f"v_in{n}") for n in range(5)]
        names = """q_ps qbd_ready tr_ps tr_read s_done biased max_ready neg_ready exp_ready p_ps pt_read
            v_done den_ready o_ready o_part o_out pt_part""".split()
        S = {n: semaphore(n) for n in names}
        KSETS = 6
        PSETS = 3

        program = ExitStack()
        block = program.enter_context(nc.Block())

        @block.sync
        def _(sp):
            at = io["cols"]["cache"]
            for dst, src in ((ident[:, :], io["consts"][:, io["cols"]["ident"]:io["cols"]["ident"] + P]),
                             (q[:, :], io["att_s"][:, 0:BW]),
                             (new[:, 0], io["att_s"][:, BW:2 * BW].rearrange("(b i) n -> i b n", i=DS)),
                             (new[:, 1], io["att_s"][:, 2 * BW:3 * BW].rearrange("(b i) n -> i b n", i=DS)),
                             (table[:, :], io["consts"][:, at:at + KEYS + H])):
                sp.dma_start(dst, src).then_inc(loads, 16)

            def cache(dst, src, sem):
                old = src[0:BUF - NEAR, :].rearrange("(f m s) n -> f m s n", f=FAR_TILES, s=STEP)
                for f in range(FAR_TILES):
                    sp.dma_start(dst[:, f, :], old[f, :, 0:USED, :]).then_inc(sem, 16)
                sp.dma_start(dst[:, FAR_TILES:, :], src[BUF - NEAR:, :].rearrange("(j p) n -> p j n", p=P))\
                    .then_inc(sem, 16)

            for b in range(DB):
                if b >= 3:
                    sp.wait_ge(S["tr_ps"], (b - 2) * KSETS)
                cache(k_buf[:, b % 3], io["cache_k"][0, b].rearrange("t h d -> t (h d)"), k_in[b % 3])
                if b >= 5:
                    sp.wait_ge(S["v_done"], b - 4)
                cache(v_buf[:, b % 5], io["cache_v"][0, b].rearrange("t h d -> t (h d)"), v_in[b % 5])

        @block.tensor
        def _(pe):
            pe.wait_ge(loads, 80)
            for half in range(2):
                last = nc.tensor.transpose(o_ps[:, half * TS:(half + 1) * TS], q[:, half * P:(half + 1) * P],
                                           ident[0:TS, 0:TS])
            last.then_inc(S["q_ps"], 1)
            pe.wait_ge(S["qbd_ready"], 4)
            for b in range(DB):
                g, bb = divmod(b, GROUP)
                pe.wait_ge(k_in[b % 3], 16 * (FAR_TILES + 1) * (b // 3 + 1))
                for n in range(KSETS):
                    if b * KSETS + n >= 4:
                        pe.wait_ge(S["tr_read"], b * KSETS + n - 3)
                    half, t0 = n // 3, (n % 3) * 4
                    out = tr[(b * KSETS + n) % 4]
                    cols = slice(half * P, (half + 1) * P)
                    for t in range(t0, min(t0 + 4, NT_ALL)):
                        if t < CACHE_TILES:
                            last = nc.tensor.transpose(out[:, (t - t0) * P:(t - t0 + 1) * P],
                                                       k_buf[:, b % 3, t, cols], ident[:, :])
                        else:
                            last = nc.tensor.transpose(out[:, (t - t0) * P:(t - t0) * P + DS],
                                                       new[:, 0, b, cols], ident[0:DS, 0:DS])
                    last.then_inc(S["tr_ps"], 1)
                pe.wait_ge(S["tr_read"], (b + 1) * KSETS)
                for n, (k0, nk) in enumerate(SPANS):
                    for half in range(2):
                        last = nc.tensor.matmul(s_ps[n][32 * bb:32 * bb + 32, 0:nk],
                                                qbd[:, half, b].rearrange("p h i -> p (h i)"),
                                                kT[:, half, k0:k0 + nk], start=(half == 0), stop=(half == 1))
                last.then_inc(S["s_done"], 1)
                if bb < GROUP - 1:
                    continue
                pe.wait_ge(S["exp_ready"], g + 1)
                for n in range(PSETS):
                    set_no = DB * KSETS + g * PSETS + n
                    out = s_ps[n]
                    for t in range(4 * n, min(4 * n + 4, NT_ALL)):
                        nk = P if t < CACHE_TILES else DS
                        last = nc.tensor.transpose(out[0:nk, (t % 4) * P:(t % 4 + 1) * P],
                                                   sc[:, t * P:t * P + nk], ident[:, :])
                    last.then_inc(S["p_ps"], 1)
                pe.wait_ge(S["pt_read"], (g + 1) * PSETS)
                if g:
                    pe.wait_ge(S["o_ready"], g)
                for bb in range(GROUP):
                    bv = g * GROUP + bb
                    pe.wait_ge(v_in[bv % 5], 16 * (FAR_TILES + 1) * (bv // 5 + 1))
                    for t in range(NT_ALL):
                        nk = P if t < CACHE_TILES else DS
                        v = v_buf[:, bv % 5, t, :] if t < CACHE_TILES else new[:, 1, bv, :]
                        last = nc.tensor.matmul(o_ps[32 * bb:32 * bb + 32, 0:BW],
                                                PT[0:nk, t, 32 * bb:32 * bb + 32], v,
                                                start=(t == 0), stop=(t == NT_ALL - 1))
                    last.then_inc(S["v_done"], 1)

        def keys_to_sbuf(eng, b, n):
            half, k0 = n // 3, (n % 3) * 512
            nk = min(512, KEYS - k0)
            eng.wait_ge(S["tr_ps"], b * KSETS + n + 1)
            if b:
                eng.wait_ge(S["s_done"], b)
            if b * KSETS + n:
                eng.wait_ge(S["tr_read"], b * KSETS + n)
            out, src = kT[:, half, k0:k0 + nk], tr[(b * KSETS + n) % 4][:, 0:nk]
            ins = (nc.vector.tensor_copy(out, src) if n % 2 else nc.scalar.activation(out, src, ACT.Copy))
            ins.then_inc(S["tr_read"], 1)

        @block.scalar
        def _(act):
            for b in range(DB):
                g, bb = divmod(b, GROUP)
                for n in range(0, KSETS, 2):
                    keys_to_sbuf(act, b, n)
                if bb < GROUP - 1:
                    continue
                act.wait_ge(S["neg_ready"], g + 1)
                nc.scalar.activation(sc[:, :], sc[:, :], ACT.Exp, bias=mx[:, 1:2],
                                     accum_out=den[:, 0:1]).then_inc(S["exp_ready"], 1)

        @block.vector
        def _(dve):
            V, M = nc.vector, ALU.mult
            V.memset(qbd[:, :, :, :, :], 0.0).then_inc(zero, 1)
            dve.wait_ge(zero, 1)
            dve.wait_ge(S["q_ps"], 1)
            for half in range(2):
                for low in range(2):
                    part = slice(64 * low, 64 * low + 64)
                    V.tensor_scalar(qbd[part, half, :, 2 * half + low, :],
                                    o_ps[part, half * TS:(half + 1) * TS].rearrange("p (b i) -> p b i", i=DS),
                                    D ** -0.5, None, M).then_inc(S["qbd_ready"], 1)
            dve.wait_ge(loads, 80)
            for b in range(DB):
                g, bb = divmod(b, GROUP)
                for n in range(1, KSETS, 2):
                    keys_to_sbuf(dve, b, n)
                if bb < GROUP - 1:
                    continue
                dve.wait_ge(S["s_done"], b + 1)
                if g:
                    dve.wait_ge(S["p_ps"], g * PSETS)
                for n, (k0, nk) in enumerate(SPANS):
                    V.tensor_tensor(sc[:, k0:k0 + nk], s_ps[n][:, 0:nk], table[:, k0:k0 + nk], ALU.add)\
                        .then_inc(S["biased"], 1)
                dve.wait_ge(S["biased"], 3 * (g + 1))
                V.tensor_reduce(mx[:, 0:1], sc[:, :], AX_X, ALU.max).then_inc(S["max_ready"], 1)
                dve.wait_ge(S["max_ready"], g + 1)
                V.tensor_scalar(mx[:, 1:2], mx[:, 0:1], -1.0, None, M).then_inc(S["neg_ready"], 1)
                if g:
                    dve.wait_ge(S["v_done"], g * GROUP)
                for n in range(PSETS):
                    dve.wait_ge(S["p_ps"], g * PSETS + n + 1)
                    full = min(4, CACHE_TILES - 4 * n)
                    ins = V.tensor_copy(PT[:, 4 * n:4 * n + full, :],
                                        s_ps[n][:, 0:full * P].rearrange("p (t r) -> p t r", t=full))
                    if full < 4:
                        ins.then_inc(S["pt_part"], 1)
                        ins = V.tensor_copy(PT[0:DS, CACHE_TILES, :], s_ps[n][0:DS, full * P:(full + 1) * P])
                    ins.then_inc(S["pt_read"], 1)
                dve.wait_ge(S["exp_ready"], g + 1)
                V.reciprocal(den[:, 1:2], den[:, 0:1]).then_inc(S["den_ready"], 1)
                dve.wait_ge(S["v_done"], (g + 1) * GROUP)
                dve.wait_ge(S["den_ready"], g + 1)
                if g:
                    dve.wait_ge(S["o_out"], 16 * GROUP * g)
                of = lambda h: table[:, KEYS + h:KEYS + h + 1]
                V.tensor_scalar(o[:, :], o_ps[:, 0:D], of(0), None, M).then_inc(S["o_part"], 1)
                for h in range(1, H):
                    dve.wait_ge(S["o_part"], g * H + h)
                    V.scalar_tensor_tensor(o[:, :], o_ps[:, h * D:(h + 1) * D], of(h), o[:, :], M, ALU.add)\
                        .then_inc(S["o_part"], 1)
                dve.wait_ge(S["o_part"], g * H + H)
                V.tensor_scalar(o[:, :], o[:, :], den[:, 1:2], None, M).then_inc(S["o_ready"], 1)

        @block.gpsimd
        def _(pool):
            for g in range(DB // GROUP):
                pool.wait_ge(S["o_ready"], g + 1)
                for bb in range(GROUP):
                    b = g * GROUP + bb
                    dst = io["att_o"][b * DS:(b + 1) * DS, :].rearrange("i (h d) -> h i d", h=H)
                    pool.dma_start(dst, o[32 * bb:32 * bb + 32, :]).then_inc(S["o_out"], 16)
            pool.wait_ge(S["o_out"], 16 * DB)

        program.close()
        nc.clear_and_free_semaphores(sems)
        nc.all_engine_barrier()


def finish(nc, io):
    with ExitStack() as ctx:
        sems = []

        def sb(name, shape):
            return ctx.enter_context(nc.sbuf_tensor(f"f_{name}", shape, F32))

        def semaphore(name):
            sems.append(ctx.enter_context(nc.semaphore(f"f_{name}")))
            return sems[-1]

        wo = sb("wo", [P, KD, DM])
        ident, eps = sb("ident", [P, P]), sb("eps", [P, 1])
        finalw = sb("finalw", [P, DM])
        parts = sb("parts", [P, 3, PART])
        gate = sb("gate", [P, BW])
        sig = sb("sig", [P, BW])
        top = sb("top", [P, 2, H])
        wgt = sb("wgt", [P, 3, H])
        dens = sb("dens", [P, 3, H])
        den = sb("den", [P, 2, H])
        y = sb("y", [P, DM])
        yT = sb("yT", [P, KD, P])
        x = sb("x", [P, DM])
        z = sb("z", [P, DM])
        sq = sb("sq", [P, DM])
        rstd = sb("rstd", [P, 2])
        out = sb("out", [P, DM])
        tp, pj = ([ctx.enter_context(nc.psum_tensor(f"f_{n}{k}", [P, 512], F32)) for k in range(2)]
                  for n in ("tp", "pj"))
        S = {n: Count(semaphore(n), per) for n, per in (
            ("parts_in", 16), ("gate_in", 16), ("y_in", 16), ("x_in", 16), ("out_out", 16),
            ("top0_ready", 1), ("top_ready", 1), ("diff_ready", 1), ("wgt_ready", 1), ("den_ready", 1),
            ("sum_ready", 1), ("inv_ready", 1), ("wn_ready", 1), ("tanh_ready", 1), ("half_ready", 1),
            ("sig_ready", 1), ("scaled_ready", 1), ("pair_ready", 1), ("num_ready", 1), ("yA_ready", 1),
            ("y_ps", 2), ("yT_ready", 2), ("o_done", 2), ("z_ready", 2), ("sq_ready", 1), ("ln_ready", 1),
            ("rstd_ready", 1), ("out_ready", 1))}
        for n in ("top0_ready", "top_ready", "diff_ready", "wgt_ready", "den_ready", "sum_ready", "inv_ready",
                  "wn_ready", "scaled_ready", "pair_ready", "num_ready"):
            S[n].first = 1
        loads, setup, loads_out = semaphore("loads"), semaphore("setup"), semaphore("loads_out")

        def need(eng, name, tile, k=None):
            S[name].wait(eng, tile, k)

        def free(eng, name, tile):
            S[name].wait(eng, tile, 0)

        def done(ins, name):
            ins.then_inc(S[name].sem, 1)

        def run(eng, iteration):
            own, tile = Tile(TS, 0, 0), lambda n: Tile(P, n + 1, n * P)
            iteration(None, own)
            iteration(own, tile(0))
            with eng.Fori(0, NT - 1) as i:
                iteration(tile(i), tile(i + 1))
            iteration(tile(NT - 1), None)

        program = ExitStack()
        block = program.enter_context(nc.Block())

        @block.sync
        def _(sp):
            sp.dma_start(wo[:, :, :], io["w_out"][0].rearrange("(k p) n -> p k n", p=P)).then_inc(loads, 16)
            sp.dma_start(ident[:, :], io["consts"][:, io["cols"]["ident"]:io["cols"]["ident"] + P])\
                .then_inc(loads, 16)
            sp.dma_start(finalw[:, :], io["final_norm_w"].broadcast_to([P, DM])).then_inc(loads, 16)

            def iteration(pr, mg):
                if mg:
                    r = mg.rows
                    free(sp, "yA_ready", mg)
                    if mg.sample:
                        sp.dma_start(parts[0:r, 0, 0:BW], io["att_o"]).then_inc(S["parts_in"].sem, 16)
                    else:
                        sp.dma_start(parts[:, :, :], io["parts"][:, bass.ds(mg.row, P), :]
                                     .rearrange("k p n -> p k n")).then_inc(S["parts_in"].sem, 16)
                    src = io["att_s"] if mg.sample else rows_of(mg, io["att_rows"])
                    sp.dma_start(gate[0:r, :], src[:, 3 * BW:]).then_inc(S["gate_in"].sem, 16)
                    free(sp, "y_ps", mg)
                    src = io["y_rows"][SEQ:, :] if mg.sample else rows_of(mg, io["y_rows"])
                    sp.dma_start(y[0:r, BW:], src).then_inc(S["y_in"].sem, 16)
                if pr:
                    r = pr.rows
                    free(sp, "z_ready", pr)
                    sp.dma_start(x[0:r, :], rows_of(pr, io["x_s" if pr.sample else "x_p"]))\
                        .then_inc(S["x_in"].sem, 16)

            run(sp, iteration)

        @block.tensor
        def _(pe):
            pe.wait_ge(loads, 48)

            def iteration(pr, mg):
                if pr:
                    need(pe, "yT_ready", pr)
                    free(pe, "z_ready", pr)
                    for half in range(2):
                        for k in range(KD):
                            last = nc.tensor.matmul(pj[half][0:pr.rows, :], yT[:, k, 0:pr.rows],
                                                    wo[:, k, 512 * half:512 * half + 512],
                                                    start=(k == 0), stop=(k == KD - 1))
                        done(last, "o_done")
                if mg:
                    r = mg.rows
                    need(pe, "yA_ready", mg)
                    need(pe, "y_in", mg)
                    free(pe, "yT_ready", mg)
                    for half in range(2):
                        for k in range(4):
                            last = nc.tensor.transpose(tp[half][:, k * r:(k + 1) * r],
                                                       y[0:r, (4 * half + k) * P:(4 * half + k + 1) * P],
                                                       ident[0:r, 0:r])
                        done(last, "y_ps")

            run(pe, iteration)

        @block.scalar
        def _(act):
            do_act = nc.scalar.activation
            act.wait_ge(setup, 1)

            def iteration(pr, mg):
                if mg:
                    r = mg.rows
                    need(act, "gate_in", mg)
                    free(act, "yA_ready", mg)
                    done(do_act(sig[0:r, :], gate[0:r, :], ACT.Tanh, scale=0.5), "tanh_ready")
                    if not mg.sample:
                        need(act, "diff_ready", mg)
                        done(do_act(wgt[:, :, :], wgt[:, :, :], ACT.Exp), "wgt_ready")
                if mg:
                    for half in range(2):
                        need(act, "y_ps", mg, half + 1)
                        if half == 0 and pr:
                            need(act, "o_done", pr)
                        done(do_act(yT[:, 4 * half:4 * half + 4, 0:r],
                                    tp[half][:, 0:4 * r].rearrange("p (k t) -> p k t", k=4), ACT.Copy),
                             "yT_ready")
                if pr:
                    r = pr.rows
                    need(act, "z_ready", pr)
                    free(act, "out_ready", pr)
                    done(do_act(sq[0:r, :], z[0:r, :], ACT.Square, accum_out=rstd[0:r, 0:1]), "sq_ready")
                    nc.scalar.preload_act_table_set("natural_log_exp_and_others")
                    need(act, "sq_ready", pr)
                    done(do_act(rstd[0:r, 1:2], rstd[0:r, 0:1], ACT.Ln, scale=1.0 / DM, bias=eps[0:r, :]),
                         "ln_ready")
                    need(act, "ln_ready", pr)
                    done(do_act(rstd[0:r, 0:1], rstd[0:r, 1:2], ACT.Exp, scale=-0.5), "rstd_ready")

            run(act, iteration)

        @block.vector
        def _(dve):
            V = nc.vector
            tt, ts, stt = V.tensor_tensor, V.tensor_scalar, V.scalar_tensor_tensor
            M, A, SUB, MAX = ALU.mult, ALU.add, ALU.subtract, ALU.max
            V.memset(eps[:, :], EPS).then_inc(setup, 1)
            dve.wait_ge(loads, 48)

            def merge(mg):
                r = mg.rows
                if not mg.sample:
                    m = [parts[:, k, BW + H:PART] for k in range(3)]
                    need(dve, "parts_in", mg)
                    done(tt(top[:, 0, :], m[0], m[1], MAX), "top0_ready")
                    need(dve, "top0_ready", mg)
                    done(tt(top[:, 1, :], top[:, 0, :], m[2], MAX), "top_ready")
                    need(dve, "top_ready", mg)
                    done(tt(wgt[:, :, :], parts[:, :, BW + H:PART],
                            top[:, 1:2, :].broadcast_to([P, 3, H]), SUB), "diff_ready")
                    need(dve, "wgt_ready", mg)
                    done(tt(dens[:, :, :], wgt[:, :, :], parts[:, :, BW:BW + H], M), "den_ready")
                    need(dve, "den_ready", mg)
                    done(V.tensor_reduce(den[:, 0, :], dens[:, :, :].rearrange("p k h -> p h k"), AX_X, A),
                         "sum_ready")
                    need(dve, "sum_ready", mg)
                    done(V.reciprocal(den[:, 1, :], den[:, 0, :]), "inv_ready")
                    need(dve, "inv_ready", mg)
                    done(tt(wgt[:, :, :], wgt[:, :, :], den[:, 1:2, :].broadcast_to([P, 3, H]), M), "wn_ready")
                    need(dve, "wn_ready", mg)
                    for k in range(3):
                        v = parts[:, k, 0:BW].rearrange("p (h d) -> p h d", h=H)
                        ins = tt(v, v, wgt[:, k, :].unsqueeze(2).broadcast_to([P, H, D]), M)
                    done(ins, "scaled_ready")
                    need(dve, "scaled_ready", mg)
                    done(tt(parts[:, 0, 0:BW], parts[:, 0, 0:BW], parts[:, 1, 0:BW], A), "pair_ready")
                    need(dve, "pair_ready", mg)
                need(dve, "tanh_ready", mg)
                done(ts(sig[0:r, :], sig[0:r, :], 0.5, 0.5, M, A), "half_ready")
                need(dve, "half_ready", mg)
                done(tt(sig[0:r, :], sig[0:r, :], gate[0:r, :], M), "sig_ready")
                need(dve, "sig_ready", mg)
                free(dve, "y_ps", mg)
                if mg.sample:
                    need(dve, "parts_in", mg)
                    done(tt(y[0:r, 0:BW], parts[0:r, 0, 0:BW], sig[0:r, :], M), "yA_ready")
                else:
                    done(tt(y[:, 0:BW], parts[:, 0, 0:BW], parts[:, 2, 0:BW], A), "num_ready")
                    need(dve, "num_ready", mg)
                    done(tt(y[:, 0:BW], y[:, 0:BW], sig[:, :], M), "yA_ready")

            def iteration(pr, mg):
                if mg:
                    merge(mg)
                if pr:
                    r = pr.rows
                    need(dve, "x_in", pr)
                    for half in range(2):
                        need(dve, "o_done", pr, half + 1)
                        cols = slice(512 * half, 512 * half + 512)
                        free(dve, "out_ready", pr)
                        done(tt(z[0:r, cols], pj[half][0:r, :], x[0:r, cols], A), "z_ready")
                    need(dve, "rstd_ready", pr)
                    free(dve, "out_out", pr)
                    done(stt(out[0:r, :], z[0:r, :], rstd[0:r, 0:1], finalw[0:r, :], M, M), "out_ready")

            run(dve, iteration)

        @block.gpsimd
        def _(pool):
            def iteration(pr, mg):
                if pr:
                    need(pool, "out_ready", pr)
                    pool.dma_start(rows_of(pr, io["out_s" if pr.sample else "out_p"]), out[0:pr.rows, :])\
                        .then_inc(S["out_out"].sem, 16)

            keep = slice(SEQ - BUF, SEQ)
            for dst, src in ((io["k_p"], io["att_rows"][keep, BW:2 * BW]),
                             (io["v_p"], io["att_rows"][keep, 2 * BW:3 * BW]),
                             (io["k_s"], io["att_s"][:, BW:2 * BW]), (io["v_s"], io["att_s"][:, 2 * BW:3 * BW])):
                pool.dma_start(dst, src).then_inc(loads_out, 16)
            run(pool, iteration)
            need(pool, "out_out", Tile(P, NT))
            pool.wait_ge(loads_out, 64)

        program.close()
        nc.clear_and_free_semaphores(sems)
        nc.all_engine_barrier()


_INS = ("cache_attn_k", "cache_attn_v", "state_delta", "state_delta_conv", "state_hgrn", "state_pool",
        "w_in", "w_out", "delta_a_log", "delta_dt_bias", "delta_norm_w", "hgrn_norm_w", "pool_w",
        "pool_scale")


def build(nc, io, y_p, y_s, k_p, k_s, v_p, v_s, d_p, d_s, dc_p, dc_s, h_p, h_s, pl_p, pl_s):
    def scratch(name, shape):
        return nc.dram_tensor(name, shape, F32, kind="Internal").ap()

    io.update(
        cache_k=io["cache_attn_k"], cache_v=io["cache_attn_v"],
        att_rows=scratch("att_rows", [SEQ, AW]), att_s=scratch("att_s", [TS, AW]),
        sample_rows=scratch("sample_rows", [TS, MW]), y_rows=scratch("y_rows", [SEQ + TS, 3 * BW]),
        parts=scratch("parts", [3, SEQ, PART]), att_o=scratch("att_o", [TS, BW]),
        conv_p=dc_p[0, 0], conv_s=dc_s[0], pool_p=pl_p[0, 0], pool_s=pl_s[0],
        delta_prompt=d_p[0], delta_sample=d_s[0], hgrn_prompt=h_p[0], hgrn_sample=h_s[0],
        out_p=y_p[0], out_s=y_s.rearrange("b t n -> (b t) n"),
        k_p=k_p[0, 0].rearrange("t h d -> t (h d)"), v_p=v_p[0, 0].rearrange("t h d -> t (h d)"),
        k_s=k_s[0].rearrange("b t h d -> (b t) (h d)"), v_s=v_s[0].rearrange("b t h d -> (b t) (h d)"))
    project_attention(nc, io)
    mixers(nc, io, io["consts"], io["cols"], "prompt")
    mixers(nc, io, io["consts"], io["cols"], "sample")
    attend_classes(nc, io)
    attend_cache(nc, io)
    finish(nc, io)


def kernel(**inputs):
    import numpy as _np
    import concourse.bacc as _bacc
    from concourse.bass_utils import run_bass_kernel_spmd as _run

    nc = _bacc.Bacc("TRN2", target_bir_lowering=False, num_devices=1)
    table, cols = host_constants()
    given = {name: _np.asarray(inputs[name]) for name in _INS}
    given["x_p"] = _np.asarray(inputs["x_prompt"])[0]
    given["x_s"] = _np.asarray(inputs["x_sample"]).reshape(TS, DM)
    given["norm_w_fm"] = _np.asarray(inputs["norm_w"])[0].reshape(KD, P).T
    given["conv_w_fm"] = _np.asarray(inputs["delta_conv_w"])[0].reshape(CONV, 6, P).transpose(2, 1, 0)
    given["final_norm_w"] = _np.asarray(inputs["final_norm_w"]).reshape(1, DM)
    given["consts"] = table
    arrays, io = {}, {"cols": cols}
    for name, a in given.items():
        arrays[f"in_{name}"] = _np.ascontiguousarray(a)
        io[name] = nc.dram_tensor(f"in_{name}", a.shape, F32, kind="ExternalInput").ap()
    shapes = ((1, SEQ, DM), (DB, DS, DM), (1, 1, BUF, H, D), (1, DB, DS, H, D), (1, 1, BUF, H, D),
              (1, DB, DS, H, D), (1, 1, H, D, D), (1, DB, H, D, D), (1, 1, CONV - 1, 3 * BW),
              (1, DB, CONV - 1, 3 * BW), (1, 1, H, D, D), (1, DB, H, D, D), (1, 1, PMAX - 1, BW),
              (1, DB, PMAX - 1, BW))
    outs = [nc.dram_tensor(f"out_{i}", shape, F32, kind="ExternalOutput").ap()
            for i, shape in enumerate(shapes)]
    build(nc, io, *outs)
    r = _run(nc, [arrays], core_ids=[0])
    return tuple(r.results[0][f"out_{i}"] for i in range(len(shapes)))
```

```python
from contextlib import ExitStack

import numpy as np

import concourse.bass as bass
from concourse import mybir

F32, F32R = mybir.dt.float32, mybir.dt.float32r
ALU = mybir.AluOpType
ACT = mybir.ActivationFunctionType
AX_X = mybir.AxisListType.X

P = 128
DM = 1024
KD = DM // P
SEQ = 4096
NT = SEQ // P
DB, DS = 8, 8
TS = DB * DS
H, D = 4, 64
BW = H * D
AW = 4 * BW
CONV = 4
PMAX = 16
POOL_WINDOWS = (2, 4, 8, 16)
EPS = 1e-6
NEG = -1e30
MW = 3 * BW + BW + 2 * H + 4 * BW + 2 * BW
GROUPS = ((0, 512), (512, 512), (1032, 512), (1544, 512), (2056, 512), (1024, 8))
Q_QKV, Q_GB, Q_CQ, Q_CF, Q_CI, Q_CG, Q_DX, Q_DG, Q_BETA, Q_A = (
    0, 768, 1024, 1280, 1536, 1792, 2048, 2304, 2560, 2564)
LEVELS = {P: 7, TS: 3}


def _segments(rows):
    seg = rows if rows == P else DS
    return np.arange(rows), seg


def tile_constants(rows):
    n, seg = _segments(rows)
    j, i = n[:, None], n[None, :]
    same = (j // seg) == (i // seg)
    tri = (same & (j <= i)).astype(np.float32)
    neg = np.where(tri > 0, 0.0, NEG).astype(np.float32)
    parts = [tri, same.astype(np.float32), neg]
    s = 1
    while s < seg:
        parts.append((((j // s) % 2 == 0) & ((i // s) % 2 == 1)
                      & (j // (2 * s) == i // (2 * s)) & same).astype(np.float32))
        s *= 2
    parts.append((np.arange(rows // seg)[None, :] == (n // seg)[:, None]).astype(np.float32))
    return np.concatenate(parts, axis=1)


def pool_constants(rows, first):
    n, seg = _segments(rows)
    own, before = [], []
    for win in POOL_WINDOWS:
        j, i = n[:, None], n[None, :]
        cnt = np.minimum(i + 1, win) if first else np.full_like(i, win)
        near = (i - j >= 0) & (i - j < win) & ((j // seg) == (i // seg))
        own.append(near / cnt - (i == j))
        m = np.zeros((P, rows))
        if rows == P:
            dist = i - (n[:, None] - P)
            if not first:
                m = (dist < win) / cnt
        else:
            r = np.arange(DB * (PMAX - 1))[:, None]
            dist = (i % seg) - (r % (PMAX - 1) - (PMAX - 1))
            m[:r.size] = ((dist < win) & (r // (PMAX - 1) == i // seg)) / cnt
        before.append(m)
    own = [np.concatenate([o, np.zeros((P - rows, rows))]) for o in own]
    return np.concatenate(own + before, axis=1).astype(np.float32)


def host_constants():
    cols, parts, at = {}, [], 0
    for name, a in (("ident", np.eye(P, dtype=np.float32)),
                    ("tile_p", tile_constants(P)), ("tile_s", tile_constants(TS)),
                    ("pool_s", pool_constants(TS, False)), ("pool_0", pool_constants(P, True)),
                    ("pool_p", pool_constants(P, False)), ("cache", cache_constants()),
                    *((f"alibi_{d}_{f}", alibi_constants(d, f)) for d in DILATIONS for f in (0, 1))):
        full = np.zeros((P, a.shape[1]), np.float32)
        full[:a.shape[0]] = a
        cols[name] = at
        at += a.shape[1]
        parts.append(full)
    return np.concatenate(parts, axis=1), cols


class Tile:

    def __init__(self, rows, t, row=0, first=False, last=False):
        self.rows, self.t, self.row, self.first, self.last = rows, t, row, first, last
        self.sample = rows == TS
        self.segs = DB if self.sample else 1
        self.seg = rows // self.segs
        self.levels = LEVELS[rows]


class Count:

    def __init__(self, sem, per=1, first=0):
        self.sem, self.per, self.first = sem, per, first

    def wait(self, eng, tile, k=None):
        k = self.per if k is None else k
        if isinstance(tile.t, int) and tile.t <= self.first and k == 0:
            return
        eng.wait_ge(self.sem, tile.t * self.per + (k - self.first * self.per))


class Steps:

    def __init__(self, count, eng):
        self.count, self.eng, self.k = count, eng, 0

    def begin(self, tile):
        self.tile, self.k = tile, 0

    def do(self, ins):
        ins.then_inc(self.count.sem, 1)
        self.k += 1

    def sync(self):
        self.count.wait(self.eng, self.tile, self.k)

    def end(self):
        assert self.k == self.count.per, (self.count.sem, self.k, self.count.per)


def rows_of(tile, dram):
    if isinstance(tile.row, int):
        return dram[tile.row:tile.row + tile.rows, :]
    return dram[bass.ds(tile.row, tile.rows), :]


MIX_STEPS = {"prompt": (45, 23, 10), "sample": (64, 25, 6)}


ACT_FILLS = (0, 2, 4)


def mixers(nc, io, consts, ccols, kind):
    prompt = kind == "prompt"
    R = P if prompt else TS
    SEGS = 1 if prompt else DB
    SEG = R // SEGS
    NL = LEVELS[R]
    FIRST = 1 if prompt else 0
    NB = P if prompt else DB * (PMAX - 1)
    with ExitStack() as ctx:
        sems = []

        def sb(name, shape):
            return ctx.enter_context(nc.sbuf_tensor(f"{kind}_{name}", shape, F32))

        def semaphore(name):
            sems.append(ctx.enter_context(nc.semaphore(f"{kind}_{name}")))
            return sems[-1]

        ident = sb("ident", [P, P])
        mask = sb("mask", [R, 3 * R + NL * R + SEGS])
        pool_step = sb("pool_step", [P, 8 * R])
        pool_first = sb("pool_first", [P, 4 * R]) if prompt else pool_step
        convw = sb("convw", [P, 6, CONV])
        gatew = sb("gatew", [P, 2 * BW])
        pscale = sb("pscale", [P, BW])
        poolw = sb("poolw", [D, 4, D])
        ealog = sb("ealog", [P, H])
        dtb = sb("dtb", [P, H])
        one = sb("one", [P, 1])
        eps = sb("eps", [P, 1])
        pt = sb("pt", [P, MW])
        if prompt:
            w = io["w_mix"]
            normw = sb("normw", [P, KD])
            xin = sb("xin", [P, DM])
            xn = sb("xn", [P, DM])
            rstd = sb("rstd", [P, 2])
            hT = sb("hT", [P, KD, P])
        else:
            before = sb("before", [P, 3 * BW])

        xc = sb("xc", [P, 6, SEGS, SEG + CONV - 1])
        levels_a = sb("levels_a", [P, 2, H * P])
        cvs = levels_a[:, :, :].rearrange("p a n -> p (a n)")[:, 0:6 * R].rearrange("p (k t) -> p k t", k=6)
        X, Y = (levels_a[0:R, n, 0:H * R].rearrange("p (h t) -> p h t", h=H) for n in range(2))
        levels_b = sb("levels_b", [P, 2, H * P])
        sig_c = levels_b[:, :, :].rearrange("p a n -> p (a n)")[:, 0:6 * R].rearrange("p (k t) -> p k t", k=6)
        Am = [levels_b[0:R, n, 0:H * R].rearrange("p (h t) -> p h t", h=H) for n in range(2)]
        Z = sb("Z", [R, H, R])
        sq = sb("sq", [R, 8, D])
        qk = sb("qk", [R, 8, D])
        vB = sb("vB", [R, H, D])
        ss8 = sb("ss8", [R, 8])
        kb = sb("kb", [R, H, D])
        qg = sb("qg", [R, H, D])
        kbg = sb("kbg", [R, H, D])
        kend = sb("kend", [R, H, D])
        vb = sb("vb", [R, H, D])
        knT, kbT, qnT = (sb(n, [D, H, R]) for n in ("knT", "kbT", "qnT"))
        gcol = sb("gcol", [R, 2, H])
        gb = sb("gb", [R, H, R])
        dec = sb("dec", [R, H, R])
        At = sb("At", [R, H, R])
        QKt = sb("QKt", [R, H, R])
        vn = sb("vn", [R, H, D])
        WIDE = H * R if prompt else H * DB * (TS + DS)
        wTx = sb("wTx", [D, WIDE])
        qgx = sb("qgx", [D, WIDE])
        qcgx = wTx
        SB = sb("SB", [D, H, SEGS, D])
        eglB = sb("eglB", [D, H, SEGS])
        sig = sb("sig", [R, 4, BW])
        bet = sb("bet", [R, H])
        zf = sb("zf", [R, BW + H])
        lab = sb("lab", [R, BW + H])
        ls = sb("ls", [R, BW + H])
        vC = sb("vC", [R, H, D])
        G = sb("G", [D, H, R])
        kgT = sb("kgT", [D, H, R])
        EG = sb("EG", [D, H, R])
        qcT, kcT = sb("qcT", [D, H, R]), sb("kcT", [D, H, R])
        kg = sb("kg", [R, H, D])
        Ml = [sb(f"Ml{n}", [D, H, R]) for n in range(2)]
        acc = sb("acc", [R, H, R])
        tmp = sb("tmp", [R, H, R])
        eglC = sb("eglC", [D, H, SEGS])
        SC = sb("SC", [D, H, SEGS, D])
        xd = sb("xd", [P, BW])
        xdp = sb("xdp", [P, BW])
        pT = sb("pT", [D, 4, R])
        oBC = sb("oBC", [R, 8, D])
        y = sb("y", [R, 3 * BW])
        if not prompt:
            vBx, vCx = sb("vBx", [R, H, DB, D]), sb("vCx", [R, H, DB, D])
        else:
            vBx, vCx = vn, vC

        def bank(name):
            return ctx.enter_context(nc.psum_tensor(f"{kind}_{name}", [P, 512], F32))

        pj = [bank("pj0"), bank("pj1")]
        c = [bank(f"c{n}") for n in range(6)]

        tri, same, neg = (mask[:, n * R:(n + 1) * R] for n in range(3))
        level = [mask[:, (3 + n) * R:(4 + n) * R] for n in range(NL)]
        segm = mask[:, (3 + NL) * R:(3 + NL) * R + SEGS]

        def pool_matrix(tile, g):
            own = pool_first if tile.first else pool_step
            return own[0:R, g * R:(g + 1) * R], pool_step[0:NB, (4 + g) * R:(5 + g) * R]

        def hv(b, rows=R, width=R):
            return b[0:rows, 0:H * width].rearrange("p (h n) -> p h n", h=H)

        def odd_heads(bank, odd):
            return bank[odd * D:(odd + 1) * D, 0:2 * R].rearrange("d (h t) -> d h t", h=2)

        def window(buf, h, b):
            per = WIDE // H
            return buf[:, h * per + b * R:h * per + (b + 1) * R]

        def own_columns(buf):
            v = buf[:, :].rearrange("d (h t) -> d h t", h=H)
            if prompt:
                return v
            return buf[:, :].rearrange("d (h b t) -> d h b t", h=H, b=SEGS)[:, :, :, 0:SEG]

        def fm(ap):
            return ap if prompt else ap.rearrange("d h (b t) -> d h b t", b=SEGS)

        def halves(t, k):
            return t[:, :, :].rearrange("d h (n a s) -> d (h n) a s", a=2, s=2 ** k)

        S = {}
        mixed = """fwd_ps xc_ready halo_ready cv_ready sigc_ready cvs_ready back_ps qkv_tm ss_ready rn_ready
            qk_normed th_ready sg_ready zf_ready lab_ready ls_ready g_ready gb_ready lk_ready kC_ready
            vC_ready xd_ready xdp_ready pool_ps pT_ready poolw_ps yD_ready G_ps G_ready gcol_ps gcol_tm
            gcol_ready R_ps R_read dec_in dec_ready kb_ready qg_ready scaled_ready knT_ps
            kbT_ps qnT_ps qgT_ps qcT_ps kcT_ps knT_ready kbT_ready qnT_ready qgx_ready qcT_ready kcT_ready
            kk_ps kq_ps At_ready QKt_ready EL_in EL_ready kgT_ready wT_ps wT_ready vn_ps vn_ready
            vBx_ready vCx_ready oB_ps dSB_ps SB_ready kg_ps kg_ready qcg_ready oC_ps dSC_ps SC_ready
            oB_tm oC_tm ss2_ready rn2_ready gates_ready y_ready ecol_ready pscaled_ready""".split()
        for n in mixed:
            S[n] = Count(semaphore(n), 1, FIRST)
        for n, per in (("am_ready", NL), ("z_ps", NL), ("z_ready", NL - 1), ("xz_ps", NL - 2),
                       ("Xt_ps", NL - 2), ("zy_ps", 1), ("X_ready", NL - 1), ("Y_ready", NL),
                       ("tmp_ready", NL), ("cd_ready", NL), ("ce_ready", NL), ("cl_ready", NL),
                       ("cprod_ps", NL + 1), ("cacc_ready", NL + 1), ("y_out", 16)):
            S[n] = Count(semaphore(n), per, FIRST)
        if prompt:
            for n, per in (("x_in", 16), ("sq_ready", 1), ("lnx_ready", 1), ("rstd_ready", 1),
                           ("xn_ready", 1), ("ht_ps", 2), ("hT_ready", 2),
                           ("pj_ps", 6), ("pt_ready", 6)):
                S[n] = Count(semaphore(n), per)
            spill = semaphore("spill")
        loads, setup, state_out = semaphore("loads"), semaphore("setup"), semaphore("state_out")
        halved = semaphore("halved")
        steps_of = dict(zip(("dve", "act", "pool"), MIX_STEPS[kind]))
        own_steps = {e: Count(semaphore(f"{e}_steps"), n, FIRST) for e, n in steps_of.items()}
        n_loads, n_setup = (12 if prompt else 21), 10

        def need(eng, name, tile, k=None):
            S[name].wait(eng, tile, k)

        def free(eng, name, tile):
            S[name].wait(eng, tile, 0)

        def done(ins, name):
            ins.then_inc(S[name].sem, 1)

        def run(eng, iteration):
            if not prompt:
                iteration(None, Tile(TS, 0, SEQ), None)
                return
            own = Tile(TS, 0, 0)
            tile = lambda n, **k: Tile(P, n + 1, n * P, **k)
            iteration(None, None, own)
            iteration(own, None, tile(0))
            iteration(tile(0), None, tile(1))
            iteration(tile(1), tile(0, first=True), tile(2))
            with eng.Fori(2, NT - 1) as i:
                iteration(tile(i), tile(i - 1), tile(i + 1))
            iteration(tile(NT - 1), tile(NT - 2), None)
            iteration(None, tile(NT - 1, last=True), None)

        program = ExitStack()
        block = program.enter_context(nc.Block())

        @block.sync
        def _(sp):
            sent = [0]

            def load(dst, src):
                sp.dma_start(dst, src).then_inc(loads, 16)
                sent[0] += 1

            cx = ccols["tile_p" if prompt else "tile_s"]
            cp = ccols["pool_p" if prompt else "pool_s"]
            if prompt:
                load(normw[:, :], io["norm_w_fm"])
                load(pool_first[:, :], consts[:, ccols["pool_0"]:ccols["pool_0"] + 4 * R])
            else:
                load(pt[0:R, :], io["sample_rows"])
                load(before[0:DB * 3, :], io["state_delta_conv"][0].rearrange("b r n -> (b r) n"))
                load(xdp[0:NB, :], io["state_pool"][0].rearrange("b r n -> (b r) n"))
                for h in range(H):
                    load(SB[:, h, :, :], io["state_delta"][0][:, h].rearrange("b k v -> k b v"))
                    load(SC[:, h, :, :], io["state_hgrn"][0][:, h].rearrange("b k v -> k b v"))
            load(ident[:, :], consts[:, ccols["ident"]:ccols["ident"] + P])
            load(mask[:, :], consts[0:R, cx:cx + 3 * R + NL * R + SEGS])
            load(pool_step[:, :], consts[:, cp:cp + 8 * R])
            load(convw[:, :, :], io["conv_w_fm"])
            for n, name in enumerate(("delta_norm_w", "hgrn_norm_w")):
                load(gatew[:, n * BW:n * BW + D], io[name].broadcast_to([P, D]))
            load(pscale[:, :], io["pool_scale"].broadcast_to([P, BW]))
            load(poolw[:, :, :], io["pool_w"][0].rearrange("g c d -> c g d"))
            load(ealog[:, :], io["delta_a_log"].broadcast_to([P, H]))
            load(dtb[:, :], io["delta_dt_bias"].broadcast_to([P, H]))
            assert sent[0] == n_loads, sent[0]

            def iteration(pr, ch, nm):
                if nm:
                    free(sp, "xn_ready", nm)
                    sp.dma_start(xin[0:nm.rows, :], rows_of(nm, io["x_s" if nm.sample else "x_p"]))\
                        .then_inc(S["x_in"].sem, 16)
                if pr and pr.sample:
                    need(sp, "pt_ready", pr)
                    sp.dma_start(io["sample_rows"], pt[0:TS, :]).then_inc(spill, 16)

            run(sp, iteration)
            n_out = 0
            if prompt:
                sp.wait_ge(spill, 16)
                need(sp, "pt_ready", Tile(P, NT))
                sp.dma_start(io["conv_p"], pt[P - 3:P, 0:3 * BW]).then_inc(state_out, 16)
                sp.dma_start(io["pool_p"], pt[P - 15:P, Q_DX:Q_DX + BW]).then_inc(state_out, 16)
                last = Tile(P, NT)
            else:
                rows = io["sample_rows"].rearrange("(b s) n -> b s n", s=DS)
                sp.dma_start(io["conv_s"], rows[:, DS - 3:DS, 0:3 * BW]).then_inc(state_out, 16)
                sp.dma_start(io["pool_s"][:, 7:15, :], rows[:, :, Q_DX:Q_DX + BW]).then_inc(state_out, 16)
                sp.dma_start(io["pool_s"][:, 0:7, :], io["state_pool"][0][:, 8:15, :])\
                    .then_inc(state_out, 16)
                n_out = 1
                last = Tile(TS, 0)
            need(sp, "SB_ready", last)
            need(sp, "SC_ready", last)
            for h in range(H):
                for name, state in (("delta", SB), ("hgrn", SC)):
                    out = io[f"{name}_{kind}"][:, h].rearrange("b k v -> k b v")
                    sp.dma_start(out, state[:, h, :, :]).then_inc(state_out, 16)
            sp.wait_ge(state_out, 16 * (2 + n_out + 2 * H))
            need(sp, "y_out", last)

        @block.tensor
        def _(pe):
            mm = nc.tensor.matmul

            def transpose(out, in_):
                k = in_.shape[0]
                return nc.tensor.transpose(out, in_, ident[0:k, 0:k])

            pe.wait_ge(loads, n_loads * 16)
            if not prompt:
                for n in range(6):
                    last = transpose(c[5][:, 24 * n:24 * n + 24], before[0:24, P * n:P * n + P])
                last.then_inc(setup, 1)
            pe.wait_ge(setup, n_setup)

            if prompt:
                pe.wait_ge(io["w_mix_in"], 16 * KD)

            def norm_transposes(tile):
                r = tile.rows
                need(pe, "xn_ready", tile)
                for half in range(2):
                    for k in range(4):
                        kk = 4 * half + k
                        last = transpose(pj[half][:, k * r:(k + 1) * r], xn[0:r, kk * P:(kk + 1) * P])
                    done(last, "ht_ps")

            def project(tile, g, k):
                at, n = GROUPS[g]
                if k == 0 and g < 2:
                    need(pe, "hT_ready", tile)
                if k == 0 and g >= 2:
                    need(pe, "pt_ready", tile, g - 1)
                last = mm(pj[g % 2][0:tile.rows, 0:n], hT[:, k, 0:tile.rows], w[:, k, at:at + n],
                          start=(k == 0), stop=(k == KD - 1))
                if k == KD - 1:
                    done(last, "pj_ps")

            def each_head(bank, width, lhs, rhs, name, rows=R):
                for h in range(H):
                    last = mm(bank[0:rows, h * width:(h + 1) * width], lhs(h), rhs(h),
                              start=True, stop=True)
                if name:
                    done(last, name)

            def settled():
                pe.wait_ge(setup, n_setup)

            def heads_to_fm(bank, src, name):
                for pair in range(2):
                    last = transpose(bank[:, pair * R:(pair + 1) * R], src[:, pair * P:(pair + 1) * P])
                done(last, name)

            def columns(rows):
                return rows.rearrange("p h d -> p (h d)")

            def iteration(pr, ch, nm):
                part = [0]

                def fill(n):
                    for _ in range(n):
                        if pr and part[0] < 6 * KD:
                            project(pr, part[0] // KD, part[0] % KD)
                            part[0] += 1

                if ch:
                    mix(ch, fill)
                fill(6 * KD)
                if nm:
                    if pr:
                        need(pe, "pt_ready", pr)
                    norm_transposes(nm)

            def mix(ch, fill):
                if prompt:
                    need(pe, "pt_ready", ch)
                free(pe, "SC_ready", ch)
                free(pe, "vn_ready", ch)
                for n in range(6):
                    b, k = (c[0], n) if n < 4 else (c[1], n - 4)
                    last = transpose(b[:, k * R:(k + 1) * R], pt[0:R, n * P:(n + 1) * P])
                done(last, "fwd_ps")
                need(pe, "xd_ready", ch)
                free(pe, "xdp_ready", ch)
                free(pe, "oB_tm", ch)
                for g in range(4):
                    own, prev = pool_matrix(ch, g)
                    out = c[2][0:D, g * R:(g + 1) * R]
                    mm(out, xd[0:R, g * D:(g + 1) * D], own, start=True, stop=False)
                    n = PMAX if prompt else R
                    last = mm(out[:, 0:n], xdp[0:NB, g * D:(g + 1) * D], prev[:, 0:n], start=False,
                              stop=True)
                done(last, "pool_ps")
                fill(4)
                need(pe, "ls_ready", ch)
                free(pe, "oC_tm", ch)
                for pair in range(2):
                    last = mm(c[5][:, pair * R:(pair + 1) * R], ls[:, pair * P:(pair + 1) * P], tri,
                              start=True, stop=True)
                done(last, "G_ps")
                need(pe, "gb_ready", ch)
                free(pe, "kg_ready", ch)
                last = mm(c[4][0:R, 0:H], tri, gb[:, :, 0], start=True, stop=True)
                if not prompt:
                    last = mm(c[4][0:R, H:2 * H], same, gb[:, :, 0], start=True, stop=True)
                done(last, "gcol_ps")
                free(pe, "SB_ready", ch)
                each_head(c[3], R, lambda h: gb[:, h, :], lambda h: tri, "R_ps")
                fill(1)
                need(pe, "pT_ready", ch)
                each_head(c[2], D, lambda g: pT[:, g, :], lambda g: poolw[:, g, :], "poolw_ps")
                fill(4)
                settled()
                need(pe, "sg_ready", ch)
                need(pe, "R_read", ch)
                heads_to_fm(c[3], sig[:, 1, :], "qcT_ps")
                need(pe, "cvs_ready", ch)
                for n in range(6):
                    b, k = (c[0], n) if n < 4 else (c[1], n - 4)
                    last = transpose(b[0:R, k * P:(k + 1) * P], cvs[:, n, :])
                done(last, "back_ps")
                fill(3)
                settled()
                need(pe, "kC_ready", ch)
                need(pe, "gcol_tm", ch)
                heads_to_fm(c[4], zf, "kcT_ps")
                fill(4)
                need(pe, "qcT_ready", ch)
                need(pe, "kcT_ready", ch)
                each_head(c[4], R, lambda h: kcT[:, h, :], lambda h: qcT[:, h, :], "cprod_ps")
                settled()
                need(pe, "qk_normed", ch)
                heads_to_fm(c[0], columns(qk[:, 4:8, :]), "knT_ps")
                settled()
                need(pe, "kb_ready", ch)
                heads_to_fm(c[1], columns(kb[:, :, :]), "kbT_ps")
                settled()
                need(pe, "yD_ready", ch)
                heads_to_fm(c[2], columns(qk[:, 0:4, :]), "qnT_ps")
                settled()
                need(pe, "G_ready", ch)
                need(pe, "qg_ready", ch)
                heads_to_fm(c[5], columns(qg[:, :, :]), "qgT_ps")
                c_level(ch, 0)
                need(pe, "knT_ready", ch)
                need(pe, "kbT_ready", ch)
                each_head(c[0], R, lambda h: knT[:, h, :], lambda h: kbT[:, h, :], "kk_ps")
                need(pe, "qnT_ready", ch)
                each_head(c[1], R, lambda h: knT[:, h, :], lambda h: qnT[:, h, :], "kq_ps")
                fill(2)
                for k in range(NL):
                    if k:
                        need(pe, "X_ready", ch, k)
                    if k >= 2:
                        for h in range(H):
                            last = transpose(c[2][0:R, h * R:(h + 1) * R], X[:, h, :])
                        done(last, "Xt_ps")
                    need(pe, "am_ready", ch, k + 1)
                    if k == 0:
                        need(pe, "At_ready", ch)
                        for h in range(H):
                            last = transpose(c[0][0:R, h * R:(h + 1) * R], Am[0][:, h, :])
                        done(last, "z_ps")
                    else:
                        each_head(c[0], R, lambda h: Am[k % 2][:, h, :], lambda h: X[:, h, :], "z_ps")
                    fill(1)
                    if k == 1:
                        need(pe, "QKt_ready", ch)
                        need(pe, "qnT_ready", ch)
                    if k:
                        need(pe, "z_ready", ch, k)
                        need(pe, "Y_ready", ch, k)
                    if 0 < k < NL - 1:
                        each_head(c[1], R, lambda h: Y[:, h, :], lambda h: Z[:, h, :], "xz_ps")
                    if k == NL - 1:
                        each_head(c[2], R, lambda h: Z[:, h, :], lambda h: Y[:, h, :], "zy_ps")
                    if k + 1 < NL:
                        c_level(ch, k + 1)
                    fill(2 if k < NL - 1 else 1)
                need(pe, "Y_ready", ch, NL)
                need(pe, "scaled_ready", ch)
                each_head(c[0], R, lambda h: kbg[:, h, :], lambda h: Y[:, h, :], "wT_ps", D)
                settled()
                need(pe, "kgT_ready", ch)
                need(pe, "tmp_ready", ch, NL)
                for h in range(H):
                    last = transpose(c[4][0:R, h * D:(h + 1) * D], kgT[:, h, :])
                done(last, "kg_ps")
                fill(1)
                need(pe, "wT_ready", ch)
                free(pe, "SB_ready", ch)
                for h in range(H):
                    out = c[1][0:R, h * D:(h + 1) * D]
                    mm(out, Y[:, h, :], vb[:, h, :], start=True, stop=False)
                    for b in range(SEGS):
                        last = mm(out, window(wTx, h, b), SB[:, h, b, :], start=False,
                                  stop=(b == SEGS - 1))
                done(last, "vn_ps")
                fill(2)
                need(pe, "vn_ready", ch)
                need(pe, "qgx_ready", ch)
                for h in range(H):
                    out = c[2][0:R, h * D:(h + 1) * D]
                    for b in range(SEGS):
                        mm(out, window(qgx, h, b), SB[:, h, b, :], start=(b == 0), stop=False)
                    last = mm(out, QKt[:, h, :], vn[:, h, :], start=False, stop=True)
                done(last, "oB_ps")
                need(pe, "qcT_ready", ch)
                need(pe, "kg_ready", ch)
                if not prompt:
                    need(pe, "vBx_ready", ch)
                for h in range(H):
                    out = c[3][0:D, h * D:(h + 1) * D] if prompt else (c[3], c[4], c[0], c[1])[h][0:D, :]
                    v = vBx[:, h, :] if prompt else vBx[:, h, :, :]
                    last = mm(out, kend[:, h, :], v, start=True, stop=True)
                done(last, "dSB_ps")
                fill(KD)
                need(pe, "qcg_ready", ch)
                need(pe, "cacc_ready", ch)
                free(pe, "SC_ready", ch)
                for h in range(H):
                    out = c[5][0:R, h * D:(h + 1) * D]
                    for b in range(SEGS):
                        mm(out, window(qcgx, h, b), SC[:, h, b, :], start=(b == 0), stop=False)
                    last = mm(out, acc[:, h, :], vC[:, h, :], start=False, stop=True)
                done(last, "oC_ps")
                need(pe, "SB_ready", ch)
                if not prompt:
                    need(pe, "vCx_ready", ch)
                for h in range(H):
                    out = c[0][0:D, h * D:(h + 1) * D] if prompt else (c[0], c[1], c[3], c[4])[h][0:D, :]
                    v = vCx[:, h, :] if prompt else vCx[:, h, :, :]
                    last = mm(out, kg[:, h, :], v, start=True, stop=True)
                done(last, "dSC_ps")

            def c_level(ch, k):
                need(pe, "cl_ready", ch, k + 1)
                if k:
                    need(pe, "tmp_ready", ch, k)
                else:
                    need(pe, "cacc_ready", ch, 1)
                each_head(c[4], R, lambda h: Ml[k % 2][:, h, :], lambda h: Ml[k % 2][:, h, :], "cprod_ps")

            run(pe, iteration)

        @block.scalar
        def _(act):
            do_act = nc.scalar.activation
            st = Steps(own_steps["act"], act)
            act.wait_ge(loads, n_loads * 16)
            act.wait_ge(setup, n_setup - 1)
            do_act(ealog[:, :], ealog[:, :], ACT.Exp).then_inc(setup, 1)
            def copy_group(tile, g):
                at = 512 * g
                n = GROUPS[g][1]
                need(act, "pj_ps", tile, g + 1)
                done(do_act(pt[0:tile.rows, at:at + n], pj[g % 2][0:tile.rows, 0:n], ACT.Copy), "pt_ready")

            def heads_from(out, bank, name):
                st.do(do_act(out[:, 0:H:2, :], odd_heads(bank, 0), ACT.Copy))
                done(do_act(out[:, 1:H:2, :], odd_heads(bank, 1), ACT.Copy), name)

            def normalise(tile):
                r = tile.rows
                need(act, "x_in", tile)
                free(act, "ht_ps", tile)
                done(do_act(xn[0:r, :], xin[0:r, :], ACT.Square, accum_out=rstd[0:r, 0:1]), "sq_ready")
                need(act, "sq_ready", tile)
                done(do_act(rstd[0:r, 1:2], rstd[0:r, 0:1], ACT.Ln, scale=1.0 / DM, bias=eps[0:r, :]),
                     "lnx_ready")
                need(act, "lnx_ready", tile)
                done(do_act(rstd[0:r, 0:1], rstd[0:r, 1:2], ACT.Exp, scale=-0.5), "rstd_ready")

            def iteration(pr, ch, nm):
                part = [0]

                def fill():
                    if pr and part[0] < 6:
                        if part[0] == 0:
                            if ch:
                                need(act, "fwd_ps", ch)
                                need(act, "sg_ready", ch)
                                need(act, "zf_ready", ch)
                            elif pr.t == 1:
                                act.wait_ge(spill, 16)
                        copy_group(pr, part[0])
                        part[0] += 1

                if ch:
                    st.begin(ch)
                    mix(ch, fill, nm)
                    st.end()
                elif nm and not pr:
                    normalise(nm)
                while pr and part[0] < 6:
                    fill()
                if pr and nm and not ch:
                    normalise(nm)

            def mix(ch, fill, nm):
                if prompt:
                    need(act, "pt_ready", ch)
                free(act, "xdp_ready", ch)
                done(do_act(xd[0:R, :], pt[0:R, Q_DX:Q_DX + BW], ACT.Copy), "xd_ready")
                free(act, "dSC_ps", ch)
                done(do_act(vC[:, :, :], pt[0:R, Q_CI:Q_CI + BW].rearrange("p (h d) -> p h d", h=H),
                            ACT.Copy), "vC_ready")
                need(act, "fwd_ps", ch)
                free(act, "halo_ready", ch)
                for b, k0, nk in ((c[0], 0, 4), (c[1], 4, 2)):
                    for k in range(nk):
                        ins = do_act(xc[:, k0 + k, :, CONV - 1:],
                                     b[:, k * R:(k + 1) * R].rearrange("p (b t) -> p b t", b=SEGS), ACT.Copy)
                        if k0 + k < 5:
                            st.do(ins)
                        else:
                            done(ins, "xc_ready")
                need(act, "zf_ready", ch)
                st.do(do_act(lab[:, :], zf[:, :], ACT.Abs))
                st.sync()
                st.do(do_act(lab[:, :], lab[:, :], ACT.Exp, scale=-1.0))
                st.sync()
                done(do_act(lab[:, :], lab[:, :], ACT.Ln, bias=one[0:R, :]), "lab_ready")
                free(act, "y_ready", ch)
                st.do(do_act(sig[:, 0:2, :], pt[0:R, Q_GB:Q_GB + 2 * BW]
                             .rearrange("p (a n) -> p a n", a=2), ACT.Tanh, scale=0.5))
                st.do(do_act(sig[:, 2, :], pt[0:R, Q_CG:Q_CG + BW], ACT.Tanh, scale=0.5))
                st.do(do_act(sig[:, 3, :], pt[0:R, Q_DG:Q_DG + BW], ACT.Tanh, scale=0.5))
                done(do_act(bet[:, :], pt[0:R, Q_BETA:Q_BETA + H], ACT.Tanh, scale=0.5), "th_ready")
                need(act, "pool_ps", ch)
                done(do_act(pT[:, :, :], hv(c[2], D), ACT.Copy), "pT_ready")
                need(act, "G_ps", ch)
                heads_from(G, c[5], "G_ready")
                need(act, "gcol_ps", ch)
                n = 1 if prompt else 2
                done(do_act(gcol[:, 0:n, :], c[4][0:R, 0:n * H].rearrange("p (a h) -> p a h", a=n), ACT.Copy),
                     "gcol_tm")
                need(act, "cv_ready", ch)
                done(do_act(sig_c, cvs, ACT.Tanh, scale=0.5), "sigc_ready")
                nc.scalar.preload_act_table_set("natural_log_exp_and_others")
                need(act, "lk_ready", ch)
                done(do_act(zf[:, 0:BW], zf[:, 0:BW], ACT.Exp), "kC_ready")
                need(act, "EL_in", ch)
                st.do(do_act(eglC[:, :, :], fm(G[:, :, :])[:, :, :, SEG - 1] if not prompt
                             else G[:, :, SEG - 1:SEG], ACT.Exp))
                need(act, "back_ps", ch)
                st.do(do_act(qk[:, :, :], c[0][0:R, :].rearrange("p (h d) -> p h d", h=8), ACT.Copy,
                             scale=0.5))
                free(act, "scaled_ready", ch)
                st.sync()
                done(do_act(vB[:, :, :], c[1][0:R, 0:BW].rearrange("p (h d) -> p h d", h=H), ACT.Copy,
                            scale=0.5), "qkv_tm")
                need(act, "gcol_ready", ch)
                need(act, "R_read", ch)
                done(do_act(gcol[:, :, :], gcol[:, :, :], ACT.Exp), "ecol_ready")
                need(act, "cd_ready", ch, 1)
                done(do_act(Ml[0][:, :, :], Ml[0][:, :, :], ACT.Exp), "ce_ready")
                need(act, "cd_ready", ch, 2)
                done(do_act(Ml[1][:, :, :], Ml[1][:, :, :], ACT.Exp), "ce_ready")
                need(act, "ss_ready", ch)
                st.do(do_act(ss8[:, :], ss8[:, :], ACT.Ln, bias=eps[0:R, :]))
                st.sync()
                done(do_act(ss8[:, :], ss8[:, :], ACT.Exp, scale=-0.5), "rn_ready")
                need(act, "dec_in", ch)
                st.do(do_act(eglB[:, :, :], eglB[:, :, :], ACT.Exp))
                done(do_act(dec[:, :, :], dec[:, :, :], ACT.Exp), "dec_ready")
                fill()
                need(act, "knT_ps", ch)
                heads_from(knT, c[0], "knT_ready")
                need(act, "kbT_ps", ch)
                heads_from(kbT, c[1], "kbT_ready")
                need(act, "qgT_ps", ch)
                if prompt:
                    heads_from(own_columns(qgx), c[5], "qgx_ready")
                else:
                    for h in range(H):
                        ins = do_act(own_columns(qgx)[:, h], odd_heads(c[5], h % 2)[:, h // 2, :]
                                     .rearrange("d (b t) -> d b t", b=SEGS), ACT.Copy)
                        if h < H - 1:
                            st.do(ins)
                        else:
                            done(ins, "qgx_ready")
                st.do(do_act(EG[:, :, :], G[:, :, :], ACT.Exp))
                done(do_act(kgT[:, :, :], kgT[:, :, :], ACT.Exp), "EL_ready")
                for k in range(NL):
                    if k:
                        need(act, "z_ps", ch, k + 1)
                        done(do_act(Z[:, :, :], hv(c[0]), ACT.Copy), "z_ready")
                    if k + 2 < NL:
                        need(act, "cd_ready", ch, k + 3)
                        m = Ml[k % 2]
                        done(do_act(m[:, :, :], m[:, :, :], ACT.Exp), "ce_ready")
                    if k in ACT_FILLS:
                        fill()
                    if k == 3 and nm:
                        normalise(nm)
                need(act, "wT_ps", ch)
                for h in range(H):
                    out = own_columns(wTx)[:, h]
                    src = c[0][0:D, h * R:(h + 1) * R]
                    ins = do_act(out, src if prompt else src.rearrange("d (b t) -> d b t", b=SEGS), ACT.Copy,
                                 scale=-1.0)
                    if h < H - 1:
                        st.do(ins)
                    else:
                        done(ins, "wT_ready")
                need(act, "kg_ps", ch)
                done(do_act(kg[:, :, :], hv(c[4], R, D), ACT.Copy), "kg_ready")
                need(act, "vn_ps", ch)
                done(do_act(vn[:, :, :], hv(c[1], R, D), ACT.Copy), "vn_ready")
                fill()
                need(act, "oB_ps", ch)
                done(do_act(oBC[:, 0:4, :], hv(c[2], R, D), ACT.Copy), "oB_tm")
                fill()
                need(act, "oC_ps", ch)
                done(do_act(oBC[:, 4:8, :], hv(c[5], R, D), ACT.Copy), "oC_tm")
                need(act, "ss2_ready", ch)
                st.do(do_act(ss8[:, :], ss8[:, :], ACT.Ln, scale=1.0 / D, bias=eps[0:R, :]))
                st.sync()
                done(do_act(ss8[:, :], ss8[:, :], ACT.Exp, scale=-0.5), "rn2_ready")

            run(act, iteration)

        @block.vector
        def _(dve):
            V = nc.vector
            tt, ts, stt = V.tensor_tensor, V.tensor_scalar, V.scalar_tensor_tensor
            M, A, SUB = ALU.mult, ALU.add, ALU.subtract
            st = Steps(own_steps["dve"], dve)
            V.memset(one[:, :], 1.0).then_inc(setup, 1)
            V.memset(eps[:, :], EPS).then_inc(setup, 1)
            if prompt:
                V.memset(SB[:, :, :, :], 0.0).then_inc(setup, 1)
                V.memset(SC[:, :, :, :], 0.0).then_inc(setup, 1)
                V.memset(xc[:, :, :, 0:CONV - 1], 0.0).then_inc(setup, 1)
                V.memset(xdp[:, :], 0.0).then_inc(setup, 1)
            else:
                V.memset(wTx[:, :], 0.0).then_inc(setup, 1)
                V.memset(qgx[:, :], 0.0).then_inc(setup, 1)
            dve.wait_ge(loads, n_loads * 16)
            V.tensor_scalar(pscale[:, :], pscale[:, :], 0.5, None, M).then_inc(setup, 1)
            halves_of = gatew[:, :].rearrange("p (n a d) -> p n a d", n=2, a=H)[:, :, 0, :]
            V.tensor_scalar(halves_of, halves_of, 0.5, None, M).then_inc(halved, 1)
            dve.wait_ge(halved, 1)
            for n in range(2):
                src = gatew[:, n * BW:n * BW + D].rearrange("p (a d) -> p a d", a=1)
                V.tensor_copy(gatew[:, n * BW + D:(n + 1) * BW].rearrange("p (a d) -> p a d", a=3),
                              src.broadcast_to([P, 3, D])).then_inc(setup, 1)
            if not prompt:
                dve.wait_ge(setup, 8)
                V.tensor_copy(xc[:, :, :, 0:CONV - 1], c[5][:, 0:144]
                              .rearrange("p (k b t) -> p k b t", k=6, b=SEGS)).then_inc(setup, 1)
            dve.wait_ge(setup, n_setup)

            def xn_rows(tile):
                r = tile.rows
                need(dve, "rstd_ready", tile)
                done(ts(xn[0:r, :], xin[0:r, :], rstd[0:r, 0:1], None, M), "xn_ready")

            def hT_rows(tile):
                r = tile.rows
                for half in range(2):
                    need(dve, "ht_ps", tile, half + 1)
                    ks = slice(4 * half, 4 * half + 4)
                    done(tt(hT[:, ks, 0:r], pj[half][:, 0:4 * r].rearrange("p (k t) -> p k t", k=4),
                            normw[:, ks].unsqueeze(2).broadcast_to([P, 4, r]), M), "hT_ready")

            def iteration(pr, ch, nm):
                if ch:
                    st.begin(ch)
                    mix(ch, nm)
                    st.end()
                elif nm:
                    xn_rows(nm)
                    hT_rows(nm)

            def over(ap, shape):
                return ap.unsqueeze(len(ap.shape)).broadcast_to(shape)

            def per_head(ap):
                return ap.unsqueeze(1).broadcast_to([R, H, R])

            def decay_rows(ch, k):
                need(dve, "ce_ready", ch, k + 1)
                need(dve, "kcT_ready", ch)
                need(dve, "qcT_ready", ch)
                m = halves(Ml[k % 2], k)
                st.do(tt(m[:, :, 0, :], m[:, :, 0, :], halves(kcT, k)[:, :, 0, :], M))
                done(tt(m[:, :, 1, :], m[:, :, 1, :], halves(qcT, k)[:, :, 1, :], M), "cl_ready")

            def mix(ch, nm):
                if prompt:
                    need(dve, "pt_ready", ch)
                free(dve, "kcT_ps", ch)
                free(dve, "lk_ready", ch)
                st.do(V.tensor_copy(zf[:, 0:BW], pt[0:R, Q_CF:Q_CF + BW]))
                done(stt(zf[:, BW:], pt[0:R, Q_A:Q_A + H], -1.0, dtb[0:R, :], M, SUB), "zf_ready")
                need(dve, "lab_ready", ch)
                done(stt(ls[:, :], zf[:, :], 0.0, lab[:, :], ALU.min, SUB), "ls_ready")
                need(dve, "ls_ready", ch)
                done(tt(ls[:, BW:], ls[:, BW:], ealog[0:R, :], M), "g_ready")
                done(tt(zf[:, 0:BW], ls[:, 0:BW], zf[:, 0:BW], SUB), "lk_ready")
                need(dve, "g_ready", ch)
                done(V.tensor_copy(gb[:, :, :], over(ls[:, BW:], [R, H, R])), "gb_ready")
                need(dve, "xc_ready", ch)
                free(dve, "vn_ps", ch)
                for tap in range(CONV):
                    for k in range(6):
                        src = xc[:, k, :, tap:tap + SEG]
                        out = cvs[:, k, :].rearrange("p (b t) -> p b t", b=SEGS)
                        if tap == 0:
                            ins = ts(out, src, convw[:, k, 0:1], None, M)
                        else:
                            ins = stt(out, src, convw[:, k, tap:tap + 1], out, M, A)
                        if tap < CONV - 1 or k < 5:
                            st.do(ins)
                        else:
                            done(ins, "cv_ready")
                    if tap < CONV - 1:
                        st.sync()
                if prompt:
                    done(V.tensor_copy(xc[:, :, 0, 0:CONV - 1], xc[:, :, 0, SEG:SEG + CONV - 1]), "halo_ready")
                need(dve, "th_ready", ch)
                st.do(stt(sig[:, 0:2, :], sig[:, 0:2, :], 1.0,
                          pt[0:R, Q_GB:Q_GB + 2 * BW].rearrange("p (a n) -> p a n", a=2), A, M))
                st.do(stt(sig[:, 2, :], sig[:, 2, :], 1.0, pt[0:R, Q_CG:Q_CG + BW], A, M))
                st.do(ts(bet[:, :], bet[:, :], 1.0, 0.5, A, M))
                done(stt(sig[:, 3, :], sig[:, 3, :], 1.0, pt[0:R, Q_DG:Q_DG + BW], A, M), "sg_ready")
                need(dve, "sigc_ready", ch)
                done(stt(cvs, sig_c, 1.0, cvs, A, M), "cvs_ready")
                need(dve, "gcol_tm", ch)
                need(dve, "R_ps", ch)
                total = hv(c[3])[:, :, R - 1] if prompt else gcol[:, 1, :]
                done(tt(gcol[:, 1, :], total, gcol[:, 0, :], SUB), "gcol_ready")
                st.do(V.tensor_copy(eglB[:, :, :], hv(c[3], D).rearrange("d h (b t) -> d h b t", b=SEGS)
                                    [:, :, :, SEG - 1]))
                done(tt(dec[:, :, :], hv(c[3]), over(gcol[:, 0, :], [R, H, R]), SUB), "R_read")
                need(dve, "R_read", ch)
                done(tt(dec[:, :, :], dec[:, :, :], per_head(neg), A), "dec_in")
                need(dve, "qkv_tm", ch)
                st.do(tt(sq[:, :, :], qk[:, :, :], qk[:, :, :], M))
                st.sync()
                done(V.tensor_reduce(ss8[:, :], sq[:, :, :], AX_X, A), "ss_ready")
                need(dve, "qcT_ps", ch)
                st.do(ts(qcT[:, 0:H:2, :], odd_heads(c[3], 0), 0.5, None, M))
                done(ts(qcT[:, 1:H:2, :], odd_heads(c[3], 1), 0.5, None, M), "qcT_ready")
                need(dve, "kcT_ps", ch)
                st.do(V.tensor_copy(kcT[:, 0:H:2, :], odd_heads(c[4], 0)))
                done(V.tensor_copy(kcT[:, 1:H:2, :], odd_heads(c[4], 1)), "kcT_ready")
                need(dve, "rn_ready", ch)
                st.do(ts(ss8[:, 0:4], ss8[:, 0:4], D ** -0.5, None, M))
                st.sync()
                done(tt(qk[:, :, :], qk[:, :, :], over(ss8[:, :], [R, 8, D]), M), "qk_normed")
                need(dve, "qk_normed", ch)
                done(tt(kb[:, :, :], qk[:, 4:8, :], over(bet[:, :], [R, H, D]), M), "kb_ready")
                need(dve, "ecol_ready", ch)
                done(tt(qg[:, :, :], qk[:, 0:4, :], over(gcol[:, 0, :], [R, H, D]), M), "qg_ready")
                need(dve, "poolw_ps", ch)
                free(dve, "y_out", ch)
                need(dve, "pscaled_ready", ch)
                done(tt(y[:, 2 * BW:], c[2][0:R, 0:BW], sig[:, 3, :], M), "yD_ready")
                need(dve, "cprod_ps", ch, 1)
                free(dve, "oC_ps", ch)
                done(tt(acc[:, :, :], hv(c[4]), per_head(ident[0:R, 0:R]), M), "cacc_ready")
                decay_rows(ch, 0)
                need(dve, "qnT_ps", ch)
                st.do(V.tensor_copy(qnT[:, 0:H:2, :], odd_heads(c[2], 0)))
                done(V.tensor_copy(qnT[:, 1:H:2, :], odd_heads(c[2], 1)), "qnT_ready")
                need(dve, "kk_ps", ch)
                need(dve, "dec_ready", ch)
                done(tt(At[:, :, :], hv(c[0]), dec[:, :, :], M), "At_ready")
                need(dve, "kq_ps", ch)
                done(tt(QKt[:, :, :], hv(c[1]), dec[:, :, :], M), "QKt_ready")
                for k in range(NL):
                    if k >= 2:
                        need(dve, "Xt_ps", ch, k - 1)
                        done(V.tensor_copy(Y[:, :, :], hv(c[2])), "Y_ready")
                    need(dve, "cprod_ps", ch, k + 2)
                    if k:
                        need(dve, "cacc_ready", ch, k + 1)
                    done(tt(tmp[:, :, :], hv(c[4]), per_head(level[k]), M), "tmp_ready")
                    if k + 1 < NL:
                        decay_rows(ch, k + 1)
                    if k == 0:
                        need(dve, "am_ready", ch, 1)
                        done(tt(Y[:, :, :], per_head(ident[0:R, 0:R]), Am[0][:, :, :], SUB), "Y_ready")
                        need(dve, "z_ps", ch, 1)
                        done(tt(X[:, :, :], per_head(ident[0:R, 0:R]), hv(c[0]), SUB), "X_ready")
                    elif k < NL - 1:
                        need(dve, "xz_ps", ch, k)
                        need(dve, "X_ready", ch, k)
                        done(tt(X[:, :, :], X[:, :, :], hv(c[1]), SUB), "X_ready")
                    else:
                        need(dve, "zy_ps", ch)
                        need(dve, "Y_ready", ch, k)
                        done(tt(Y[:, :, :], Y[:, :, :], hv(c[2]), SUB), "Y_ready")
                    if k == 3 and nm:
                        xn_rows(nm)
                need(dve, "EL_ready", ch)
                done(tt(kgT[:, :, :], kgT[:, :, :], kcT[:, :, :], M), "kgT_ready")
                if not prompt:
                    for b in range(SEGS):
                        ins = ts(vCx[:, :, b, :], vC[:, :, :], segm[:, b:b + 1], None, M)
                        if b < SEGS - 1:
                            st.do(ins)
                        else:
                            done(ins, "vCx_ready")
                need(dve, "vn_ps", ch)
                for h in range(H if not prompt else 1):
                    out, e, q = (own_columns(qcgx), EG, qcT) if prompt else \
                        (own_columns(qcgx)[:, h], fm(EG[:, :, :])[:, h], fm(qcT[:, :, :])[:, h])
                    ins = tt(out, e[:, :, :], q[:, :, :], M)
                    if prompt or h == H - 1:
                        done(ins, "qcg_ready")
                    else:
                        st.do(ins)
                if not prompt:
                    need(dve, "vn_ready", ch)
                    for b in range(SEGS):
                        ins = ts(vBx[:, :, b, :], vn[:, :, :], segm[:, b:b + 1], None, M)
                        if b < SEGS - 1:
                            st.do(ins)
                        else:
                            done(ins, "vBx_ready")
                for state, egl, read, inc, banks, name in (
                        (SB, eglB, "oB_ps", "dSB_ps", (3, 4, 0, 1), "SB_ready"),
                        (SC, eglC, "oC_ps", "dSC_ps", (0, 1, 3, 4), "SC_ready")):
                    need(dve, read, ch)
                    flat = state[:, :, :, :].rearrange("k h b v -> k (h b) v")
                    st.do(tt(flat, flat, over(egl[:, :, :].rearrange("k h b -> k (h b)"),
                                              [D, H * SEGS, D]), M))
                    st.sync()
                    need(dve, inc, ch)
                    if prompt:
                        done(tt(flat, flat, hv(c[banks[0]], D, D), A), name)
                    else:
                        for h in range(H):
                            ins = tt(state[:, h, :, :], state[:, h, :, :],
                                     c[banks[h]][0:D, :].rearrange("k (b v) -> k b v", b=SEGS), A)
                            if h < H - 1:
                                st.do(ins)
                            else:
                                done(ins, name)
                need(dve, "oB_tm", ch)
                need(dve, "oC_tm", ch)
                st.do(tt(sq[:, :, :], oBC[:, :, :], oBC[:, :, :], M))
                st.sync()
                done(V.tensor_reduce(ss8[:, :], sq[:, :, :], AX_X, A), "ss2_ready")
                if nm:
                    hT_rows(nm)
                need(dve, "rn2_ready", ch)
                st.do(tt(oBC[:, :, :], oBC[:, :, :], over(ss8[:, :], [R, 8, D]), M))
                st.sync()
                need(dve, "gates_ready", ch)
                st.do(tt(y[:, 0:BW], oBC[:, 0:4, :].rearrange("p h d -> p (h d)"), sig[:, 0, :], M))
                done(tt(y[:, BW:2 * BW], oBC[:, 4:8, :].rearrange("p h d -> p (h d)"), sig[:, 2, :], M),
                     "y_ready")

            run(dve, iteration)

        @block.gpsimd
        def _(pool):
            V = nc.gpsimd
            tt = V.tensor_tensor
            M, ADD, SUB = ALU.mult, ALU.add, ALU.subtract
            st = Steps(own_steps["pool"], pool)
            pool.wait_ge(setup, n_setup)

            def iteration(pr, ch, nm):
                if ch:
                    st.begin(ch)
                    mix(ch)
                    st.end()

            def over(ap, shape):
                return ap.unsqueeze(len(ap.shape)).broadcast_to(shape)

            def coupling(ch, k):
                if k >= 2:
                    need(pool, "z_ps", ch, k - 1)
                    need(pool, "Y_ready", ch, 1)
                done(tt(Am[k % 2][:, :, :], At[:, :, :],
                        level[k].unsqueeze(1).broadcast_to([R, H, R]), M), "am_ready")

            def mix(ch):
                need(pool, "sg_ready", ch)
                done(tt(sig[:, 3, :], sig[:, 3, :], pscale[0:R, :], M), "pscaled_ready")
                st.do(tt(sig[:, 0, :], sig[:, 0, :], gatew[0:R, 0:BW], M))
                done(tt(sig[:, 2, :], sig[:, 2, :], gatew[0:R, BW:], M), "gates_ready")
                if prompt:
                    pool.wait_ge(setup, n_setup)
                    need(pool, "pool_ps", ch)
                    done(V.tensor_copy(xdp[:, :], xd[:, :]), "xdp_ready")
                need(pool, "G_ready", ch)
                free(pool, "kg_ps", ch)
                g4 = G[:, :, :].rearrange("d h (b t) -> d (h b) t", b=SEGS)
                done(tt(kgT[:, :, :].rearrange("d h (b t) -> d (h b) t", b=SEGS),
                        g4[:, :, SEG - 1:SEG].broadcast_to([D, H * SEGS, SEG]), g4, SUB), "EL_in")

                def differences(k):
                    if k >= 2:
                        need(pool, "cprod_ps", ch, k)
                    g, m = halves(G, k), halves(Ml[k % 2], k)
                    n, s = H * R // 2 ** (k + 1), 2 ** k
                    edge = g[:, :, 0, s - 1:s].broadcast_to([D, n, s])
                    st.do(tt(m[:, :, 0, :], edge, g[:, :, 0, :], SUB))
                    done(tt(m[:, :, 1, :], g[:, :, 1, :], edge, SUB), "cd_ready")

                free(pool, "cprod_ps", ch)
                differences(0)
                differences(1)
                need(pool, "qkv_tm", ch)
                need(pool, "th_ready", ch)
                need(pool, "sg_ready", ch)
                free(pool, "dSB_ps", ch)
                st.do(tt(vb[:, :, :], vB[:, :, :], over(bet[:, :], [R, H, D]), M))
                need(pool, "ecol_ready", ch)
                need(pool, "kb_ready", ch)
                st.do(tt(kend[:, :, :], qk[:, 4:8, :], over(gcol[:, 1, :], [R, H, D]), M))
                done(tt(kbg[:, :, :], kb[:, :, :], over(gcol[:, 0, :], [R, H, D]), M), "scaled_ready")
                need(pool, "At_ready", ch)
                coupling(ch, 0)
                coupling(ch, 1)
                for k in range(NL):
                    if k + 2 < NL:
                        coupling(ch, k + 2)
                        differences(k + 2)
                    need(pool, "tmp_ready", ch, k + 1)
                    need(pool, "cacc_ready", ch, k + 1)
                    done(tt(acc[:, :, :], acc[:, :, :], tmp[:, :, :], ADD), "cacc_ready")
                need(pool, "y_ready", ch)
                pool.dma_start(rows_of(ch, io["y_rows"]), y[:, :]).then_inc(S["y_out"].sem, 16)

            run(pool, iteration)

        program.close()
        nc.clear_and_free_semaphores(sems)
        nc.all_engine_barrier()


def split_products(nc, out, lhs, rhs, k, cols, start, stop):
    passes = ((0, 0), (0, 1), (1, 0))
    for n, (a, b) in enumerate(passes):
        last = nc.tensor.matmul(out, lhs[a], rhs[b][:, k, cols], start=start and n == 0,
                                stop=stop and n == 2)
    return last


def project_attention(nc, io):
    with ExitStack() as ctx:
        sems = []

        def sb(name, shape, dtype=F32):
            return ctx.enter_context(nc.sbuf_tensor(f"a_{name}", shape, dtype))

        def semaphore(name):
            sems.append(ctx.enter_context(nc.semaphore(f"a_{name}")))
            return sems[-1]

        w = sb("w", [P, KD, AW])
        w_parts = [sb(f"w_{n}", [P, KD, AW], F32R) for n in ("high", "low")]
        ident, normw, eps = sb("ident", [P, P]), sb("normw", [P, KD]), sb("eps", [P, 1])
        xin, xn, hT = sb("xin", [P, DM]), sb("xn", [P, DM]), sb("hT", [P, KD, P])
        hT_parts = [sb(f"hT_{n}", [P, KD, P], F32R) for n in ("high", "low")]
        rstd = sb("rstd", [P, 2])
        rows = sb("rows", [P, AW])
        nt, pj = ([ctx.enter_context(nc.psum_tensor(f"a_{n}{k}", [P, 512], F32)) for k in range(2)]
                  for n in ("nt", "pj"))
        S = {n: Count(semaphore(n), per) for n, per in (
            ("x_in", 16), ("sq_ready", 1), ("ln_ready", 1), ("rstd_ready", 1), ("xn_ready", 1),
            ("ht_ps", 2), ("hT_ready", 2), ("high_ready", 2), ("low_ready", 2), ("half_used", 1),
            ("pj_ps", 2), ("rows_ready", 2), ("rows_out0", 16),
            ("rows_out1", 16))}
        loads, setup = semaphore("loads"), semaphore("setup")
        w_in = [semaphore(f"w_in{n}") for n in range(4)]
        w_high, w_low = semaphore("w_high"), semaphore("w_low")

        def need(eng, name, tile, k=None):
            S[name].wait(eng, tile, k)

        def free(eng, name, tile):
            S[name].wait(eng, tile, 0)

        def done(ins, name):
            ins.then_inc(S[name].sem, 1)

        def run(eng, iteration):
            own, tile = Tile(TS, 0, 0), lambda n: Tile(P, n + 1, n * P)
            iteration(None, own)
            iteration(own, tile(0))
            with eng.Fori(0, NT - 1) as i:
                iteration(tile(i), tile(i + 1))
            iteration(tile(NT - 1), None)

        program = ExitStack()
        block = program.enter_context(nc.Block())

        @block.sync
        def _(sp):
            sp.dma_start(ident[:, :], io["consts"][:, io["cols"]["ident"]:io["cols"]["ident"] + P])\
                .then_inc(loads, 16)
            sp.dma_start(normw[:, :], io["norm_w_fm"]).then_inc(loads, 16)
            sp.dma_start(xin[0:TS, :], io["x_s"]).then_inc(S["x_in"].sem, 16)
            win = io["w_in"][0].rearrange("(k p) n -> p k n", p=P)
            for n in range(4):
                ks = slice(2 * n, 2 * n + 2)
                sp.dma_start(w[:, ks, :], win[:, ks, 0:AW]).then_inc(w_in[n], 16)

            def iteration(pr, nm):
                if nm and not nm.sample:
                    free(sp, "xn_ready", nm)
                    sp.dma_start(xin[0:nm.rows, :], rows_of(nm, io["x_s" if nm.sample else "x_p"]))\
                        .then_inc(S["x_in"].sem, 16)

            every = NT // KD
            iteration(None, Tile(TS, 0, 0))
            iteration(Tile(TS, 0, 0), Tile(P, 1, 0))
            for k in range(KD):
                with sp.Fori(k * every, min((k + 1) * every, NT - 1)) as i:
                    iteration(Tile(P, i + 1, i * P), Tile(P, i + 2, (i + 1) * P))
                sp.dma_start(io["w_mix"][:, k, :], win[:, k, AW:AW + MW]).then_inc(io["w_mix_in"], 16)

        @block.gpsimd
        def _(pool):
            def iteration(pr, nm):
                if pr:
                    out = io["att_s"] if pr.sample else rows_of(pr, io["att_rows"])
                    for g in range(2):
                        need(pool, "rows_ready", pr, g + 1)
                        cols = slice(512 * g, 512 * g + 512)
                        pool.dma_start(out[:, cols], rows[0:pr.rows, cols])\
                            .then_inc(S[f"rows_out{g}"].sem, 16)

            run(pool, iteration)
            need(pool, "rows_out0", Tile(P, NT))
            need(pool, "rows_out1", Tile(P, NT))

        @block.tensor
        def _(pe):
            pe.wait_ge(loads, 32)

            def project(pr, half):
                need(pe, "low_ready", pr, half + 1)
                for g in range(2):
                    if half == 0 and not pr.sample:
                        pe.wait_ge(S["rows_ready"].sem, pr.t * 2 + (g - 1))
                    for k in range(4 * half, 4 * half + 4):
                        last = split_products(nc, pj[g][0:pr.rows, :], [t[:, k, 0:pr.rows] for t in hT_parts],
                                              w_parts, k, slice(512 * g, 512 * g + 512),
                                              start=(k == 0), stop=(k == KD - 1))
                    if half:
                        done(last, "pj_ps")
                return last

            def iteration(pr, nm):
                if pr:
                    if pr.sample:
                        pe.wait_ge(w_low, KD)
                    done(project(pr, 0), "half_used")
                if nm:
                    need(pe, "xn_ready", nm)
                    free(pe, "hT_ready", nm)
                    for half in range(2):
                        for k in range(4):
                            last = nc.tensor.transpose(
                                nt[half][:, k * nm.rows:(k + 1) * nm.rows],
                                xn[0:nm.rows, (4 * half + k) * P:(4 * half + k + 1) * P],
                                ident[0:nm.rows, 0:nm.rows])
                        done(last, "ht_ps")
                if pr:
                    project(pr, 1)

            run(pe, iteration)

        @block.scalar
        def _(act):
            nc.scalar.preload_act_table_set("natural_log_exp_and_others")
            act.wait_ge(setup, 1)

            def high(nm, half):
                r = nm.rows
                ks = slice(4 * half, 4 * half + 4)
                need(act, "hT_ready", nm, half + 1)
                free(act, "pj_ps" if half else "half_used", nm)
                done(nc.scalar.activation(hT_parts[0][:, ks, 0:r], hT[:, ks, 0:r], ACT.Copy), "high_ready")

            def iteration(pr, nm):
                if nm:
                    r = nm.rows
                    need(act, "x_in", nm)
                    free(act, "ht_ps", nm)
                    done(nc.scalar.activation(xn[0:r, :], xin[0:r, :], ACT.Square,
                                              accum_out=rstd[0:r, 0:1]), "sq_ready")
                    need(act, "sq_ready", nm)
                    done(nc.scalar.activation(rstd[0:r, 1:2], rstd[0:r, 0:1], ACT.Ln, scale=1.0 / DM,
                                              bias=eps[0:r, :]), "ln_ready")
                    need(act, "ln_ready", nm)
                    done(nc.scalar.activation(rstd[0:r, 0:1], rstd[0:r, 1:2], ACT.Exp, scale=-0.5),
                         "rstd_ready")
                if nm and nm.sample:
                    for k in range(KD):
                        if k % 2 == 0:
                            act.wait_ge(w_in[k // 2], 16)
                        nc.scalar.activation(w_parts[0][:, k, :], w[:, k, :], ACT.Copy).then_inc(w_high, 1)
                if nm:
                    high(nm, 0)
                if pr:
                    for g in range(2):
                        free(act, f"rows_out{g}", pr)
                        need(act, "pj_ps", pr, g + 1)
                        cols = slice(512 * g, 512 * g + 512)
                        done(nc.scalar.activation(rows[0:pr.rows, cols], pj[g][0:pr.rows, :], ACT.Copy),
                             "rows_ready")
                if nm:
                    high(nm, 1)

            run(act, iteration)

        @block.vector
        def _(dve):
            nc.vector.memset(eps[:, :], EPS).then_inc(setup, 1)
            dve.wait_ge(loads, 32)

            def iteration(pr, nm):
                if nm and nm.sample:
                    normalise(nm)
                    for k in range(KD):
                        dve.wait_ge(w_high, k + 1)
                        nc.vector.tensor_tensor(w_parts[1][:, k, :], w[:, k, :], w_parts[0][:, k, :],
                                                ALU.subtract).then_inc(w_low, 1)
                if nm:
                    if not nm.sample:
                        normalise(nm)
                    r = nm.rows
                    for half in range(2):
                        need(dve, "ht_ps", nm, half + 1)
                        ks = slice(4 * half, 4 * half + 4)
                        free(dve, "low_ready", nm)
                        done(nc.vector.tensor_tensor(
                            hT[:, ks, 0:r], nt[half][:, 0:4 * r].rearrange("p (k t) -> p k t", k=4),
                            normw[:, ks].unsqueeze(2).broadcast_to([P, 4, r]), ALU.mult), "hT_ready")
                        need(dve, "high_ready", nm, half + 1)
                        done(nc.vector.tensor_tensor(hT_parts[1][:, ks, 0:r], hT[:, ks, 0:r],
                                                     hT_parts[0][:, ks, 0:r], ALU.subtract), "low_ready")

            def normalise(nm):
                r = nm.rows
                need(dve, "rstd_ready", nm)
                done(nc.vector.tensor_scalar(xn[0:r, :], xin[0:r, :], rstd[0:r, 0:1], None, ALU.mult),
                     "xn_ready")

            run(dve, iteration)

        program.close()
        nc.clear_and_free_semaphores(sems)
        nc.all_engine_barrier()


PATTERNS = ((128, 1), (512, 4), (2048, 16))
DILATIONS = (16, 4, 1)
SLOPES = [2.0 ** (-8.0 * (h + 1) / H) for h in range(H)]
PART = BW + 2 * H
OCTET = 8


def alibi_constants(dil, first):
    q, k = np.arange(P)[:, None], np.arange(P)[None, :]
    out = []
    for slope in SLOPES:
        own = np.where(q >= k, -slope * dil * (q - k), NEG)
        prev = np.where((q <= k) & (not first), -slope * dil * (q + P - k), NEG)
        out.append(np.concatenate([prev, own, prev], axis=1))
    return np.concatenate(out, axis=1).astype(np.float32)


def attend_classes(nc, io):
    BLOCKS = SEQ // P
    with ExitStack() as ctx:
        sems = []

        def sb(name, shape, dtype=F32):
            return ctx.enter_context(nc.sbuf_tensor(f"c_{name}", shape, dtype))

        def semaphore(name):
            sems.append(ctx.enter_context(nc.semaphore(f"c_{name}")))
            return sems[-1]

        def bank(name):
            return ctx.enter_context(nc.psum_tensor(f"c_{name}", [P, 512], F32))

        ident = sb("ident", [P, P])
        bias = {(d, f): sb(f"bias{d}_{f}", [P, H, 3 * P]) for d in DILATIONS for f in (0, 1)}
        rows = sb("rows", [P, OCTET, 3 * BW])
        qT = [sb(f"qT_{n}", [P, 2, 2, P], F32R) for n in ("high", "low")]
        kT = [sb(f"kT_{n}", [P, 2, 2, P], F32R) for n in ("high", "low")]
        sc = sb("sc", [P, 4, H, 2 * P])
        mx = sb("mx", [P, 4, H])
        PT = sb("PT", [P, 2, H * 2, P])
        res = sb("res", [P, OCTET, PART])
        tq, tk, o_ps = bank("tq"), bank("tk"), bank("o")
        s_ps, pt_ps = [bank("s0"), bank("s1")], [bank("p0"), bank("p1")]

        S = {n: Count(semaphore(n), per) for n, per in (
            ("q_ps", 1), ("k_ps", 1), ("q_high", 1), ("q_low", 1), ("k_high", 1), ("k_low", 1),
            ("s_done", 1),
            ("biased", 2), ("max_ready", 1), ("neg_ready", 1), ("exp_ready", 4), ("p_ps", 2),
            ("PT_ready", 2), ("o_done", 1), ("res_ready", 1))}
        loads, kT_zero = semaphore("loads"), semaphore("kT_zero")
        passed = {nc.tensor: semaphore("pe_passed"), nc.sync: semaphore("sp_passed")}
        n_loads = 7
        rows_in = [semaphore(f"rows_in{n}") for n in range(OCTET)]
        res_out = [semaphore(f"res_out{n}") for n in range(OCTET)]

        class At:

            def __init__(self, o, n):
                self.t, self.octet, self.n = o * OCTET + n, o + n // OCTET, n % OCTET

        def need(eng, name, b, k=None):
            S[name].wait(eng, b, k)

        def ago(eng, name, b, blocks):
            per = S[name].per
            if isinstance(b.t, int) and b.t < blocks:
                return
            eng.wait_ge(S[name].sem, b.t * per + per * (1 - blocks))

        def stored(eng, b):
            if isinstance(b.t, int) and b.t < OCTET:
                return
            eng.wait_ge(res_out[b.n], b.octet * 16)

        def apart(eng):
            eng.sem_inc(passed[eng], 1)

        def done(ins, name):
            ins.then_inc(S[name].sem, 1)

        def run(eng, step, by_dilation=False, lag=0):

            def octet(o, d, peeled=None):
                for n in range(OCTET):
                    first = (n % 2 == 0) if d == 16 else (n == 0 if d == 4 else peeled == 8 and n == 0)
                    step(o, n, d, first)
            octet(0, 16, 0)
            if by_dilation:
                with eng.Fori(1, 4) as o:
                    octet(o, 16)
                with eng.Fori(4, 8) as o:
                    octet(o, 4)
                octet(8, 1, 8)
                with eng.Fori(9, 11) as o:
                    octet(o, 1)
                octet(11, 1, 11)
            else:
                with eng.Fori(1, 12) as o:
                    octet(o, None)
            for n in range(lag):
                step(NOCT, n, None, False)

        NOCT = 3 * BLOCKS // OCTET

        def live(o, n, k=0):
            return not isinstance(o, int) or 0 <= o * OCTET + n - k < 3 * BLOCKS

        def row(d, o, n):
            if d == 16:
                return o * 4 + (n // 2 + (n % 2) * P * 16)
            if d == 4:
                return (o - 4) + n * P * 4
            return (o - 8) * (OCTET * P) + n * P

        def dram_rows(dram, d, o, n):
            r = row(d, o, n)
            if isinstance(r, int):
                return dram[r:r + (P - 1) * d + 1:d, :]
            return dram[bass.ds(r, P, step=d), :]

        program = ExitStack()
        block = program.enter_context(nc.Block())

        @block.sync
        def _(sp):
            sp.dma_start(ident[:, :], io["consts"][:, io["cols"]["ident"]:io["cols"]["ident"] + P])\
                .then_inc(loads, 16)
            for (d, f), buf in sorted(bias.items()):
                at = io["cols"][f"alibi_{d}_{f}"]
                sp.dma_start(buf[:, :, :].rearrange("p h k -> p (h k)"),
                             io["consts"][:, at:at + H * 3 * P]).then_inc(loads, 16)

            sp.wait_ge(kT_zero, 3)

            def step(o, n, d, first):
                b = At(o, n)
                ago(sp, "o_done", b, OCTET - 1)
                apart(sp)
                sp.dma_start(rows[:, n, :], dram_rows(io["att_rows"][:, 0:3 * BW], d, o, n))\
                    .then_inc(rows_in[n], 16)

            run(sp, step, by_dilation=True)

        @block.tensor
        def _(pe):
            pe.wait_ge(loads, 16 * n_loads)

            def step(o, n, d, first):
                if live(o, n):
                    b = At(o, n)
                    pe.wait_ge(rows_in[b.n], b.octet * 16 + 16)
                    ago(pe, "q_low", b, 1)
                    apart(pe)
                    for pair in range(2):
                        last = nc.tensor.transpose(tq[:, pair * P:(pair + 1) * P],
                                                   rows[:, b.n, pair * P:(pair + 1) * P], ident[:, :])
                    done(last, "q_ps")
                    ago(pe, "k_low", b, 1)
                    apart(pe)
                    for pair in range(2):
                        last = nc.tensor.transpose(tk[:, pair * P:(pair + 1) * P],
                                                   rows[:, b.n, BW + pair * P:BW + (pair + 1) * P],
                                                   ident[:, :])
                    done(last, "k_ps")
                if live(o, n, 4):
                    b = At(o, n - 4)
                    for half in range(2):
                        need(pe, "exp_ready", b)
                        ago(pe, "PT_ready", b, 1)
                        apart(pe)
                        for k in range(4):
                            h, s = 2 * half + k // 2, k % 2
                            last = nc.tensor.transpose(pt_ps[half][:, k * P:(k + 1) * P],
                                                       sc[:, b.n % 4, h, s * P:(s + 1) * P], ident[:, :])
                        done(last, "p_ps")
                if live(o, n, 1):
                    b = At(o, n - 1)
                    need(pe, "k_low", b)
                    need(pe, "q_low", b)
                    ago(pe, "biased", b, 1)
                    for h in (0, 2, 1, 3):
                        d = slice((h % 2) * D, (h % 2 + 1) * D)
                        for n_pass, (x, y) in enumerate(((0, 0), (0, 1), (1, 0))):
                            last = nc.tensor.matmul(s_ps[h % 2][:, (h // 2) * 2 * P:(h // 2 + 1) * 2 * P],
                                                    qT[x][d, b.n % 2, h // 2, :],
                                                    kT[y][d, h // 2, :, :].rearrange("d s k -> d (s k)"),
                                                    start=(n_pass == 0), stop=(n_pass == 2))
                    done(last, "s_done")
                if live(o, n, 5):
                    b = At(o, n - 5)
                    need(pe, "PT_ready", b)
                    ago(pe, "res_ready", b, 1)
                    for h in range(H):
                        for s in range(2):
                            v = rows[:, b.n if s == b.n % 2 else (b.n - 1) % OCTET,
                                     2 * BW + h * D:2 * BW + (h + 1) * D]
                            last = nc.tensor.matmul(o_ps[:, h * D:(h + 1) * D], PT[:, b.n % 2, 2 * h + s, :],
                                                    v, start=(s == 0), stop=(s == 1))
                    done(last, "o_done")

            run(pe, step, lag=5)

        @block.scalar
        def _(act):
            act.wait_ge(kT_zero, 3)

            def step(o, n, d, first):
                if live(o, n):
                    b = At(o, n)
                    need(act, "q_ps", b)
                    ago(act, "s_done", b, 2)
                    done(nc.scalar.activation(qT[0][:, b.n % 2, :, :],
                                              tq[:, 0:2 * P].rearrange("d (h t) -> d h t", h=2), ACT.Copy,
                                              scale=D ** -0.5), "q_high")
                if live(o, n, 4):
                    b = At(o, n - 4)
                    need(act, "p_ps", b, 1)
                    ago(act, "o_done", b, 2)
                    done(nc.scalar.activation(PT[:, b.n % 2, 0:4, :],
                                              pt_ps[0][:, :].rearrange("p (k t) -> p k t", k=4), ACT.Copy),
                         "PT_ready")
                if live(o, n, 6):
                    b = At(o, n - 6)
                    need(act, "o_done", b)
                    done(nc.scalar.activation(res[:, b.n, 0:BW], o_ps[:, 0:BW], ACT.Copy), "res_ready")
                if live(o, n):
                    b = At(o, n)
                    need(act, "k_ps", b)
                    ago(act, "s_done", b, 1)
                    done(nc.scalar.activation(kT[0][:, :, b.n % 2, :],
                                              tk[:, 0:2 * P].rearrange("d (h t) -> d h t", h=2), ACT.Copy),
                         "k_high")
                if live(o, n, 2):
                    b = At(o, n - 2)
                    need(act, "neg_ready", b)
                    stored(act, b)
                    for h in range(H):
                        done(nc.scalar.activation(sc[:, b.n % 4, h, :], sc[:, b.n % 4, h, :], ACT.Exp,
                                                  bias=mx[:, b.n % 4, h:h + 1],
                                                  accum_out=res[:, b.n, BW + h:BW + h + 1]), "exp_ready")

            run(act, step, lag=6)

        @block.vector
        def _(dve):
            for part in kT:
                nc.vector.memset(part[:, :, :, :].bitcast(F32), 0.0).then_inc(kT_zero, 1)
            nc.vector.memset(rows[:, OCTET - 1, 2 * BW:], 0.0).then_inc(kT_zero, 1)
            dve.wait_ge(kT_zero, 3)
            dve.wait_ge(loads, 16 * n_loads)

            def biased(o, n, d, first, odd):
                b = At(o, n)
                need(dve, "s_done", b)
                ago(dve, "p_ps", b, 4)
                stored(dve, b)
                cols = slice(P, 3 * P) if b.n % 2 == 0 else slice(0, 2 * P)
                table = bias[d, int(first)]
                hs = slice(odd, H, 2)
                done(nc.vector.tensor_tensor(
                    sc[:, b.n % 4, hs, :], s_ps[odd][:, :].rearrange("p (h k) -> p h k", h=2),
                    table[:, hs, cols], ALU.add), "biased")

            def maxima(o, n):
                b = At(o, n)
                need(dve, "biased", b)
                done(nc.vector.tensor_reduce(res[:, b.n, BW + H:], sc[:, b.n % 4, :, :], AX_X, ALU.max),
                     "max_ready")
                need(dve, "max_ready", b)
                ago(dve, "exp_ready", b, 4)
                done(nc.vector.tensor_scalar(mx[:, b.n % 4, :], res[:, b.n, BW + H:], -1.0, None,
                                             ALU.mult), "neg_ready")

            def low_queries(o, n):
                b = At(o, n)
                need(dve, "q_high", b)
                ago(dve, "s_done", b, 2)
                done(nc.vector.scalar_tensor_tensor(
                    qT[1][:, b.n % 2, :, :], tq[:, 0:2 * P].rearrange("d (h t) -> d h t", h=2), D ** -0.5,
                    qT[0][:, b.n % 2, :, :], ALU.mult, ALU.subtract), "q_low")

            def low_keys(o, n):
                b = At(o, n)
                need(dve, "k_high", b)
                ago(dve, "s_done", b, 1)
                done(nc.vector.tensor_tensor(
                    kT[1][:, :, b.n % 2, :], tk[:, 0:2 * P].rearrange("d (h t) -> d h t", h=2),
                    kT[0][:, :, b.n % 2, :], ALU.subtract), "k_low")

            def probabilities(o, n):
                b = At(o, n)
                need(dve, "p_ps", b)
                ago(dve, "o_done", b, 2)
                done(nc.vector.tensor_copy(PT[:, b.n % 2, 4:8, :],
                                           pt_ps[1][:, :].rearrange("p (k t) -> p k t", k=4)), "PT_ready")

            def step(o, n, d, first):
                if live(o, n + 1):
                    low_queries(o, n + 1)
                if live(o, n, 3):
                    probabilities(o, n - 3)
                if live(o, n):
                    biased(o, n, d, first, 0)
                if live(o, n + 1):
                    low_keys(o, n + 1)
                if live(o, n):
                    biased(o, n, d, first, 1)
                    maxima(o, n)

            low_queries(0, 0)
            low_keys(0, 0)
            run(dve, step, by_dilation=True, lag=3)

        @block.gpsimd
        def _(pool):
            def step(o, n, d, first):
                b = At(o, n)
                need(pool, "res_ready", b)
                part = DILATIONS.index(d)
                pool.dma_start(dram_rows(io["parts"][part], d, o, n), res[:, b.n, :])\
                    .then_inc(res_out[n], 16)

            run(pool, step, by_dilation=True)
            for sem in res_out:
                pool.wait_ge(sem, 16 * NOCT)

        program.close()
        nc.clear_and_free_semaphores(sems)
        nc.all_engine_barrier()


BUF = 2048
NEAR = 512
STEP, USED = 16, DS
FAR_TILES = (BUF - NEAR) // STEP * USED // P
CACHE_TILES = FAR_TILES + NEAR // P
KEYS = CACHE_TILES * P + DS
GROUP = 4


def cache_constants():
    pos = []
    for f in range(FAR_TILES):
        p = np.arange(P)
        pos.append((f * (P // USED) + p // USED) * STEP + p % USED)
    pos.append(np.arange(BUF - NEAR, BUF + DS))
    pos = np.concatenate(pos)
    rows = np.arange(P)
    head, new = (rows // DS) % H, rows % DS
    dist = BUF + new[:, None] - pos[None, :]
    times = sum(((dist >= 0) & (dist <= win) & (dist % dil == 0)).astype(np.float64)
                for win, dil in PATTERNS)
    slope = np.array(SLOPES)[head][:, None]
    bias = np.where(times > 0, -slope * dist + np.log(np.maximum(times, 1.0)), NEG)
    of_head = head[:, None] == np.arange(H)[None, :]
    return np.concatenate([bias, of_head], axis=1).astype(np.float32)


def attend_cache(nc, io):
    SPANS = ((0, 512), (512, 512), (1024, KEYS - 1024))
    NT_ALL = CACHE_TILES + 1
    with ExitStack() as ctx:
        sems = []

        def sb(name, shape):
            return ctx.enter_context(nc.sbuf_tensor(f"s_{name}", shape, F32))

        def semaphore(name):
            sems.append(ctx.enter_context(nc.semaphore(f"s_{name}")))
            return sems[-1]

        def bank(name):
            return ctx.enter_context(nc.psum_tensor(f"s_ps_{name}", [P, 512], F32))

        ident = sb("ident", [P, P])
        table = sb("table", [P, KEYS + H])
        new = sb("new", [DS, 2, DB, BW])
        q = sb("q", [TS, BW])
        k_buf = sb("k", [P, 3, CACHE_TILES, BW])
        v_buf = sb("v", [P, 5, CACHE_TILES, BW])
        qbd = sb("qbd", [P, 2, DB, H, DS])
        kT = sb("kT", [P, 2, KEYS])
        sc = sb("sc", [P, KEYS])
        mx = sb("mx", [P, 2])
        den = sb("den", [P, 2])
        PT = sb("PT", [P, NT_ALL, P])
        o = sb("o", [P, D])
        tr = [bank(f"t{n}") for n in range(4)]
        s_ps = [bank(f"s{n}") for n in range(3)]
        o_ps = bank("o")

        loads, zero = semaphore("loads"), semaphore("zero")
        k_in = [semaphore(f"k_in{n}") for n in range(3)]
        v_in = [semaphore(f"v_in{n}") for n in range(5)]
        names = """q_ps qbd_ready tr_ps tr_read s_done biased max_ready neg_ready exp_ready p_ps pt_read
            v_done den_ready o_ready o_part o_out pt_part""".split()
        S = {n: semaphore(n) for n in names}
        KSETS = 6
        PSETS = 3

        program = ExitStack()
        block = program.enter_context(nc.Block())

        @block.sync
        def _(sp):
            at = io["cols"]["cache"]
            for dst, src in ((ident[:, :], io["consts"][:, io["cols"]["ident"]:io["cols"]["ident"] + P]),
                             (q[:, :], io["att_s"][:, 0:BW]),
                             (new[:, 0], io["att_s"][:, BW:2 * BW].rearrange("(b i) n -> i b n", i=DS)),
                             (new[:, 1], io["att_s"][:, 2 * BW:3 * BW].rearrange("(b i) n -> i b n", i=DS)),
                             (table[:, :], io["consts"][:, at:at + KEYS + H])):
                sp.dma_start(dst, src).then_inc(loads, 16)

            def cache(dst, src, sem):
                old = src[0:BUF - NEAR, :].rearrange("(f m s) n -> f m s n", f=FAR_TILES, s=STEP)
                for f in range(FAR_TILES):
                    sp.dma_start(dst[:, f, :], old[f, :, 0:USED, :]).then_inc(sem, 16)
                sp.dma_start(dst[:, FAR_TILES:, :], src[BUF - NEAR:, :].rearrange("(j p) n -> p j n", p=P))\
                    .then_inc(sem, 16)

            for b in range(DB):
                if b >= 3:
                    sp.wait_ge(S["tr_ps"], (b - 2) * KSETS)
                cache(k_buf[:, b % 3], io["cache_k"][0, b].rearrange("t h d -> t (h d)"), k_in[b % 3])
                if b >= 5:
                    sp.wait_ge(S["v_done"], b - 4)
                cache(v_buf[:, b % 5], io["cache_v"][0, b].rearrange("t h d -> t (h d)"), v_in[b % 5])
            for n in range(4):
                ks = slice(2 * n, 2 * n + 2)
                sp.dma_start(io["wo"][:, ks, :], io["w_out"][0].rearrange("(k p) n -> p k n", p=P)[:, ks, :])\
                    .then_inc(io["wo_in"], 16)

        @block.tensor
        def _(pe):
            pe.wait_ge(loads, 80)
            for half in range(2):
                last = nc.tensor.transpose(o_ps[:, half * TS:(half + 1) * TS], q[:, half * P:(half + 1) * P],
                                           ident[0:TS, 0:TS])
            last.then_inc(S["q_ps"], 1)
            pe.wait_ge(S["qbd_ready"], 4)
            for b in range(DB):
                g, bb = divmod(b, GROUP)
                pe.wait_ge(k_in[b % 3], 16 * (FAR_TILES + 1) * (b // 3 + 1))
                for n in range(KSETS):
                    if b * KSETS + n >= 4:
                        pe.wait_ge(S["tr_read"], b * KSETS + n - 3)
                    half, t0 = n // 3, (n % 3) * 4
                    out = tr[(b * KSETS + n) % 4]
                    cols = slice(half * P, (half + 1) * P)
                    for t in range(t0, min(t0 + 4, NT_ALL)):
                        if t < CACHE_TILES:
                            last = nc.tensor.transpose(out[:, (t - t0) * P:(t - t0 + 1) * P],
                                                       k_buf[:, b % 3, t, cols], ident[:, :])
                        else:
                            last = nc.tensor.transpose(out[:, (t - t0) * P:(t - t0) * P + DS],
                                                       new[:, 0, b, cols], ident[0:DS, 0:DS])
                    last.then_inc(S["tr_ps"], 1)
                pe.wait_ge(S["tr_read"], (b + 1) * KSETS)
                for n, (k0, nk) in enumerate(SPANS):
                    for half in range(2):
                        last = nc.tensor.matmul(s_ps[n][32 * bb:32 * bb + 32, 0:nk],
                                                qbd[:, half, b].rearrange("p h i -> p (h i)"),
                                                kT[:, half, k0:k0 + nk], start=(half == 0), stop=(half == 1))
                last.then_inc(S["s_done"], 1)
                if bb < GROUP - 1:
                    continue
                pe.wait_ge(S["exp_ready"], g + 1)
                for n in range(PSETS):
                    out = s_ps[n]
                    for t in range(4 * n, min(4 * n + 4, NT_ALL)):
                        nk = P if t < CACHE_TILES else DS
                        last = nc.tensor.transpose(out[0:nk, (t % 4) * P:(t % 4 + 1) * P],
                                                   sc[:, t * P:t * P + nk], ident[:, :])
                    last.then_inc(S["p_ps"], 1)
                pe.wait_ge(S["pt_read"], (g + 1) * PSETS)
                if g:
                    pe.wait_ge(S["o_ready"], g)
                for bb in range(GROUP):
                    bv = g * GROUP + bb
                    pe.wait_ge(v_in[bv % 5], 16 * (FAR_TILES + 1) * (bv // 5 + 1))
                    for t in range(NT_ALL):
                        nk = P if t < CACHE_TILES else DS
                        v = v_buf[:, bv % 5, t, :] if t < CACHE_TILES else new[:, 1, bv, :]
                        last = nc.tensor.matmul(o_ps[32 * bb:32 * bb + 32, 0:BW],
                                                PT[0:nk, t, 32 * bb:32 * bb + 32], v,
                                                start=(t == 0), stop=(t == NT_ALL - 1))
                    last.then_inc(S["v_done"], 1)

        def keys_to_sbuf(eng, b, n):
            half, k0 = n // 3, (n % 3) * 512
            nk = min(512, KEYS - k0)
            eng.wait_ge(S["tr_ps"], b * KSETS + n + 1)
            if b:
                eng.wait_ge(S["s_done"], b)
            if b * KSETS + n:
                eng.wait_ge(S["tr_read"], b * KSETS + n)
            out, src = kT[:, half, k0:k0 + nk], tr[(b * KSETS + n) % 4][:, 0:nk]
            ins = (nc.vector.tensor_copy(out, src) if n % 2 else nc.scalar.activation(out, src, ACT.Copy))
            ins.then_inc(S["tr_read"], 1)

        @block.scalar
        def _(act):
            for b in range(DB):
                g, bb = divmod(b, GROUP)
                for n in range(0, KSETS, 2):
                    keys_to_sbuf(act, b, n)
                if bb < GROUP - 1:
                    continue
                act.wait_ge(S["neg_ready"], g + 1)
                nc.scalar.activation(sc[:, :], sc[:, :], ACT.Exp, bias=mx[:, 1:2],
                                     accum_out=den[:, 0:1]).then_inc(S["exp_ready"], 1)

        @block.vector
        def _(dve):
            V, M = nc.vector, ALU.mult
            V.memset(qbd[:, :, :, :, :], 0.0).then_inc(zero, 1)
            dve.wait_ge(zero, 1)
            dve.wait_ge(S["q_ps"], 1)
            for half in range(2):
                for low in range(2):
                    part = slice(64 * low, 64 * low + 64)
                    V.tensor_scalar(qbd[part, half, :, 2 * half + low, :],
                                    o_ps[part, half * TS:(half + 1) * TS].rearrange("p (b i) -> p b i", i=DS),
                                    D ** -0.5, None, M).then_inc(S["qbd_ready"], 1)
            dve.wait_ge(loads, 80)
            for b in range(DB):
                g, bb = divmod(b, GROUP)
                for n in range(1, KSETS, 2):
                    keys_to_sbuf(dve, b, n)
                if bb < GROUP - 1:
                    continue
                dve.wait_ge(S["s_done"], b + 1)
                if g:
                    dve.wait_ge(S["p_ps"], g * PSETS)
                for n, (k0, nk) in enumerate(SPANS):
                    V.tensor_tensor(sc[:, k0:k0 + nk], s_ps[n][:, 0:nk], table[:, k0:k0 + nk], ALU.add)\
                        .then_inc(S["biased"], 1)
                dve.wait_ge(S["biased"], 3 * (g + 1))
                V.tensor_reduce(mx[:, 0:1], sc[:, :], AX_X, ALU.max).then_inc(S["max_ready"], 1)
                dve.wait_ge(S["max_ready"], g + 1)
                V.tensor_scalar(mx[:, 1:2], mx[:, 0:1], -1.0, None, M).then_inc(S["neg_ready"], 1)
                if g:
                    dve.wait_ge(S["v_done"], g * GROUP)
                for n in range(PSETS):
                    dve.wait_ge(S["p_ps"], g * PSETS + n + 1)
                    full = min(4, CACHE_TILES - 4 * n)
                    ins = V.tensor_copy(PT[:, 4 * n:4 * n + full, :],
                                        s_ps[n][:, 0:full * P].rearrange("p (t r) -> p t r", t=full))
                    if full < 4:
                        ins.then_inc(S["pt_part"], 1)
                        ins = V.tensor_copy(PT[0:DS, CACHE_TILES, :], s_ps[n][0:DS, full * P:(full + 1) * P])
                    ins.then_inc(S["pt_read"], 1)
                dve.wait_ge(S["exp_ready"], g + 1)
                V.reciprocal(den[:, 1:2], den[:, 0:1]).then_inc(S["den_ready"], 1)
                dve.wait_ge(S["v_done"], (g + 1) * GROUP)
                dve.wait_ge(S["den_ready"], g + 1)
                if g:
                    dve.wait_ge(S["o_out"], 16 * GROUP * g)
                of = lambda h: table[:, KEYS + h:KEYS + h + 1]
                V.tensor_scalar(o[:, :], o_ps[:, 0:D], of(0), None, M).then_inc(S["o_part"], 1)
                for h in range(1, H):
                    dve.wait_ge(S["o_part"], g * H + h)
                    V.scalar_tensor_tensor(o[:, :], o_ps[:, h * D:(h + 1) * D], of(h), o[:, :], M, ALU.add)\
                        .then_inc(S["o_part"], 1)
                dve.wait_ge(S["o_part"], g * H + H)
                V.tensor_scalar(o[:, :], o[:, :], den[:, 1:2], None, M).then_inc(S["o_ready"], 1)

        @block.gpsimd
        def _(pool):
            for g in range(DB // GROUP):
                pool.wait_ge(S["o_ready"], g + 1)
                for bb in range(GROUP):
                    b = g * GROUP + bb
                    dst = io["att_o"][b * DS:(b + 1) * DS, :].rearrange("i (h d) -> h i d", h=H)
                    pool.dma_start(dst, o[32 * bb:32 * bb + 32, :]).then_inc(S["o_out"], 16)
            pool.wait_ge(S["o_out"], 16 * DB)

        program.close()
        nc.clear_and_free_semaphores(sems)
        nc.all_engine_barrier()


def finish(nc, io):
    with ExitStack() as ctx:
        sems = []

        def sb(name, shape, dtype=F32):
            return ctx.enter_context(nc.sbuf_tensor(f"f_{name}", shape, dtype))

        def semaphore(name):
            sems.append(ctx.enter_context(nc.semaphore(f"f_{name}")))
            return sems[-1]

        wo = io["wo"]
        wo_parts = [sb(f"wo_{n}", [P, KD, DM], F32R) for n in ("high", "low")]
        ident, eps = sb("ident", [P, P]), sb("eps", [P, 1])
        finalw = sb("finalw", [P, DM])
        parts_of = [sb(f"parts{n}", [P, 3, PART]) for n in range(2)]
        gate_of = [sb(f"gate{n}", [P, BW]) for n in range(2)]
        sig = sb("sig", [P, BW])
        top = sb("top", [P, 2, H])
        wgt = sb("wgt", [P, 3, H])
        dens = sb("dens", [P, 3, H])
        den = sb("den", [P, 2, H])
        y_of = [sb(f"y{n}", [P, DM]) for n in range(2)]
        yT_parts = [sb(f"yT_{n}", [P, KD, P], F32R) for n in ("high", "low")]
        x_of = [sb(f"x{n}", [P, DM]) for n in range(2)]
        z = sb("z", [P, DM])
        sq = sb("sq", [P, DM])
        rstd = sb("rstd", [P, 2])
        out = sb("out", [P, DM])
        tp, pj = ([ctx.enter_context(nc.psum_tensor(f"f_{n}{k}", [P, 512], F32)) for k in range(2)]
                  for n in ("tp", "pj"))
        S = {n: Count(semaphore(n), per) for n, per in (
            ("out_out", 16),
            ("top0_ready", 1), ("top_ready", 1), ("diff_ready", 1), ("wgt_ready", 1), ("den_ready", 1),
            ("sum_ready", 1), ("inv_ready", 1), ("wn_ready", 1), ("tanh_ready", 1), ("half_ready", 1),
            ("sig_ready", 1), ("scaled_ready", 1), ("pair_ready", 1), ("num_ready", 1), ("yA_ready", 1),
            ("y_ps", 2), ("high_ready", 2), ("low_ready", 2), ("half_used", 1),
            ("o_done", 2), ("z_ready", 2), ("sq_ready", 1), ("ln_ready", 1),
            ("rstd_ready", 1), ("out_ready", 1))}
        for n in ("top0_ready", "top_ready", "diff_ready", "wgt_ready", "den_ready", "sum_ready", "inv_ready",
                  "wn_ready", "scaled_ready", "pair_ready", "num_ready"):
            S[n].first = 1
        loads, setup, loads_out = semaphore("loads"), semaphore("setup"), semaphore("loads_out")
        wo_high, wo_low, passed = semaphore("wo_high"), semaphore("wo_low"), semaphore("sp_passed")
        loaded = {n: [semaphore(f"{n}_in{k}") for k in range(2)] for n in ("parts", "gate", "y", "x")}

        def arrived(eng, name, tile):
            eng.wait_ge(loaded[name][tile.slot], 16 * tile.turn + 16)

        def slot_free(eng, name, tile):
            if not isinstance(tile.t, int) or tile.t >= 2:
                eng.wait_ge(S[name].sem, S[name].per * (tile.t - 1))

        def need(eng, name, tile, k=None):
            S[name].wait(eng, tile, k)

        def free(eng, name, tile):
            S[name].wait(eng, tile, 0)

        def done(ins, name):
            ins.then_inc(S[name].sem, 1)

        def apart(eng, tile):
            if not isinstance(tile.t, int):
                eng.sem_inc(passed, 1)

        def tile(half, odd):
            n = half * 2 + odd
            t = Tile(P, n + 1, n * P)
            t.slot, t.turn = 1 - odd, half + odd
            return t

        def run(eng, iteration):
            own, end = Tile(TS, 0, 0), NT // 2 - 1
            own.slot, own.turn = 0, 0
            iteration(None, None, own)
            iteration(None, own, tile(0, 0))
            iteration(own, tile(0, 0), tile(0, 1))
            with eng.Fori(0, end) as i:
                iteration(tile(i, 0), tile(i, 1), tile(i + 1, 0))
                iteration(tile(i, 1), tile(i + 1, 0), tile(i + 1, 1))
            iteration(tile(end, 0), tile(end, 1), None)
            iteration(tile(end, 1), None, None)

        program = ExitStack()
        block = program.enter_context(nc.Block())

        @block.sync
        def _(sp):
            sp.dma_start(ident[:, :], io["consts"][:, io["cols"]["ident"]:io["cols"]["ident"] + P])\
                .then_inc(loads, 16)
            sp.dma_start(finalw[:, :], io["final_norm_w"].broadcast_to([P, DM])).then_inc(loads, 16)

            def iteration(pr, tr, mg):
                if mg:
                    r, s = mg.rows, mg.slot
                    slot_free(sp, "yA_ready", mg)
                    apart(sp, mg)
                    if mg.sample:
                        sp.dma_start(parts_of[s][0:r, 0, 0:BW], io["att_o"]).then_inc(loaded["parts"][s], 16)
                    else:
                        sp.dma_start(parts_of[s][:, :, :], io["parts"][:, bass.ds(mg.row, P), :]
                                     .rearrange("k p n -> p k n")).then_inc(loaded["parts"][s], 16)
                    src = io["att_s"] if mg.sample else rows_of(mg, io["att_rows"])
                    sp.dma_start(gate_of[s][0:r, :], src[:, 3 * BW:]).then_inc(loaded["gate"][s], 16)
                    slot_free(sp, "y_ps", mg)
                    apart(sp, mg)
                    src = io["y_rows"][SEQ:, :] if mg.sample else rows_of(mg, io["y_rows"])
                    sp.dma_start(y_of[s][0:r, BW:], src).then_inc(loaded["y"][s], 16)
                    slot_free(sp, "z_ready", mg)
                    apart(sp, mg)
                    sp.dma_start(x_of[s][0:r, :], rows_of(mg, io["x_s" if mg.sample else "x_p"]))\
                        .then_inc(loaded["x"][s], 16)

            run(sp, iteration)

        @block.tensor
        def _(pe):
            pe.wait_ge(loads, 32)

            def project(pr, half):
                need(pe, "low_ready", pr, half + 1)
                for g in range(2):
                    if half == 0 and not pr.sample:
                        pe.wait_ge(S["z_ready"].sem, pr.t * 2 + (g - 1))
                    for k in range(4 * half, 4 * half + 4):
                        last = split_products(nc, pj[g][0:pr.rows, :], [t[:, k, 0:pr.rows] for t in yT_parts],
                                              wo_parts, k, slice(512 * g, 512 * g + 512),
                                              start=(k == 0), stop=(k == KD - 1))
                    if half:
                        done(last, "o_done")
                return last

            def iteration(pr, tr, mg):
                if pr:
                    if pr.sample:
                        pe.wait_ge(wo_low, KD)
                    done(project(pr, 0), "half_used")
                if tr:
                    r, y = tr.rows, y_of[tr.slot]
                    need(pe, "yA_ready", tr)
                    arrived(pe, "y", tr)
                    free(pe, "low_ready", tr)
                    for half in range(2):
                        for k in range(4):
                            last = nc.tensor.transpose(tp[half][:, k * r:(k + 1) * r],
                                                       y[0:r, (4 * half + k) * P:(4 * half + k + 1) * P],
                                                       ident[0:r, 0:r])
                        done(last, "y_ps")
                if pr:
                    project(pr, 1)

            run(pe, iteration)

        @block.scalar
        def _(act):
            do_act = nc.scalar.activation
            nc.scalar.preload_act_table_set("natural_log_exp_and_others")
            act.wait_ge(setup, 1)
            act.wait_ge(io["wo_in"], 64)
            for k in range(KD):
                do_act(wo_parts[0][:, k, :], wo[:, k, :], ACT.Copy).then_inc(wo_high, 1)

            def high(mg, half):
                r = mg.rows
                need(act, "y_ps", mg, half + 1)
                free(act, "o_done" if half else "half_used", mg)
                done(do_act(yT_parts[0][:, 4 * half:4 * half + 4, 0:r],
                            tp[half][:, 0:4 * r].rearrange("p (k t) -> p k t", k=4), ACT.Copy),
                     "high_ready")

            def iteration(pr, tr, mg):
                if mg and not mg.sample:
                    need(act, "diff_ready", mg)
                    done(do_act(wgt[:, :, :], wgt[:, :, :], ACT.Exp), "wgt_ready")
                if tr:
                    high(tr, 0)
                if mg:
                    r = mg.rows
                    arrived(act, "gate", mg)
                    free(act, "yA_ready", mg)
                    done(do_act(sig[0:r, :], gate_of[mg.slot][0:r, :], ACT.Tanh, scale=0.5), "tanh_ready")
                    nc.scalar.preload_act_table_set("natural_log_exp_and_others")
                if tr:
                    high(tr, 1)
                if pr:
                    r = pr.rows
                    need(act, "z_ready", pr)
                    free(act, "out_ready", pr)
                    done(do_act(sq[0:r, :], z[0:r, :], ACT.Square, accum_out=rstd[0:r, 0:1]), "sq_ready")
                    need(act, "sq_ready", pr)
                    done(do_act(rstd[0:r, 1:2], rstd[0:r, 0:1], ACT.Ln, scale=1.0 / DM, bias=eps[0:r, :]),
                         "ln_ready")
                    need(act, "ln_ready", pr)
                    done(do_act(rstd[0:r, 0:1], rstd[0:r, 1:2], ACT.Exp, scale=-0.5), "rstd_ready")

            run(act, iteration)

        @block.vector
        def _(dve):
            V = nc.vector
            tt, ts, stt = V.tensor_tensor, V.tensor_scalar, V.scalar_tensor_tensor
            M, A, SUB, MAX = ALU.mult, ALU.add, ALU.subtract, ALU.max
            V.memset(eps[:, :], EPS).then_inc(setup, 1)
            dve.wait_ge(loads, 32)

            def weigh(mg):
                parts = parts_of[mg.slot]
                m = [parts[:, k, BW + H:PART] for k in range(3)]
                arrived(dve, "parts", mg)
                done(tt(top[:, 0, :], m[0], m[1], MAX), "top0_ready")
                need(dve, "top0_ready", mg)
                done(tt(top[:, 1, :], top[:, 0, :], m[2], MAX), "top_ready")
                need(dve, "top_ready", mg)
                done(tt(wgt[:, :, :], parts[:, :, BW + H:PART],
                        top[:, 1:2, :].broadcast_to([P, 3, H]), SUB), "diff_ready")
                need(dve, "wgt_ready", mg)
                done(tt(dens[:, :, :], wgt[:, :, :], parts[:, :, BW:BW + H], M), "den_ready")
                need(dve, "den_ready", mg)
                done(V.tensor_reduce(den[:, 0, :], dens[:, :, :].rearrange("p k h -> p h k"), AX_X, A),
                     "sum_ready")
                need(dve, "sum_ready", mg)
                done(V.reciprocal(den[:, 1, :], den[:, 0, :]), "inv_ready")
                need(dve, "inv_ready", mg)
                done(tt(wgt[:, :, :], wgt[:, :, :], den[:, 1:2, :].broadcast_to([P, 3, H]), M), "wn_ready")

            def merge(mg):
                r, parts, gate, y = mg.rows, parts_of[mg.slot], gate_of[mg.slot], y_of[mg.slot]
                if not mg.sample:
                    need(dve, "wn_ready", mg)
                    for k in range(3):
                        v = parts[:, k, 0:BW].rearrange("p (h d) -> p h d", h=H)
                        ins = tt(v, v, wgt[:, k, :].unsqueeze(2).broadcast_to([P, H, D]), M)
                    done(ins, "scaled_ready")
                    need(dve, "scaled_ready", mg)
                    done(tt(parts[:, 0, 0:BW], parts[:, 0, 0:BW], parts[:, 1, 0:BW], A), "pair_ready")
                    need(dve, "pair_ready", mg)
                need(dve, "tanh_ready", mg)
                done(ts(sig[0:r, :], sig[0:r, :], 0.5, 0.5, M, A), "half_ready")
                need(dve, "half_ready", mg)
                done(tt(sig[0:r, :], sig[0:r, :], gate[0:r, :], M), "sig_ready")
                need(dve, "sig_ready", mg)
                slot_free(dve, "y_ps", mg)
                if mg.sample:
                    arrived(dve, "parts", mg)
                    done(tt(y[0:r, 0:BW], parts[0:r, 0, 0:BW], sig[0:r, :], M), "yA_ready")
                else:
                    done(tt(y[:, 0:BW], parts[:, 0, 0:BW], parts[:, 2, 0:BW], A), "num_ready")
                    need(dve, "num_ready", mg)
                    done(tt(y[:, 0:BW], y[:, 0:BW], sig[:, :], M), "yA_ready")

            def low(mg, half):
                r = mg.rows
                need(dve, "high_ready", mg, half + 1)
                ks = slice(4 * half, 4 * half + 4)
                done(tt(yT_parts[1][:, ks, 0:r], tp[half][:, 0:4 * r].rearrange("p (k t) -> p k t", k=4),
                        yT_parts[0][:, ks, 0:r], SUB), "low_ready")

            def iteration(pr, tr, mg):
                if mg and not mg.sample:
                    weigh(mg)
                if tr:
                    low(tr, 0)
                if mg:
                    merge(mg)
                if pr:
                    r = pr.rows
                    arrived(dve, "x", pr)
                    for half in range(2):
                        need(dve, "o_done", pr, half + 1)
                        cols = slice(512 * half, 512 * half + 512)
                        free(dve, "out_ready", pr)
                        done(tt(z[0:r, cols], pj[half][0:r, :], x_of[pr.slot][0:r, cols], A), "z_ready")
                if tr:
                    low(tr, 1)
                if pr:
                    need(dve, "rstd_ready", pr)
                    free(dve, "out_out", pr)
                    done(stt(out[0:r, :], z[0:r, :], rstd[0:r, 0:1], finalw[0:r, :], M, M), "out_ready")

            for k in range(KD):
                dve.wait_ge(wo_high, k + 1)
                tt(wo_parts[1][:, k, :], wo[:, k, :], wo_parts[0][:, k, :], SUB).then_inc(wo_low, 1)
            run(dve, iteration)

        @block.gpsimd
        def _(pool):
            def iteration(pr, tr, mg):
                if pr:
                    need(pool, "out_ready", pr)
                    pool.dma_start(rows_of(pr, io["out_s" if pr.sample else "out_p"]), out[0:pr.rows, :])\
                        .then_inc(S["out_out"].sem, 16)

            keep = slice(SEQ - BUF, SEQ)
            for dst, src in ((io["k_p"], io["att_rows"][keep, BW:2 * BW]),
                             (io["v_p"], io["att_rows"][keep, 2 * BW:3 * BW]),
                             (io["k_s"], io["att_s"][:, BW:2 * BW]),
                             (io["v_s"], io["att_s"][:, 2 * BW:3 * BW])):
                pool.dma_start(dst, src).then_inc(loads_out, 16)
            run(pool, iteration)
            need(pool, "out_out", Tile(P, NT))
            pool.wait_ge(loads_out, 64)

        program.close()
        nc.clear_and_free_semaphores(sems)
        nc.all_engine_barrier()


_INS = ("cache_attn_k", "cache_attn_v", "state_delta", "state_delta_conv", "state_hgrn", "state_pool",
        "w_in", "w_out", "delta_a_log", "delta_dt_bias", "delta_norm_w", "hgrn_norm_w", "pool_w",
        "pool_scale")


def build(nc, io, y_p, y_s, k_p, k_s, v_p, v_s, d_p, d_s, dc_p, dc_s, h_p, h_s, pl_p, pl_s):
    def scratch(name, shape):
        return nc.dram_tensor(name, shape, F32, kind="Internal").ap()

    io.update(
        cache_k=io["cache_attn_k"], cache_v=io["cache_attn_v"],
        att_rows=scratch("att_rows", [SEQ, AW]), att_s=scratch("att_s", [TS, AW]),
        sample_rows=scratch("sample_rows", [TS, MW]), y_rows=scratch("y_rows", [SEQ + TS, 3 * BW]),
        parts=scratch("parts", [3, SEQ, PART]), att_o=scratch("att_o", [TS, BW]),
        conv_p=dc_p[0, 0], conv_s=dc_s[0], pool_p=pl_p[0, 0], pool_s=pl_s[0],
        delta_prompt=d_p[0], delta_sample=d_s[0], hgrn_prompt=h_p[0], hgrn_sample=h_s[0],
        out_p=y_p[0], out_s=y_s.rearrange("b t n -> (b t) n"),
        k_p=k_p[0, 0].rearrange("t h d -> t (h d)"), v_p=v_p[0, 0].rearrange("t h d -> t (h d)"),
        k_s=k_s[0].rearrange("b t h d -> (b t) (h d)"), v_s=v_s[0].rearrange("b t h d -> (b t) (h d)"))
    with ExitStack() as ctx:
        io["w_mix"] = ctx.enter_context(nc.sbuf_tensor("w_mix", [P, KD, MW], F32))
        io["w_mix_in"] = ctx.enter_context(nc.semaphore("w_mix_in"))
        project_attention(nc, io)
        mixers(nc, io, io["consts"], io["cols"], "prompt")
    mixers(nc, io, io["consts"], io["cols"], "sample")
    attend_classes(nc, io)
    with ExitStack() as ctx:
        io["wo"] = ctx.enter_context(nc.sbuf_tensor("wo", [P, KD, DM], F32))
        io["wo_in"] = ctx.enter_context(nc.semaphore("wo_in"))
        attend_cache(nc, io)
        finish(nc, io)


def kernel(**inputs):
    import numpy as _np
    import concourse.bacc as _bacc
    from concourse.bass_utils import run_bass_kernel_spmd as _run

    nc = _bacc.Bacc("TRN2", target_bir_lowering=False, num_devices=1)
    table, cols = host_constants()
    given = {name: _np.asarray(inputs[name]) for name in _INS}
    given["x_p"] = _np.asarray(inputs["x_prompt"])[0]
    given["x_s"] = _np.asarray(inputs["x_sample"]).reshape(TS, DM)
    given["norm_w_fm"] = _np.asarray(inputs["norm_w"])[0].reshape(KD, P).T
    given["conv_w_fm"] = _np.asarray(inputs["delta_conv_w"])[0].reshape(CONV, 6, P).transpose(2, 1, 0)
    given["final_norm_w"] = _np.asarray(inputs["final_norm_w"]).reshape(1, DM)
    given["consts"] = table
    arrays, io = {}, {"cols": cols}
    for name, a in given.items():
        arrays[f"in_{name}"] = _np.ascontiguousarray(a)
        io[name] = nc.dram_tensor(f"in_{name}", a.shape, F32, kind="ExternalInput").ap()
    shapes = ((1, SEQ, DM), (DB, DS, DM), (1, 1, BUF, H, D), (1, DB, DS, H, D), (1, 1, BUF, H, D),
              (1, DB, DS, H, D), (1, 1, H, D, D), (1, DB, H, D, D), (1, 1, CONV - 1, 3 * BW),
              (1, DB, CONV - 1, 3 * BW), (1, 1, H, D, D), (1, DB, H, D, D), (1, 1, PMAX - 1, BW),
              (1, DB, PMAX - 1, BW))
    outs = [nc.dram_tensor(f"out_{i}", shape, F32, kind="ExternalOutput").ap()
            for i, shape in enumerate(shapes)]
    build(nc, io, *outs)
    r = _run(nc, [arrays], core_ids=[0])
    return tuple(r.results[0][f"out_{i}"] for i in range(len(shapes)))
```
